# Optimizing a Trainium2 kernel written in Bass

```python
import jax, jax.numpy as jnp
from jax import lax
import numpy as np

D_MODEL = 1024
BATCH = 1
SEQ = 512
DEPTH = 1

D_MIX = 2 * D_MODEL
D_POOL = D_MIX // 2
D_MLSTM = D_MIX - D_POOL
POOL_WINDOWS = (2, 4, 8, 16)
N_POOL_GROUPS = len(POOL_WINDOWS)
POOL_GROUP_DIM = D_POOL // N_POOL_GROUPS
N_HEADS = 4
HEAD_DIM = D_MLSTM // N_HEADS
QKV_BLOCK = 4
N_QKV_BLOCKS = D_MLSTM // QKV_BLOCK
CONV_WIDTH = 5
CHUNK = 128
N_DIRS = 2
EPS = 1e-6
NEG_INF = -1e30


def rms_norm(x, g):
    xf = x.astype(jnp.float32)
    y = xf * lax.rsqrt(jnp.mean(xf * xf, axis=-1, keepdims=True) + EPS)
    return (y * g.astype(jnp.float32)).astype(x.dtype)

def window_mean_minus_self(u, w):
    S = u.shape[1]
    left = (w - 1) // 2
    right = w - 1 - left
    uf = u.astype(jnp.float32)
    cs = jnp.concatenate([jnp.zeros_like(uf[:, :1]), jnp.cumsum(uf, axis=1)], axis=1)
    t = np.arange(S)
    lo = np.maximum(t - left, 0)
    hi = np.minimum(t + right, S - 1)
    total = cs[:, hi + 1] - cs[:, lo]
    count = (hi - lo + 1).astype(np.float32)[None, :, None]
    return (total / count - uf).astype(u.dtype)

def pool_mixer(u, pool_w, pool_scale):
    B, S, _ = u.shape
    ug = u.reshape(B, S, N_POOL_GROUPS, POOL_GROUP_DIM)
    pooled = jnp.stack([window_mean_minus_self(ug[:, :, g], w) for g, w in enumerate(POOL_WINDOWS)], axis=2)
    mixed = jnp.einsum('bsgc,gcd->bsgd', pooled, pool_w).reshape(B, S, D_POOL)
    return mixed * pool_scale

def centred_depthwise_conv(u, w, b):
    K, C = w.shape
    pad = K // 2
    y = lax.conv_general_dilated(u, w[:, None, :].astype(u.dtype), window_strides=(1,),
                                 padding=[(pad, pad)], dimension_numbers=('NWC', 'WIO', 'NWC'),
                                 feature_group_count=C)
    return y + b

def headwise(u, w):
    B, S, _ = u.shape
    return jnp.einsum('bsni,nio->bsno', u.reshape(B, S, w.shape[0], w.shape[1]), w).reshape(B, S, -1)

def mlstm_chunkwise(q, k, v, log_i, log_f):
    B, H, S, d = q.shape
    nc = S // CHUNK

    def to_chunks(a):
        return jnp.moveaxis(a.reshape(B, H, nc, CHUNK, *a.shape[3:]), 2, 0)

    qc, kc, vc, ic, fc = map(to_chunks, (q, k, v, log_i, log_f))
    lower_tri = jnp.tril(jnp.ones((CHUNK, CHUNK), dtype=bool))

    def step(carry, xs):
        C, n, m = carry
        qj, kj, vj, ij, fj = xs
        b = jnp.cumsum(fj, axis=-1)
        log_inter = b + m[..., None]
        log_D = b[..., :, None] - b[..., None, :] + ij[..., None, :]
        log_D = jnp.where(lower_tri, log_D, NEG_INF)
        m_t = jnp.maximum(log_inter, jnp.max(log_D, axis=-1))
        inter_w = jnp.exp(log_inter - m_t)
        s = jnp.einsum('bhtd,bhsd->bhts', qj, kj) * jnp.exp(log_D - m_t[..., None])
        num = jnp.einsum('bhts,bhse->bhte', s, vj) + inter_w[..., None] * jnp.einsum('bhtd,bhde->bhte', qj, C)
        den = jnp.sum(s, axis=-1) + inter_w * jnp.einsum('bhtd,bhd->bht', qj, n)
        h = num / jnp.maximum(jnp.abs(den), jnp.exp(-m_t))[..., None]
        bL = b[..., -1]
        log_s = bL[..., None] - b + ij
        m_new = jnp.maximum(bL + m, jnp.max(log_s, axis=-1))
        decay = jnp.exp(bL + m - m_new)
        ws = jnp.exp(log_s - m_new[..., None])
        C_new = decay[..., None, None] * C + jnp.einsum('bhs,bhsd,bhse->bhde', ws, kj, vj)
        n_new = decay[..., None] * n + jnp.einsum('bhs,bhsd->bhd', ws, kj)
        return (C_new, n_new, m_new), h

    init = (jnp.zeros((B, H, d, d), jnp.float32), jnp.zeros((B, H, d), jnp.float32),
            jnp.zeros((B, H), jnp.float32))
    _, hs = lax.scan(step, init, (qc, kc, vc, ic, fc))
    return jnp.moveaxis(hs, 0, 2).reshape(B, H, S, d)

def mlstm_branch(u, conv_w, conv_b, w_q, w_k, w_v, w_gates, b_gates, mh_norm_w, skip_w):
    B, S, _ = u.shape
    c = jax.nn.silu(centred_depthwise_conv(u, conv_w, conv_b))
    q = headwise(c, w_q)
    k = headwise(c, w_k)
    v = headwise(u, w_v)
    qkv = jnp.concatenate([q, k, v], axis=-1).astype(jnp.float32)
    gates = jnp.einsum('bsc,ncg->nbsg', qkv, w_gates.astype(jnp.float32)) \
        + b_gates.astype(jnp.float32)[:, None, None, :]
    gates = jnp.transpose(gates, (0, 1, 3, 2))
    log_i = gates[:, :, :N_HEADS]
    log_f = jax.nn.log_sigmoid(gates[:, :, N_HEADS:])

    def heads(a):
        return a.reshape(B, S, N_HEADS, HEAD_DIM).transpose(0, 2, 1, 3).astype(jnp.float32)

    qh, kh, vh = heads(q), heads(k) * (HEAD_DIM ** -0.5), heads(v)
    h_fwd = mlstm_chunkwise(qh, kh, vh, log_i[0], log_f[0])
    h_bwd = jnp.flip(mlstm_chunkwise(jnp.flip(qh, 2), jnp.flip(kh, 2), jnp.flip(vh, 2),
                                     jnp.flip(log_i[1], -1), jnp.flip(log_f[1], -1)), 2)
    h = h_fwd + h_bwd
    mu = jnp.mean(h, axis=-1, keepdims=True)
    var = jnp.mean(jnp.square(h - mu), axis=-1, keepdims=True)
    h = (h - mu) * lax.rsqrt(var + EPS)
    h = h.transpose(0, 2, 1, 3).reshape(B, S, D_MLSTM)
    out = h * mh_norm_w.astype(jnp.float32) + skip_w.astype(jnp.float32) * c.astype(jnp.float32)
    return out.astype(u.dtype)

def first_inputs(seed: int = 0) -> dict:
    key = jax.random.key(seed)
    ks = jax.random.split(key, 20)
    nrm = jax.random.normal
    f32 = jnp.float32
    x = nrm(ks[0], (BATCH, SEQ, D_MODEL), f32)
    norm_in_g = 1.0 + 0.1 * nrm(ks[1], (DEPTH, D_MODEL), f32)
    w_in = nrm(ks[2], (DEPTH, D_MODEL, 2 * D_MIX), f32) * D_MODEL ** -0.5
    pool_w = nrm(ks[3], (DEPTH, N_POOL_GROUPS, POOL_GROUP_DIM, POOL_GROUP_DIM), f32) * POOL_GROUP_DIM ** -0.5
    pool_scale = 1.0 + 0.1 * nrm(ks[4], (DEPTH, D_POOL), f32)
    conv_w = nrm(ks[5], (DEPTH, CONV_WIDTH, D_MLSTM), f32) * CONV_WIDTH ** -0.5
    conv_b = 0.01 * nrm(ks[6], (DEPTH, D_MLSTM), f32)
    w_q = nrm(ks[7], (DEPTH, N_QKV_BLOCKS, QKV_BLOCK, QKV_BLOCK), f32) * QKV_BLOCK ** -0.5
    w_k = nrm(ks[8], (DEPTH, N_QKV_BLOCKS, QKV_BLOCK, QKV_BLOCK), f32) * QKV_BLOCK ** -0.5
    w_v = nrm(ks[9], (DEPTH, N_QKV_BLOCKS, QKV_BLOCK, QKV_BLOCK), f32) * QKV_BLOCK ** -0.5
    w_gates = nrm(ks[10], (DEPTH, N_DIRS, 3 * D_MLSTM, 2 * N_HEADS), f32) * (3 * D_MLSTM) ** -0.5
    b_i = 0.1 * nrm(ks[11], (DEPTH, N_DIRS, N_HEADS), f32)
    b_f = jnp.linspace(3.0, 6.0, N_HEADS, dtype=f32) + 0.1 * nrm(ks[12], (DEPTH, N_DIRS, N_HEADS), f32)
    b_gates = jnp.concatenate([b_i, b_f], axis=-1)
    mh_norm_w = 1.0 + 0.1 * nrm(ks[13], (DEPTH, D_MLSTM), f32)
    skip_w = 1.0 + 0.1 * nrm(ks[14], (DEPTH, D_MLSTM), f32)
    w_out = nrm(ks[15], (DEPTH, D_MIX, D_MODEL), f32) * D_MIX ** -0.5
    norm_out_g = 1.0 + 0.1 * nrm(ks[16], (D_MODEL,), f32)
    return {"x": x, "norm_in_g": norm_in_g, "w_in": w_in, "pool_w": pool_w, "pool_scale": pool_scale,
            "conv_w": conv_w, "conv_b": conv_b, "w_q": w_q, "w_k": w_k, "w_v": w_v,
            "w_gates": w_gates, "b_gates": b_gates, "mh_norm_w": mh_norm_w, "skip_w": skip_w,
            "w_out": w_out, "norm_out_g": norm_out_g}

def first_block(x, norm_in_g, w_in, pool_w, pool_scale, conv_w, conv_b, w_q, w_k, w_v,
              w_gates, b_gates, mh_norm_w, skip_w, w_out, norm_out_g):
    h = x
    for l in range(DEPTH):
        u = rms_norm(h, norm_in_g[l])
        proj = jnp.einsum('bsd,de->bse', u, w_in[l])
        pool_x, pool_z, m_x, m_z = jnp.split(proj, [D_POOL, 2 * D_POOL, 2 * D_POOL + D_MLSTM], axis=-1)
        y_pool = pool_mixer(pool_x, pool_w[l], pool_scale[l]) * jax.nn.silu(pool_z)
        y_m = mlstm_branch(m_x, conv_w[l], conv_b[l], w_q[l], w_k[l], w_v[l], w_gates[l],
                           b_gates[l], mh_norm_w[l], skip_w[l]) * jax.nn.silu(m_z)
        y = jnp.concatenate([y_pool.astype(h.dtype), y_m.astype(h.dtype)], axis=-1)
        h = h + jnp.einsum('bse,ed->bsd', y, w_out[l])
    return rms_norm(h, norm_out_g)


DEPTH_2 = 2

N_MIXERS = 2
HEAD_DIM_2 = 64
ROPE_THETA = 10000.0
NORM_EPS = 1e-6

NSA_HEADS = 16
NSA_KV_HEADS = 4
CMP_LEN = 32
CMP_STRIDE = 16
CMP_HIDDEN = 256
SLC_LEN = 64
SLC_TOPK = 16
WIN_LEN = 512
FORCE_BONUS = 1e4
SLC_Q_CHUNK = 16
NSA_IN_DIM = NSA_HEADS * HEAD_DIM_2 + 6 * NSA_KV_HEADS * HEAD_DIM_2 + 3 * NSA_HEADS

SWA_HEADS = 16
SWA_KV_HEADS = 2
SWA_WINDOW = 128
SWA_IN_DIM = SWA_HEADS * HEAD_DIM_2 + 2 * SWA_KV_HEADS * HEAD_DIM_2

Q_BLOCK = 128

D_FF = 2816
CONV_WIDTH_2 = 3

N_A = (DEPTH_2 + 1) // 2
N_B = DEPTH_2 // 2


def rms_norm_2(x, gain):
    xf = x.astype(jnp.float32)
    y = xf * lax.rsqrt(jnp.mean(xf * xf, axis=-1, keepdims=True) + NORM_EPS)
    return (y * gain.astype(jnp.float32)).astype(x.dtype)

def rope_tables(seq):
    pos = jnp.arange(seq, dtype=jnp.float32)
    inv = ROPE_THETA ** (-jnp.arange(0, HEAD_DIM_2, 2, dtype=jnp.float32) / HEAD_DIM_2)
    ang = pos[:, None] * inv[None, :]
    return jnp.cos(ang), jnp.sin(ang)

def apply_rope(x, cos, sin):
    c = cos[None, :, None, :].astype(x.dtype)
    s = sin[None, :, None, :].astype(x.dtype)
    x1, x2 = jnp.split(x, 2, axis=-1)
    return jnp.concatenate([x1 * c - x2 * s, x2 * c + x1 * s], axis=-1)

def to_q_groups(q, n_groups):
    b, s, h, d = q.shape
    return q.reshape(b, s, n_groups, h // n_groups, d).transpose(0, 2, 3, 1, 4)

def from_q_groups(o):
    b, g, r, s, d = o.shape
    return o.transpose(0, 3, 1, 2, 4).reshape(b, s, g * r * d)

def masked_softmax(s, mask):
    s = jnp.where(mask, s, -jnp.inf)
    m = jnp.max(s, axis=-1, keepdims=True)
    m = jnp.where(jnp.isfinite(m), m, 0.0)
    p = jnp.exp(s - m)
    d = jnp.sum(p, axis=-1, keepdims=True)
    return p / jnp.where(d > 0.0, d, 1.0)

def banded_attention(q, k, v, window, sinks=None):
    b, g, r, seq, hd = q.shape
    nqb = seq // Q_BLOCK
    span = Q_BLOCK + window
    pad = ((0, 0), (0, 0), (window, 0), (0, 0))
    k_pad = jnp.pad(k, pad)
    v_pad = jnp.pad(v, pad)
    qb = q.reshape(b, g, r, nqb, Q_BLOCK, hd).transpose(3, 0, 1, 2, 4, 5)
    scale = hd ** -0.5

    def block(args):
        blk, q_blk = args
        start = blk * Q_BLOCK
        kb = lax.dynamic_slice_in_dim(k_pad, start, span, axis=2)
        vb = lax.dynamic_slice_in_dim(v_pad, start, span, axis=2)
        qpos = start + jnp.arange(Q_BLOCK)
        kpos = start - window + jnp.arange(span)
        rel = qpos[:, None] - kpos[None, :]
        mask = (rel >= 0) & (rel < window) & (kpos[None, :] >= 0)
        s = jnp.einsum('bgrqd,bgkd->bgrqk', q_blk, kb).astype(jnp.float32) * scale
        if sinks is None:
            p = masked_softmax(s, mask)
        else:
            s = jnp.where(mask, s, -jnp.inf)
            sink = sinks.astype(jnp.float32)[None, :, :, None, None]
            m = jnp.maximum(jnp.max(s, axis=-1, keepdims=True), sink)
            p = jnp.exp(s - m)
            p = p / (jnp.sum(p, axis=-1, keepdims=True) + jnp.exp(sink - m))
        return jnp.einsum('bgrqk,bgkd->bgrqd', p.astype(vb.dtype), vb)

    o = lax.map(block, (jnp.arange(nqb), qb))
    return o.transpose(1, 2, 3, 0, 4, 5).reshape(b, g, r, seq, hd)

def nsa_mixer(h, cos, sin, w_in, cmp_pe, cmp_w1, cmp_w2, gate_b, w_o):
    b, seq, _ = h.shape
    g, r, hd = NSA_KV_HEADS, NSA_HEADS // NSA_KV_HEADS, HEAD_DIM_2
    sizes = [NSA_HEADS * hd] + [g * hd] * 6 + [3 * NSA_HEADS]
    splits = np.cumsum(sizes)[:-1].tolist()
    q, kc, vc, ks, vs, kw, vw, gt = jnp.split(h @ w_in, splits, axis=-1)

    q = to_q_groups(apply_rope(q.reshape(b, seq, NSA_HEADS, hd), cos, sin), g)

    def kv(t, rotate):
        t = t.reshape(b, seq, g, hd)
        if rotate:
            t = apply_rope(t, cos, sin)
        return t.transpose(0, 2, 1, 3)

    kc, ks, kw = kv(kc, True), kv(ks, True), kv(kw, True)
    vc, vs, vw = kv(vc, False), kv(vs, False), kv(vw, False)
    pos = jnp.arange(seq)
    scale = hd ** -0.5

    n_cmp = (seq - CMP_LEN) // CMP_STRIDE + 1
    cstart = jnp.arange(n_cmp) * CMP_STRIDE
    cidx = cstart[:, None] + jnp.arange(CMP_LEN)[None, :]

    def compress(t, pe, w1, w2):
        blk = (t[:, :, cidx] + pe).reshape(b, g, n_cmp, CMP_LEN * hd)
        return jax.nn.gelu(blk @ w1) @ w2

    kc = compress(kc, cmp_pe[0], cmp_w1[0], cmp_w2[0])
    vc = compress(vc, cmp_pe[1], cmp_w1[1], cmp_w2[1])
    s_cmp = jnp.einsum('bgrqd,bgcd->bgrqc', q, kc).astype(jnp.float32) * scale
    cmask = (cstart + CMP_LEN - 1)[None, :] <= pos[:, None]
    p_cmp = masked_softmax(s_cmp, cmask)
    o_cmp = jnp.einsum('bgrqc,bgcd->bgrqd', p_cmp.astype(vc.dtype), vc)

    n_slc = seq // SLC_LEN
    top_n = min(SLC_TOPK, n_slc)
    sstart = jnp.arange(n_slc) * SLC_LEN
    overlap = ((cstart[:, None] <= sstart[None, :] + SLC_LEN - 1)
               & (cstart[:, None] + CMP_LEN - 1 >= sstart[None, :])).astype(jnp.float32)
    imp = jnp.einsum('bgrqc,cn->bgqn', p_cmp, overlap)
    cur = pos // SLC_LEN
    blk = jnp.arange(n_slc)
    forced = (blk[None, :] == 0) | (blk[None, :] == cur[:, None]) | (blk[None, :] == cur[:, None] - 1)
    causal = blk[None, :] <= cur[:, None]
    score = jnp.where(causal, imp + jnp.where(forced, FORCE_BONUS, 0.0), -1.0)
    top_score, sel = lax.top_k(score, top_n)
    sel_valid = top_score >= 0.0

    nqc = seq // SLC_Q_CHUNK
    q_ch = q.reshape(b, g, r, nqc, SLC_Q_CHUNK, hd).transpose(3, 0, 1, 2, 4, 5)
    sel_ch = sel.reshape(b, g, nqc, SLC_Q_CHUNK, top_n).transpose(2, 0, 1, 3, 4)
    val_ch = sel_valid.reshape(b, g, nqc, SLC_Q_CHUNK, top_n).transpose(2, 0, 1, 3, 4)
    pos_ch = pos.reshape(nqc, SLC_Q_CHUNK)
    gather_rows = jax.vmap(jax.vmap(lambda t, i: t[i]))
    n_keys = top_n * SLC_LEN

    def slc_block(args):
        q_c, sel_c, val_c, qpos = args
        tok = sel_c[..., None] * SLC_LEN + jnp.arange(SLC_LEN)
        tmask = val_c[..., None] & (tok <= qpos[None, None, :, None, None])
        tok = tok.reshape(b, g, SLC_Q_CHUNK, n_keys)
        tmask = tmask.reshape(b, g, SLC_Q_CHUNK, n_keys)
        kg = gather_rows(ks, tok)
        vg = gather_rows(vs, tok)
        s = jnp.einsum('bgrqd,bgqkd->bgrqk', q_c, kg).astype(jnp.float32) * scale
        p = masked_softmax(s, tmask[:, :, None])
        return jnp.einsum('bgrqk,bgqkd->bgrqd', p.astype(vg.dtype), vg)

    o_slc = lax.map(slc_block, (q_ch, sel_ch, val_ch, pos_ch))
    o_slc = o_slc.transpose(1, 2, 3, 0, 4, 5).reshape(b, g, r, seq, hd)

    o_win = banded_attention(q, kw, vw, WIN_LEN)

    gates = jax.nn.sigmoid((gt + gate_b).astype(jnp.float32))
    gates = gates.reshape(b, seq, g, r, 3).transpose(0, 2, 3, 1, 4).astype(q.dtype)
    o = gates[..., 0, None] * o_cmp + gates[..., 1, None] * o_slc + gates[..., 2, None] * o_win
    return from_q_groups(o) @ w_o

def swa_mixer(h, cos, sin, w_qkv, b_qkv, sinks, w_o, b_o):
    b, seq, _ = h.shape
    g, r, hd = SWA_KV_HEADS, SWA_HEADS // SWA_KV_HEADS, HEAD_DIM_2
    q, k, v = jnp.split(h @ w_qkv + b_qkv, [SWA_HEADS * hd, SWA_HEADS * hd + g * hd], axis=-1)
    q = to_q_groups(apply_rope(q.reshape(b, seq, SWA_HEADS, hd), cos, sin), g)
    k = apply_rope(k.reshape(b, seq, g, hd), cos, sin).transpose(0, 2, 1, 3)
    v = v.reshape(b, seq, g, hd).transpose(0, 2, 1, 3)
    o = banded_attention(q, k, v, SWA_WINDOW, sinks.reshape(g, r))
    return from_q_groups(o) @ w_o + b_o

def causal_depthwise_conv(a, w, bias):
    f = a.shape[-1]
    y = lax.conv_general_dilated(a, w.astype(a.dtype)[:, None, :], window_strides=(1,),
                                 padding=[(CONV_WIDTH_2 - 1, 0)],
                                 dimension_numbers=('NWC', 'WIO', 'NWC'),
                                 feature_group_count=f)
    return y + bias.astype(a.dtype)

def conv_ffn(h, w_gu, conv_w, conv_b, w_down):
    a, u = jnp.split(h @ w_gu, 2, axis=-1)
    a = causal_depthwise_conv(a, conv_w, conv_b)
    return (jax.nn.silu(a) * u) @ w_down

def second_inputs(seed: int = 0) -> dict:
    key = jax.random.key(seed)
    ks = jax.random.split(key, 20)
    f32 = jnp.float32

    def nrm(k, shape, scale):
        return jax.random.normal(k, shape, f32) * scale

    att_w = NSA_HEADS * HEAD_DIM_2
    swa_w = SWA_HEADS * HEAD_DIM_2
    return {
        'x': nrm(ks[0], (BATCH, SEQ, D_MODEL), 1.0),
        'nsa_w_in': nrm(ks[1], (N_A, D_MODEL, NSA_IN_DIM), D_MODEL ** -0.5),
        'nsa_cmp_pe': nrm(ks[2], (N_A, 2, CMP_LEN, HEAD_DIM_2), 0.02),
        'nsa_cmp_w1': nrm(ks[3], (N_A, 2, CMP_LEN * HEAD_DIM_2, CMP_HIDDEN), (CMP_LEN * HEAD_DIM_2) ** -0.5),
        'nsa_cmp_w2': nrm(ks[4], (N_A, 2, CMP_HIDDEN, HEAD_DIM_2), CMP_HIDDEN ** -0.5),
        'nsa_gate_b': nrm(ks[5], (N_A, 3 * NSA_HEADS), 0.1),
        'nsa_w_o': nrm(ks[6], (N_A, att_w, D_MODEL), att_w ** -0.5),
        'swa_w_qkv': nrm(ks[7], (N_B, D_MODEL, SWA_IN_DIM), D_MODEL ** -0.5),
        'swa_b_qkv': nrm(ks[8], (N_B, SWA_IN_DIM), 0.02),
        'swa_sinks': nrm(ks[9], (N_B, SWA_HEADS), 1.0),
        'swa_w_o': nrm(ks[10], (N_B, swa_w, D_MODEL), swa_w ** -0.5),
        'swa_b_o': nrm(ks[11], (N_B, D_MODEL), 0.02),
        'ffn_w_gu': nrm(ks[12], (DEPTH_2, D_MODEL, 2 * D_FF), D_MODEL ** -0.5),
        'ffn_conv_w': nrm(ks[13], (DEPTH_2, CONV_WIDTH_2, D_FF), CONV_WIDTH_2 ** -0.5),
        'ffn_conv_b': nrm(ks[14], (DEPTH_2, D_FF), 0.02),
        'ffn_w_down': nrm(ks[15], (DEPTH_2, D_FF, D_MODEL), D_FF ** -0.5),
        'norm_mix': 1.0 + nrm(ks[16], (DEPTH_2, D_MODEL), 0.02),
        'norm_ffn': 1.0 + nrm(ks[17], (DEPTH_2, D_MODEL), 0.02),
        'norm_final': 1.0 + nrm(ks[18], (D_MODEL,), 0.02),
    }

def second_block(x, nsa_w_in, nsa_cmp_pe, nsa_cmp_w1, nsa_cmp_w2, nsa_gate_b, nsa_w_o,
              swa_w_qkv, swa_b_qkv, swa_sinks, swa_w_o, swa_b_o,
              ffn_w_gu, ffn_conv_w, ffn_conv_b, ffn_w_down,
              norm_mix, norm_ffn, norm_final):
    cos, sin = rope_tables(x.shape[1])
    for i in range(DEPTH_2):
        j = i // N_MIXERS
        h = rms_norm_2(x, norm_mix[i])
        if i % N_MIXERS == 0:
            x = x + nsa_mixer(h, cos, sin, nsa_w_in[j], nsa_cmp_pe[j], nsa_cmp_w1[j],
                              nsa_cmp_w2[j], nsa_gate_b[j], nsa_w_o[j])
        else:
            x = x + swa_mixer(h, cos, sin, swa_w_qkv[j], swa_b_qkv[j], swa_sinks[j],
                              swa_w_o[j], swa_b_o[j])
        h = rms_norm_2(x, norm_ffn[i])
        x = x + conv_ffn(h, ffn_w_gu[i], ffn_conv_w[i], ffn_conv_b[i], ffn_w_down[i])
    return rms_norm_2(x, norm_final)


def setup_inputs(seed=0):
    out = dict(first_inputs(seed))
    for name, value in second_inputs(seed + 1).items():
        if name != "x":
            out[name + "_2"] = value
    return out


def reference(
    x, norm_in_g, w_in, pool_w, pool_scale, conv_w, conv_b, w_q, w_k, w_v, w_gates, b_gates,
    mh_norm_w, skip_w, w_out, norm_out_g, nsa_w_in_2, nsa_cmp_pe_2, nsa_cmp_w1_2, nsa_cmp_w2_2,
    nsa_gate_b_2, nsa_w_o_2, swa_w_qkv_2, swa_b_qkv_2, swa_sinks_2, swa_w_o_2, swa_b_o_2,
    ffn_w_gu_2, ffn_conv_w_2, ffn_conv_b_2, ffn_w_down_2, norm_mix_2, norm_ffn_2, norm_final_2,
):
    x = first_block(
        x, norm_in_g, w_in, pool_w, pool_scale, conv_w, conv_b, w_q, w_k, w_v, w_gates, b_gates,
        mh_norm_w, skip_w, w_out, norm_out_g,
    )
    return second_block(
        x, nsa_w_in_2, nsa_cmp_pe_2, nsa_cmp_w1_2, nsa_cmp_w2_2, nsa_gate_b_2, nsa_w_o_2,
        swa_w_qkv_2, swa_b_qkv_2, swa_sinks_2, swa_w_o_2, swa_b_o_2, ffn_w_gu_2, ffn_conv_w_2,
        ffn_conv_b_2, ffn_w_down_2, norm_mix_2, norm_ffn_2, norm_final_2,
    )


_drawn_inputs = setup_inputs


def setup_inputs(seed=0):
    import zlib

    import numpy as np

    out = dict(_drawn_inputs(seed))
    spreads = {}
    factors = {'conv_b': 3.187,
     'nsa_cmp_pe_2': 6.799,
     'nsa_gate_b_2': 3.787,
     'swa_b_qkv_2': 2.982,
     'swa_sinks_2': 59.28,
     'swa_b_o_2': 23.921,
     'ffn_conv_b_2': 3.977,
     'norm_mix_2': 6.056,
     'norm_ffn_2': 2.712,
     'norm_final_2': 7.768}
    for name, (base, spread) in spreads.items():
        noise = np.random.default_rng([zlib.crc32(name.encode()), seed]).standard_normal(out[name].shape)
        drawn = base * np.exp(spread * noise) if base else spread * noise
        out[name] = __import__('jax').numpy.asarray(drawn.astype(out[name].dtype))
    for name, factor in factors.items():
        out[name] = (out[name] * factor).astype(out[name].dtype)
    return out
```

```python
from contextlib import ExitStack

import numpy as np

import concourse.bass as bass
from concourse import mybir

F32 = mybir.dt.float32
F32R = mybir.dt.float32r
BF16 = mybir.dt.bfloat16
ALU = mybir.AluOpType
ACT = mybir.ActivationFunctionType
AX = mybir.AxisListType

P = 128
S = 512
NT = S // P
D = 1024
KT = D // P
EPS = 1e-6

HEADS = 4
HD = 256
WINDOWS = (2, 4, 8, 16)
TAPS = 5
UPAD = 2
US = S + 2 * UPAD

HQ = 16
DH = 64
NG = 4
CMP = 31
CP = 32
CLEN = 32
FF = 2816
FT = FF // P
FTAPS = 3

RAW = 4
SPL = 2

STAGES = [("in", 32), ("wo_pool", 8), ("wo_m", 8), ("nsa", 21), ("nsa_o", 8), ("gu0", 2 * FT),
          ("down0", FT), ("swa", 10), ("swa_o", 8), ("gu1", 2 * FT), ("down1", FT)]
W0, T0, _w, _t = {}, {}, 0, 0
for _name, _n in STAGES:
    W0[_name], T0[_name] = _w, _t
    _w += _n
    _t += 0 if _name.startswith("down") else _n
NW = _w

XST = [("in", 8), ("wo_pool", 8), ("wo_m", 8), ("nsa", 8), ("nsa_o", 8), ("gu0", 8), ("down0", FT),
       ("swa", 8), ("swa_o", 8), ("gu1", 8), ("down1", FT)]
X0, _x = {}, 0
for _name, _n in XST:
    X0[_name] = _x
    _x += _n

COLS, _c = {}, 0
for _name, _n in [("g_in", 8), ("g_out", 8), ("pool_scale", 8), ("conv_w", 40), ("conv_b", 8), ("mh", 8),
                  ("skip", 8), ("b_gates", 1), ("g_mix0", 8), ("g_mix1", 8), ("g_ffn0", 8), ("g_ffn1", 8),
                  ("g_fin", 8), ("b_q", 8), ("b_k", 1), ("b_o", 8), ("fcw0", 3 * FT), ("fcw1", 3 * FT),
                  ("fcb0", FT), ("fcb1", FT), ("pe_k", 32), ("pe_v", 32)]:
    COLS[_name] = _c
    _c += _n
NCOL = _c

ROWS = {"gate_b": (0, 48), "b_v": (48, 128), "sinks": (176, 16)}
NROW = 192

NSA_UNITS = [(c, m, i) for c in range(8) for m in range(2) for i in range(NT)]
SWA_UNITS = [(c, 0, i) for c in range(8) for i in range(NT)]


class Steps:

    def __init__(self, eng, sem):
        self.eng, self.sem, self.n, self.off = eng, sem, 0, 0

    def mark(self, ins):
        ins.then_inc(self.sem, 1)
        self.n += 1
        return self.n

    def wait(self, n=None):
        self.eng.wait_ge(self.sem, self.off + (self.n if n is None else n))


def build(nc, a):
    with ExitStack() as ctx:
        def sb(name, shape, dt=F32):
            return ctx.enter_context(nc.sbuf_tensor("sb_" + name, shape, dt))

        def sem(name):
            return ctx.enter_context(nc.semaphore(name))

        R = sb("resid", [P, KT, S])
        XH = sb("x_hi", [P, KT, S], F32R)
        XL = sb("x_lo", [P, KT, S], F32R)
        raw = sb("raw", [P, RAW, KT, P])
        WH = sb("w_hi", [P, SPL, KT, P], F32R)
        WL = sb("w_lo", [P, SPL, KT, P], F32R)
        cols = sb("cols", [P, NCOL])
        rows = sb("rows", [P, NROW])
        ident = sb("ident", [P, P])
        ones = sb("ones", [P, P])
        identb = sb("identb", [P, P], BF16)
        masks = sb("masks", [P, 3, P], BF16)
        cmask = sb("cmask", [P, NT, CP], BF16)
        rstd = sb("rstd", [P, S])
        small = sb("small", [P, 160])
        PS = ctx.enter_context(nc.psum_tensor("ps", [P, 8, S], F32))
        NA = 30712
        arena = sb("arena", [P, NA])

        def col(name, k=0):
            return cols[:, COLS[name] + k:COLS[name] + k + 1]

        def carve(at, *shape):
            n = int(np.prod(shape))
            v = arena[:, at:at + n]
            if len(shape) == 2:
                v = v.rearrange("p (a b) -> p a b", b=shape[1])
            if len(shape) == 3:
                v = v.rearrange("p (a b c) -> p a b c", b=shape[1], c=shape[2])
            if len(shape) == 4:
                v = v.rearrange("p (a b c d) -> p a b c d", b=shape[1], c=shape[2], d=shape[3])
            return v

        o_u, o_mz, o_c, o_q, o_k, o_v = 0, 4128, 8224, 12320, 16416, 20512
        o_b = o_v + NT * HEADS * 257
        o_nm = o_b + 4608
        U = carve(o_u, KT, US)
        H = carve(o_u, NT, 1024)
        MZ = carve(o_mz, KT, S)
        px = [carve(o_mz + 544 * i, 544) for i in range(3)]
        C = carve(o_c, KT, S)
        Q1, K1 = carve(o_q, KT, S), carve(o_k, KT, S)
        pooled, SZ = Q1, K1
        V1 = carve(o_v, NT, HEADS, 257)
        poolw = carve(o_v, 16, P)
        invc = carve(o_v + 2048, 4, S)
        BD = [carve(o_b + 1024 * i, KT, 32, 4) for i in range(3)]
        wg = carve(o_b + 3072, 24, 16)
        VT = carve(o_b + 3456, 2, S)
        PW = [carve(o_b, 1280), carve(o_b + 1280, 1280)]
        WD = carve(o_b + 2560, 2, NT, P)
        WE = carve(o_b + 3584, 2, S)
        NM = carve(o_nm, S)
        ACOL = carve(o_nm + S, 8, DH)
        wqkv = carve(o_c, 3, KT, 4)
        bdm = carve(o_c + 96, 32)
        place_w = carve(o_nm, P)
        masks32, cmask32 = carve(o_q, 3, P), carve(o_q + 384, NT, CP)
        G16 = carve(o_u, S)
        gr = [carve(o_u + S * (i + 1), S) for i in range(6)]
        one5 = carve(o_u + S * 7, S)
        SQ, RMS = carve(0, 2, S), carve(1024, S)

        o = 1536
        cs, sn = carve(o, S), carve(o + 512, S)
        csr, snr = carve(o + 1024, S), carve(o + 1536, S)
        QN = carve(o + 2048, KT, S)
        KC, VC = carve(o + 6144, 2, S), carve(o + 7168, 2, S)
        KS, KW = carve(o + 8192, 2, S), carve(o + 9216, 2, S)
        VS, VW = carve(o + 10240, NT, NG, 65), carve(o + 11280, NT, NG, 65)
        CW1 = [carve(o + 12320 + 4096 * i, 16, 2 * P) for i in range(2)]
        OA = carve(o + 12320, NT, 8, 2, DH)
        XB = [carve(o + 20512 + 2048 * i, 16, NG, CP) for i in range(2)]
        PE_ = carve(o + 20512, 2, 2, S)
        PT_ = carve(o + 20512 + 2048, 2, 2, S)
        o2 = o + 24608
        CW2 = carve(o2, 2, 2, P)
        HID = [carve(o2 + 512 + 256 * i, 2, NG, CP) for i in range(2)]
        HIDR = carve(o2 + 1024, 2 * NG, 4, CP)
        KCC = carve(o2 + 2048, NG, CP)
        BDV = carve(o2 + 2176, NG, 4, DH)
        TS, TM = carve(o2 + 3200, S), carve(o2 + 3712, S)
        GT = carve(o2 + 4224, NT, 48)
        SX, PTC = carve(o + 20512, HQ, CP), carve(o + 22560, NG, P)
        assert o2 + 4416 <= NA
        MID = carve(o, FT, S)
        AP_ = carve(o + 11264, 2, S + 2)
        CV = carve(o + 12292, 2, S)
        SA = carve(o + 13316, 2, S)
        TU = carve(o + 14340, 2, S)

        TB = KW
        rcol = small[:, 0:4]
        nmx = small[:, 4:12].rearrange("p (a b) -> p a b", b=2)
        nmr = small[:, 12:20].rearrange("p (a b) -> p a b", b=2)
        esk = small[:, 20:28].rearrange("p (a b) -> p a b", b=2)
        ske = small[:, 28:36].rearrange("p (a b) -> p a b", b=2)
        rec = small[:, 36:44].rearrange("p (a b) -> p a b", b=2)
        nsk = small[:, 44:60]
        cst = small[:, 60:108].rearrange("p (a b) -> p a b", b=16)
        bn6 = small[:, 108:114]
        zero = sb("zero", [P, KT])[:, :]
        mv = sb("mv", [P, 16, 2])
        rv = sb("rv", [P, 16])
        dn = sb("dn", [P, 4])

        consts_in = sem("consts_in")
        x_in = sem("x_in")
        raw_in = [sem(f"raw_in{i}") for i in range(RAW)]
        zero_set = sem("zero_set")
        hi_made = sem("hi_made")
        tile_split = sem("tile_split")
        tile_used = sem("tile_used")
        freed = sem("freed")
        xh_ready, xl_ready = sem("xh_ready"), sem("xl_ready")
        sq_ready, sq_sum, rms_ready, std_ready = sem("sq_ready"), sem("sq_sum"), sem("rms_ready"), sem("std_ready")
        rstd_ready = sem("rstd_ready")
        dve_step = sem("dve_step")
        act_step = sem("act_step")
        normed = sem("normed")
        down_added = sem("down_added")
        bd_ready = sem("bd_ready")
        pool_in = sem("pool_in")
        conv_ready, c_ready, mz_raw, mz_ready = sem("conv_ready"), sem("c_ready"), sem("mz_raw"), sem("mz_ready")
        pooled_ready, sz_ready, pool_mm, yp_ready = sem("pooled_ready"), sem("sz_ready"), sem("pool_mm"), sem("yp_ready")
        q_mm, q_out, vt_mm, vt_out, gate_mm, g16 = (sem(x) for x in ("q_mm", "q_out", "vt_mm", "vt_out", "gate_mm", "g16"))
        g_placed, f_rest, nm_ready, fm_ready, emt_ready, cols_mm, acol_ready = (
            sem(x) for x in ("g_placed", "f_rest", "nm_ready", "fm_ready", "emt_ready", "cols_mm", "acol_ready"))
        a_ready = sem("a_ready")
        m_bc, s_mm1, wd_ready, w_exp, p_ready, num_mm, num_out = (
            sem(x) for x in ("m_bc", "s_mm1", "wd_ready", "w_exp", "p_ready", "num_mm", "num_out"))
        var_ready, hstd, xhat, yt_mm, skip_ready, ym_ready = (
            sem(x) for x in ("var_ready", "hstd", "xhat", "yt_mm", "skip_ready", "ym_ready"))
        rope_in, rc_mm, kv_ready, q_ready = sem("rope_in"), sem("rc_mm"), sem("kv_ready"), sem("q_ready")
        tok_ready = sem("tok_ready")
        gt_raw, gt_ready = sem("gt_raw"), sem("gt_ready")
        xb_ready, hid_mm, hid_ready, cmp_mm, cmp_ready = (
            sem(x) for x in ("xb_ready", "hid_mm", "hid_ready", "cmp_mm", "cmp_ready"))
        cs_mm, cs_arg, cs_exp, cs_norm, cs_t, cs_tout, cs_o, cs_out = (
            sem(x) for x in ("cs_mm", "cs_arg", "cs_exp", "cs_norm", "cs_t", "cs_tout", "cs_o", "cs_out"))
        s_mm, nmax, p_exp, pt_mm, pt_d, pt_a, o_mm, o_done = (
            sem(x) for x in ("s_mm", "nmax", "p_exp", "pt_mm", "pt_d", "pt_a", "o_mm", "o_done"))
        oa_mm = sem("oa_mm")
        qb_raw, qb_ready = sem("qb_raw"), sem("qb_ready")
        ff_conv, ff_silu, mid_ready, down_mm = sem("ff_conv"), sem("ff_silu"), sem("mid_ready"), sem("down_mm")
        out_ready, out_done = sem("out_ready"), sem("out_done")

        block = ctx.enter_context(nc.Block())

        def psum(bank, n=S):
            return PS[:, bank, 0:n]

        def xst(name):
            return X0[name]

        @block.sync
        def _(sp):
            for k in range(KT):
                sp.dma_start(R[:, k, :], a["x"][:, k, :]).then_inc(x_in, 16)

            def load(it, s, first=False):
                if not first:
                    sp.wait_ge(tile_split, 4 * it + (s - RAW + 1))
                sp.dma_start(raw[:, s], a["w"][bass.ds(4 * it + s, 1)].rearrange("o p k m -> (o p) k m")
                             ).then_inc(raw_in[s], 16)

            for s in range(RAW):
                load(0, s, first=True)
            with sp.Fori(1, NW // RAW) as it:
                for s in range(RAW):
                    load(it, s)
            for s in range(NW % RAW):
                load(NW // RAW, s)
            for k in range(KT):
                sp.wait_ge(normed, KT + k + 1)
                sp.dma_start(a["out"][:, k, :], R[:, k, :]).then_inc(out_done, 16)
            sp.wait_ge(out_done, 16 * KT)

        @block.gpsimd
        def _(pool):
            def split(it, s, first=False):
                pool.wait_ge(raw_in[s], 16 * (it + 1))
                if not first:
                    pool.wait_ge(tile_used, 4 * it + (s - SPL + 1))
                nc.gpsimd.tensor_tensor(WH[:, s % SPL], raw[:, s], zero.unsqueeze(2).broadcast_to([P, KT, P]), ALU.add
                                        ).then_inc(hi_made, 1)
                pool.wait_ge(hi_made, 4 * it + (s + 1))
                nc.gpsimd.tensor_tensor(WL[:, s % SPL], raw[:, s], WH[:, s % SPL].bitcast(F32),
                                        ALU.subtract).then_inc(tile_split, 1)

            nc.gpsimd.memset(zero, 0.0).then_inc(zero_set, 1)
            pool.wait_ge(zero_set, 1)
            for s in range(RAW):
                split(0, s, first=s < SPL)
            with pool.Fori(1, NW // RAW) as it:
                for s in range(RAW):
                    split(it, s)
            for s in range(NW % RAW):
                split(NW // RAW, s)

        @block.scalar
        def _(act):
            step = Steps(act, act_step)
            for dst, name in ((cols[:], "cols"), (ones[:], "ones"), (wqkv, "wqkv"), (bdm, "bdm"), (poolw, "pool_w"),
                              (invc, "invc"), (wg, "wg"), (ident[:], "ident"), (rows[:], "rows"),
                              (masks32, "masks"), (cmask32, "cmask"),
                              (place_w[0:16], "place")):
                act.dma_start(dst, a[name]).then_inc(consts_in, 16)

            def norm(q, ready, gain=None, x=None, used=0):
                for k in range(KT):
                    act.wait_ge(*ready(k))
                    if 8 * q + k >= 2:
                        act.wait_ge(sq_sum, 8 * q + k - 1)
                    nc.scalar.activation(SQ[:, k % 2], R[:, k], ACT.Square).then_inc(sq_ready, 1)
                    if gain:
                        if used and k == 0:
                            act.wait_ge(tile_used, used)
                        nc.scalar.mul(XH[:, k], R[:, k], col(gain, k)).then_inc(xh_ready, 1)
                act.wait_ge(rms_ready, q + 1)
                nc.scalar.activation(RMS, RMS, ACT.Sqrt).then_inc(std_ready, 1)

            act.wait_ge(consts_in, 16 * 12)
            norm(0, lambda k: (x_in, 16 * KT), "g_in")
            for j in range(KT):
                act.wait_ge(conv_ready, j + 1)
                nc.scalar.activation(C[:, j], C[:, j], ACT.Silu).then_inc(c_ready, 1)
            for j in range(KT):
                act.wait_ge(freed, 16 + j + 1)
                nc.scalar.activation(SZ[:, j], SZ[:, j], ACT.Silu).then_inc(sz_ready, 1)
            for j in range(KT):
                act.wait_ge(freed, 24 + j + 1)
                nc.scalar.activation(MZ[:, j], MZ[:, j], ACT.Silu).then_inc(mz_ready, 1)
            act.wait_ge(tile_used, W0["wo_pool"])
            for k in range(KT):
                act.wait_ge(yp_ready, k + 1)
                nc.scalar.copy(XH[:, k], SZ[:, k]).then_inc(xh_ready, 1)
            act.wait_ge(xl_ready, X0["wo_pool"] + KT)
            for j in range(KT):
                act.wait_ge(q_mm, 3 * j + 1)
                nc.scalar.copy(Q1[:, j], psum(2)).then_inc(q_out, 1)
                act.wait_ge(q_mm, 3 * j + 2)
                nc.scalar.copy(K1[:, j], psum(3)).then_inc(q_out, 1)
                act.wait_ge(q_mm, 3 * j + 3)
                if j >= 2:
                    act.wait_ge(gate_mm, j - 1)
                nc.scalar.copy(VT[:, j % 2], psum(4)).then_inc(q_out, 1)
            act.wait_ge(gate_mm, KT)
            nc.scalar.activation(G16[0:16], PS[0:16, 7, :], ACT.Identity, bias=cols[0:16, COLS["b_gates"]:COLS["b_gates"] + 1]
                                 ).then_inc(g16, 1)
            act.wait_ge(g_placed, 1)
            t = gr[1]
            step.mark(nc.scalar.activation(t[64:128], PS[64:128, 6, :], ACT.Abs))
            step.wait()
            step.mark(nc.scalar.activation(t[64:128], t[64:128], ACT.Exp, scale=-1.0))
            step.wait()
            nc.scalar.activation(t[64:128], t[64:128], ACT.Ln, bias=1.0).then_inc(f_rest, 1)
            act.wait_ge(fm_ready, 1)
            nc.scalar.activation(gr[5][0:64], gr[4][0:64], ACT.Exp, scale=-1.0).then_inc(emt_ready, 1)
            act.wait_ge(acol_ready, 1)
            for h in range(HEADS):
                act.wait_ge(wd_ready, 2 * (h + 1))
                for j in range(NT):
                    for d in range(2):
                        n = 8 * h + 2 * j + d
                        if n >= 2:
                            act.wait_ge(p_ready, n - 1)
                        bias = ACOL[:, j, 32 * d + h:32 * d + h + 1]
                        w = WE[:, n % 2]
                        dg, rest = (0, P) if d == 0 else (P * j, 0)
                        others = (P * (j + 1), S) if d == 0 else (0, P * j)
                        if others[1] > others[0]:
                            nc.scalar.activation(w[:, rest:rest + others[1] - others[0]],
                                                 PS[:, 6 + d, others[0]:others[1]], ACT.Exp, bias=bias)
                        nc.scalar.activation(w[:, dg:dg + P], WD[:, d, j], ACT.Exp, bias=bias).then_inc(w_exp, 1)
            for j in range(KT):
                nc.scalar.mul(C[:, j], C[:, j], col("skip", j)).then_inc(skip_ready, 1)
            act.wait_ge(var_ready, 1)
            nc.scalar.activation(rv[:], rv[:], ACT.Sqrt).then_inc(hstd, 1)
            act.wait_ge(tile_used, W0["wo_m"])
            for k in range(KT):
                act.wait_ge(ym_ready, k + 1)
                nc.scalar.copy(XH[:, k], MZ[:, k]).then_inc(xh_ready, 1)
            act.wait_ge(xl_ready, X0["wo_m"] + KT)
            for dst, name in ((cs, "cos"), (sn, "sin"), (CW1[0], "cmp_w1k"), (CW1[1], "cmp_w1v"), (CW2, "cmp_w2")):
                act.dma_start(dst, a[name]).then_inc(consts_in, 16)
            norm(1, lambda k: (freed, T0["wo_m"] + k + 1))
            norm(2, lambda k: (normed, k + 1), "g_mix0", used=W0["nsa"])
            for i in range(NT):
                act.wait_ge(freed, T0["nsa"] + 21)
                nc.scalar.activation(GT[:, i], GT[:, i], ACT.Sigmoid).then_inc(gt_ready, 1)
            for kv in range(2):
                act.wait_ge(hid_mm, kv + 1)
                nc.scalar.activation(HID[kv], PS[:, 2 + kv, 0:2 * P].rearrange("p (a b c) -> p a b c", a=2, b=NG),
                                     ACT.Gelu_apprx_tanh).then_inc(hid_ready, 1)
            for i in range(NT):
                act.wait_ge(cs_arg, i + 1)
                nc.scalar.activation(SX, SX, ACT.Exp).then_inc(cs_exp, 1)
                act.wait_ge(cs_t, i + 1)
                nc.scalar.copy(PTC, psum(6).rearrange("p (g t) -> p g t", g=NG)).then_inc(cs_tout, 1)
                for g in range(NG):
                    act.wait_ge(cs_o, 4 * i + 2 * (g // 2) + 2)
                    ins = nc.scalar.copy(OA[:, i, 4 * (g // 2):4 * (g // 2) + 4, g % 2, :],
                                         PS[:, 4 + g // 2, 256 * (g % 2):256 * (g % 2) + 256].rearrange(
                                             "p (r d) -> p r d", r=4))
                    ins.then_inc(cs_out, 1)

            def n_keys(i, swa):
                return P * min(i + 1, 2) if swa else P * (i + 1)

            def attention(units, v0, swa):
                def exps(v):
                    n = n_keys(units[v - v0][2], swa)
                    act.wait_ge(nmax, v + 1)
                    if v >= 2:
                        act.wait_ge(pt_mm, v - 1)
                    if swa:
                        act.wait_ge(qb_raw, v - v0 + 1)
                        nc.scalar.activation(esk[:, v % 4], ske[:, v % 4], ACT.Exp)
                    nc.scalar.activation(PE_[:, v % 2, 0, 0:n], PS[:, 2 + 2 * (v % 2), 0:n], ACT.Exp,
                                         bias=nmr[:, v % 4, 0:1])
                    nc.scalar.activation(PE_[:, v % 2, 1, 0:n], PS[:, 3 + 2 * (v % 2), 0:n], ACT.Exp,
                                         bias=nmr[:, v % 4, 1:2]).then_inc(p_exp, 1)

                def evac(v):
                    n = n_keys(units[v - v0][2], swa)
                    act.wait_ge(pt_mm, v + 1)
                    if v >= 2:
                        act.wait_ge(o_mm, v - 1)
                    nc.scalar.copy(PT_[:, v % 2, 1, 0:n], psum(7, n)).then_inc(pt_a, 1)

                last = v0 + len(units)
                exps(v0)
                for v in range(v0, last):
                    if v + 1 < last:
                        exps(v + 1)
                    evac(v)

            def attention_out(stage, n0):
                act.wait_ge(tile_used, W0[stage])
                for c in range(KT):
                    act.wait_ge(oa_mm, n0 + c + 1)
                    nc.scalar.copy(XH[:, c], psum(2 + c % 2)).then_inc(xh_ready, 1)

            def ffn(layer):
                with act.Fori(0, FT // 2) as it:
                    for b in range(2):
                        act.wait_ge(ff_conv, layer * FT + 2 * it + (b + 1))
                        nc.scalar.activation(SA[:, b], CV[:, b], ACT.Silu).then_inc(ff_silu, 1)
                x0, w0, wd = X0[f"down{layer}"], W0[f"gu{layer}"], W0[f"down{layer}"]
                for f in range(FT):
                    if f < 4:
                        act.wait_ge(tile_used, wd)
                    else:
                        act.wait_ge(tile_used, wd + f - 3)
                    act.wait_ge(mid_ready, layer * FT + f + 1)
                    nc.scalar.copy(XH[:, f % 4], MID[:, f]).then_inc(xh_ready, 1)

            attention(NSA_UNITS, 0, False)
            attention_out("nsa_o", 0)
            norm(3, lambda k: (freed, T0["nsa_o"] + k + 1), "g_ffn0", used=W0["gu0"])
            ffn(0)
            act.wait_ge(mid_ready, FT)
            act.wait_ge(tile_used, W0["swa"])
            for dst, name in ((cs, "cos"), (sn, "sin")):
                act.dma_start(dst, a[name]).then_inc(consts_in, 16)
            norm(4, lambda k: (down_added, k + 1), "g_mix1", used=W0["swa"])
            for j in range(9):
                act.wait_ge(freed, T0["swa"] + j + 1)
                b = TB[:, j % 2]
                nc.scalar.activation(b, b, ACT.Identity, bias=col("b_k") if j == 0 else col("b_q", j - 1)
                                     ).then_inc(qb_ready, 1)
            attention(SWA_UNITS, len(NSA_UNITS), True)
            attention_out("swa_o", KT)
            norm(5, lambda k: (freed, T0["swa_o"] + k + 1), "g_ffn1", used=W0["gu1"])
            ffn(1)
            norm(6, lambda k: (down_added, KT + k + 1))

        @block.vector
        def _(dve):
            step = Steps(dve, dve_step)

            def norm(q, x=None, gain=None):
                if gain:
                    for k in range(KT):
                        dve.wait_ge(xh_ready, X0[x] + k + 1)
                        nc.vector.scalar_tensor_tensor(XL[:, k], R[:, k], col(gain, k), XH[:, k].bitcast(F32),
                                                       ALU.mult, ALU.subtract).then_inc(xl_ready, 1)
                if q == 2:
                    dve.wait_ge(normed, KT)
                dve.wait_ge(sq_sum, 8 * (q + 1))
                nc.vector.tensor_scalar(RMS, psum(7), 1.0 / D, EPS, ALU.mult, ALU.add).then_inc(rms_ready, 1)
                dve.wait_ge(std_ready, q + 1)
                nc.vector.reciprocal(rstd[:], RMS).then_inc(rstd_ready, 1)
                dve.wait_ge(rstd_ready, q + 1)

            def product(stage, j):
                dve.wait_ge(tile_used, W0[stage] + j + 1)
                return (T0[stage] + j) % 2

            def lo(stage, k, src):
                dve.wait_ge(xh_ready, X0[stage] + k + 1)
                nc.vector.tensor_tensor(XL[:, k], src, XH[:, k].bitcast(F32), ALU.subtract).then_inc(xl_ready, 1)

            def add_residual(stage, bias=None):
                for k in range(KT):
                    b = product(stage, k)
                    if bias:
                        ins = nc.vector.scalar_tensor_tensor(R[:, k], psum(b), col(bias, k), R[:, k], ALU.add, ALU.add)
                    else:
                        ins = nc.vector.tensor_tensor(R[:, k], psum(b), R[:, k], ALU.add)
                    ins.then_inc(freed, 1)

            def norm_in_place(gain, n0):
                for k in range(KT):
                    nc.vector.scalar_tensor_tensor(R[:, k], R[:, k], col(gain, k), rstd[:], ALU.mult, ALU.mult
                                                   ).then_inc(normed, 1)

            dve.wait_ge(consts_in, 16 * 12)
            for n in range(3):
                step.mark(nc.vector.tensor_tensor(
                    BD[n], wqkv[:, n].unsqueeze(2).broadcast_to([P, KT, 32, 4]),
                    bdm.unsqueeze(1).unsqueeze(3).broadcast_to([P, KT, 32, 4]), ALU.mult))
            for dst, src in ((identb[:], ident[:]), (masks[:], masks32), (cmask[:], cmask32)):
                step.mark(nc.vector.tensor_copy(dst, src))
            norm(0, "in", "g_in")
            step.mark(nc.vector.memset(U[:, :, 0:UPAD], 0.0))
            step.mark(nc.vector.memset(U[:, :, US - UPAD:US], 0.0))
            for p in px:
                step.mark(nc.vector.memset(p, 0.0))
            step.wait()
            for j in range(KT):
                b = product("in", j)
                nc.vector.tensor_tensor(U[:, j, UPAD:UPAD + S], psum(b), rstd[:], ALU.mult).then_inc(freed, 1)
                dve.wait_ge(freed, j + 1)
                step.mark(nc.vector.tensor_scalar(C[:, j], U[:, j, 0:S], col("conv_w", j), col("conv_b", j), ALU.mult, ALU.add))
                for t in range(1, TAPS):
                    step.wait()
                    ins = nc.vector.scalar_tensor_tensor(C[:, j], U[:, j, t:t + S], col("conv_w", 8 * t + j), C[:, j],
                                                         ALU.mult, ALU.add)
                    if t < TAPS - 1:
                        step.mark(ins)
                    else:
                        ins.then_inc(conv_ready, 1)
            for j in range(KT):
                w = WINDOWS[j // 2]
                left = (w - 1) // 2
                b = product("in", 8 + j)
                x, s0, s1 = px
                if j >= 1:
                    dve.wait_ge(pooled_ready, j)
                nc.vector.tensor_tensor(x[:, 8:8 + S], psum(b), rstd[:], ALU.mult).then_inc(freed, 1)
                dve.wait_ge(freed, 8 + j + 1)
                src, dst, width, sh = x, s0, 536, 1
                while sh < w:
                    width -= sh
                    step.mark(nc.vector.tensor_tensor(dst[:, 0:width], src[:, 0:width], src[:, sh:sh + width], ALU.add))
                    step.wait()
                    src, dst, sh = dst, (s1 if dst is s0 else s0), 2 * sh
                step.mark(nc.vector.tensor_tensor(dst[:, 0:S], src[:, 8 - left:8 - left + S], invc[:, j // 2], ALU.mult))
                step.wait()
                nc.vector.tensor_tensor(pooled[:, j], dst[:, 0:S], x[:, 8:8 + S], ALU.subtract).then_inc(pooled_ready, 1)
            for j in range(KT):
                b = product("in", 16 + j)
                nc.vector.tensor_tensor(SZ[:, j], psum(b), rstd[:], ALU.mult).then_inc(freed, 1)
            dve.wait_ge(pooled_ready, KT)
            for j in range(KT):
                b = product("in", 24 + j)
                nc.vector.tensor_tensor(MZ[:, j], psum(b), rstd[:], ALU.mult).then_inc(freed, 1)
            for j in range(KT):
                dve.wait_ge(pool_mm, j + 1)
                dve.wait_ge(sz_ready, j + 1)
                nc.vector.scalar_tensor_tensor(SZ[:, j], psum(2 + j % 2), col("pool_scale", j), SZ[:, j], ALU.mult, ALU.mult
                                               ).then_inc(yp_ready, 1)
            for k in range(KT):
                lo("wo_pool", k, SZ[:, k])
            nc.vector.memset(V1[:, :, :, 256:257], 1.0)
            for j in range(KT):
                dve.wait_ge(vt_mm, j + 1)
                nc.vector.tensor_copy(V1[:, :, j // 2, P * (j % 2):P * (j % 2) + P],
                                      psum(5).rearrange("p (t e) -> p t e", t=NT)).then_inc(vt_out, 1)
            lf, t, F, A, FM, EM = gr
            dve.wait_ge(g_placed, 1)
            step.mark(nc.vector.memset(one5, 1.0))
            dve.wait_ge(f_rest, 1)
            step.mark(nc.vector.scalar_tensor_tensor(lf[64:128], PS[64:128, 6, :], 0.0, t[64:128], ALU.min, ALU.subtract))
            step.wait()
            step.mark(nc.vector.tensor_tensor_scan(F[0:32], one5[64:96], lf[64:96], 0.0, ALU.mult, ALU.add))
            step.mark(nc.vector.tensor_tensor_scan(F[32:64, ::-1], one5[96:128, ::-1], lf[96:128, ::-1], 0.0, ALU.mult, ALU.add))
            step.wait()
            nc.vector.tensor_tensor(A[0:64], PS[0:64, 6, :], F[0:64], ALU.subtract).then_inc(a_ready, 1)
            dve.wait_ge(a_ready, 1)
            M = t
            step.mark(nc.vector.tensor_tensor_scan(M[0:32], one5[0:32], A[0:32], 0.0, ALU.mult, ALU.max))
            step.mark(nc.vector.tensor_tensor_scan(M[32:64, ::-1], one5[32:64, ::-1], A[32:64, ::-1], 0.0, ALU.mult, ALU.max))
            step.wait()
            nc.vector.tensor_scalar(NM[0:64], M[0:64], -1.0, None, ALU.mult).then_inc(nm_ready, 1)
            nc.vector.tensor_tensor(FM[0:64], F[0:64], M[0:64], ALU.add).then_inc(fm_ready, 1)
            add_residual("wo_pool")
            dve.wait_ge(cols_mm, 1)
            nc.vector.tensor_copy(ACOL, psum(7).rearrange("p (a b) -> p a b", b=64)).then_inc(acol_ready, 1)
            dve.wait_ge(acol_ready, 1)

            offs = [[0, 512, 896, 1152], [0, 128, 384, 768]]

            def weights(h):
                for d in range(2):
                    dve.wait_ge(m_bc, 2 * h + d + 1)
                    nc.vector.tensor_tensor(WD[:, d], psum(6 + d).rearrange("p (j t) -> p j t", j=NT),
                                            masks[:, d].unsqueeze(1).broadcast_to([P, NT, P]), ALU.add).then_inc(wd_ready, 1)
                if h >= 1:
                    dve.wait_ge(num_mm, 8 * h)
                for j in range(NT):
                    dve.wait_ge(s_mm1, NT * h + j + 1)
                    for d in range(2):
                        n = 8 * h + 2 * j + d
                        dve.wait_ge(w_exp, n + 1)
                        lo_, hi_ = (P * j, S) if d == 0 else (0, P * (j + 1))
                        nc.vector.scalar_tensor_tensor(PW[d][:, offs[d][j]:offs[d][j] + hi_ - lo_], PS[:, 2 + j, lo_:hi_],
                                                       float(HD) ** -0.5, WE[:, n % 2, 0:hi_ - lo_], ALU.mult, ALU.mult
                                                       ).then_inc(p_ready, 1)

            def head_out(h):
                for i in range(NT):
                    for d in range(2):
                        n = 8 * h + 2 * i + d
                        dve.wait_ge(num_mm, n + 1)
                        emt = ACOL[:, 4 + i, 32 * d + h:32 * d + h + 1]
                        b = n % 2
                        step.mark(nc.vector.tensor_scalar(dn[:, 0:1], PS[:, b, 256:257], -1.0, emt, ALU.mult, ALU.max))
                        step.wait()
                        step.mark(nc.vector.tensor_tensor(dn[:, 1:2], PS[:, b, 256:257], dn[:, 0:1], ALU.max))
                        step.wait()
                        step.mark(nc.vector.reciprocal(dn[:, 2:3], dn[:, 1:2]))
                        step.wait()
                        out = H[:, i, HD * h:HD * (h + 1)]
                        if d == 0:
                            nc.vector.tensor_scalar(out, PS[:, b, 0:HD], dn[:, 2:3], None, ALU.mult).then_inc(num_out, 1)
                        else:
                            nc.vector.scalar_tensor_tensor(out, PS[:, b, 0:HD], dn[:, 2:3], out, ALU.mult, ALU.add
                                                           ).then_inc(num_out, 1)
                        dve.wait_ge(num_out, n + 1)
                    step.mark(nc.vector.bn_stats(bn6, H[:, i, HD * h:HD * (h + 1)]))
                    step.wait()
                    step.mark(nc.vector.bn_aggr(mv[:, 4 * h + i], bn6))
                    step.wait()

            weights(0)
            for h in range(HEADS):
                head_out(h)
                if h + 1 < HEADS:
                    weights(h + 1)
            nc.vector.tensor_scalar(rv[:], mv[:, :, 1], EPS, None, ALU.add).then_inc(var_ready, 1)
            dve.wait_ge(hstd, 1)
            step.mark(nc.vector.reciprocal(rv[:], rv[:]))
            step.wait()
            for h in range(HEADS):
                for i in range(NT):
                    hh = H[:, i, HD * h:HD * (h + 1)]
                    nc.vector.tensor_scalar(hh, hh, mv[:, 4 * h + i, 0:1], rv[:, 4 * h + i:4 * h + i + 1],
                                            ALU.subtract, ALU.mult).then_inc(xhat, 1)
            for j in range(KT):
                dve.wait_ge(yt_mm, j + 1)
                dve.wait_ge(skip_ready, j + 1)
                dve.wait_ge(mz_ready, j + 1)
                step.mark(nc.vector.scalar_tensor_tensor(C[:, j], psum(2 + j % 2), col("mh", j), C[:, j], ALU.mult, ALU.add))
                step.wait()
                nc.vector.tensor_tensor(MZ[:, j], C[:, j], MZ[:, j], ALU.mult).then_inc(ym_ready, 1)
            for k in range(KT):
                lo("wo_m", k, MZ[:, k])
            add_residual("wo_m")
            norm(1)
            norm_in_place("g_out", 0)

            norm(2, "nsa", "g_mix0")
            dve.wait_ge(consts_in, 16 * 17)
            rotary_tables = [(csr, cs), (snr, sn)]
            for dst, src in rotary_tables:
                step.mark(nc.vector.tensor_tensor(dst, src, rstd[:], ALU.mult))
            for kv in range(2):
                step.mark(nc.vector.memset(XB[kv], 0.0))
            step.mark(nc.vector.memset(BDV, 0.0))
            step.mark(nc.vector.memset(VS[:, :, :, DH:DH + 1], 1.0))
            step.mark(nc.vector.memset(VW[:, :, :, DH:DH + 1], 1.0))
            step.wait()

            swap = [p ^ 16 for p in range(32)]
            ropes = [0]

            def rotary(src, c_, s_, out, scale, signal, first=None):
                if ropes[0]:
                    dve.wait_ge(rope_in, ropes[0])
                ropes[0] += 1
                step.mark(nc.vector.stream_shuffle(TS, src, swap))
                ins = nc.vector.scalar_tensor_tensor(TM, src, scale, c_, ALU.mult, ALU.mult)
                if signal is not None:
                    ins.then_inc(signal, 1)
                else:
                    step.mark(ins)
                step.wait()
                step.mark(nc.vector.scalar_tensor_tensor(TS, TS, scale, s_, ALU.mult, ALU.mult))
                step.wait()
                if signal is not None:
                    dve.wait_ge(signal, first)
                nc.vector.tensor_tensor(out, TM, TS, ALU.add).then_inc(rope_in, 1)

            def compression_input(kv, src):
                pe0 = COLS["pe_k" if kv == 0 else "pe_v"]
                for g in range(NG):
                    half = slice(DH * (g % 2), DH * (g % 2) + DH)
                    tok = src[half, g // 2].rearrange("p (c x two) -> p two x c", two=2, x=8)
                    pe = cols[half, pe0:pe0 + CLEN].rearrange("p (m two) -> p two m", two=2)
                    for par in range(2):
                        for mh in range(2):
                            ins = nc.vector.tensor_tensor(
                                XB[kv][DH * par:DH * par + DH, 8 * mh:8 * mh + 8, g, 0:CMP],
                                tok[:, par, :, mh:mh + CMP],
                                pe[:, par, 8 * mh:8 * mh + 8].unsqueeze(2).broadcast_to([DH, 8, CMP]), ALU.add)
                            ins.then_inc(xb_ready, 1)

            t0 = T0["nsa"]
            for j, out in ((0, KC[:, 0]), (1, KC[:, 1])):
                rotary(psum(product("nsa", j)), csr, snr, out, 1.0, freed, t0 + j + 1)
            for j in range(2):
                nc.vector.tensor_tensor(VC[:, j], psum(product("nsa", 2 + j)), rstd[:], ALU.mult).then_inc(freed, 1)
            for n, out in enumerate((KS[:, 0], KS[:, 1], KW[:, 0], KW[:, 1])):
                rotary(psum(product("nsa", 4 + n)), csr, snr, out, 1.0, freed, t0 + 5 + n)
            dve.wait_ge(rope_in, 6)
            dve.wait_ge(freed, t0 + 4)
            compression_input(0, KC)
            for n in range(4):
                rotary(psum(product("nsa", 8 + n)), csr, snr, QN[:, n], float(DH) ** -0.5, freed, t0 + 9 + n)
            compression_input(1, VC)
            for n in range(4, 8):
                rotary(psum(product("nsa", 8 + n)), csr, snr, QN[:, n], float(DH) ** -0.5, freed, t0 + 9 + n)
            dve.wait_ge(rc_mm, 1)
            step.mark(nc.vector.tensor_copy(rcol, psum(6).rearrange("p (t x) -> p t x", x=P)[:, :, 0]))
            step.wait()

            def values(stage, j, dst, bias=None):
                b = product(stage, j)
                for i in range(NT):
                    src = PS[:, b, P * i:P * (i + 1)]
                    if bias is None:
                        ins = nc.vector.tensor_scalar(dst(i), src.rearrange("p (g d) -> p g d", d=DH), rcol[:, i:i + 1],
                                                      None, ALU.mult)
                    else:
                        ins = nc.vector.scalar_tensor_tensor(dst(i), src.rearrange("p (g d) -> p g d", d=DH),
                                                             rcol[:, i:i + 1], bias, ALU.mult, ALU.add)
                    if i < NT - 1:
                        step.mark(ins)
                    else:
                        ins.then_inc(freed, 1)

            for n, V in ((0, VS), (1, VS), (2, VW), (3, VW)):
                values("nsa", 16 + n, lambda i, V=V, g=2 * (n % 2): V[:, i, g:g + 2, 0:DH])
            b = product("nsa", 20)
            for i in range(NT):
                ins = nc.vector.scalar_tensor_tensor(GT[:, i], PS[:, b, 48 * i:48 * (i + 1)], rcol[:, i:i + 1], rows[:, 0:48],
                                                     ALU.mult, ALU.add)
                if i < NT - 1:
                    step.mark(ins)
                else:
                    ins.then_inc(freed, 1)
            dve.wait_ge(hid_ready, 2)
            nc.vector.tensor_copy(HIDR, HID[1].rearrange("p a g c -> p (a g) c").unsqueeze(2).broadcast_to(
                [P, 2 * NG, 4, CP])).then_inc(kv_ready, 1)
            dve.wait_ge(cmp_mm, 1)
            nc.vector.tensor_copy(KCC, PS[:, 4, 0:P].rearrange("p (g c) -> p g c", g=NG)).then_inc(cmp_ready, 1)
            dve.wait_ge(cmp_mm, 2)
            for r in range(4):
                q = slice(32 * r, 32 * r + 32)
                nc.vector.tensor_copy(BDV[q, :, r, :], PS[q, 5, 0:256].rearrange("p (g d) -> p g d", g=NG)).then_inc(cmp_ready, 1)
            dve.wait_ge(gt_ready, NT)
            for i in range(NT):
                dve.wait_ge(cs_mm, i + 1)
                if i >= 1:
                    dve.wait_ge(cs_norm, i)
                s_ = PS[:, 2:4, 0:256].rearrange("p o (h c) -> p o h c", c=CP)
                step.mark(nc.vector.tensor_reduce(cst[:, 0], s_, AX.X, ALU.max, negate=True))
                step.wait()
                step.mark(nc.vector.tensor_scalar(cst[:, 0], cst[:, 0], 1e20, None, ALU.min))
                step.wait()
                if i >= 1:
                    dve.wait_ge(cs_t, i)
                nc.vector.tensor_tensor(SX.rearrange("p (o h) c -> p o h c", o=2), s_,
                                        cst[:, 0].rearrange("p (o h) -> p o h", o=2).unsqueeze(3).broadcast_to([P, 2, HQ // 2, CP]),
                                        ALU.add).then_inc(cs_arg, 1)
                dve.wait_ge(cs_exp, i + 1)
                step.mark(nc.vector.tensor_reduce(cst[:, 1], SX, AX.X, ALU.add))
                step.wait()
                step.mark(nc.vector.tensor_scalar(cst[:, 1], cst[:, 1], 1e-30, None, ALU.max))
                step.wait()
                step.mark(nc.vector.reciprocal(cst[:, 2], cst[:, 1]))
                step.wait()
                step.mark(nc.vector.tensor_tensor(
                    cst[:, 2].rearrange("p (o g r) -> p o g r", o=2, g=2), cst[:, 2].rearrange("p (o g r) -> p o g r", o=2, g=2),
                    GT[:, i].rearrange("p (g o r m) -> p o g r m", g=2, o=2, m=3)[:, :, :, :, 0], ALU.mult))
                step.wait()
                nc.vector.tensor_tensor(SX, SX, cst[:, 2].unsqueeze(2).broadcast_to([P, HQ, CP]), ALU.mult).then_inc(cs_norm, 1)

            def attention(units, v0, swa):
                def maxima(v):
                    c, m, i = units[v - v0]
                    n = P * min(i + 1, 2) if swa else P * (i + 1)
                    dve.wait_ge(s_mm, v + 1)
                    b = 2 + 2 * (v % 2)
                    s_ = PS[:, b:b + 2, 0:n]
                    if not swa:
                        nc.vector.tensor_reduce(nmr[:, v % 4], s_, AX.X, ALU.max, negate=True).then_inc(nmax, 1)
                        return
                    step.mark(nc.vector.tensor_reduce(nmx[:, v % 4], s_, AX.X, ALU.max, negate=True))
                    step.wait()
                    nc.vector.tensor_tensor(nmr[:, v % 4], nmx[:, v % 4], nsk.rearrange("p (a b) -> p a b", a=2)[:, :, c],
                                            ALU.min).then_inc(nmax, 1)
                    dve.wait_ge(nmax, v + 1)
                    nc.vector.tensor_tensor(ske[:, v % 4], nmr[:, v % 4], nsk.rearrange("p (a b) -> p a b", a=2)[:, :, c],
                                            ALU.subtract).then_inc(qb_raw, 1)

                def evac(v):
                    c, m, i = units[v - v0]
                    n = P * min(i + 1, 2) if swa else P * (i + 1)
                    dve.wait_ge(pt_mm, v + 1)
                    if v >= 2:
                        dve.wait_ge(o_mm, v - 1)
                    nc.vector.tensor_copy(PT_[:, v % 2, 0, 0:n], psum(6, n)).then_inc(pt_d, 1)

                def output(v):
                    c, m, i = units[v - v0]
                    dve.wait_ge(o_mm, v + 1)
                    o_ = PS[:, v % 2, 0:130].rearrange("p (a b) -> p a b", b=65)
                    if swa:
                        dve.wait_ge(p_exp, v + 1)
                        step.mark(nc.vector.tensor_tensor(rec[:, 2], o_[:, :, DH], esk[:, v % 4], ALU.add))
                        step.wait()
                        step.mark(nc.vector.reciprocal(rec[:, 0], rec[:, 2]))
                    else:
                        step.mark(nc.vector.reciprocal(rec[:, 0], o_[:, :, DH]))
                    step.wait()
                    w = rec[:, 0]
                    if not swa:
                        g = GT[:, i].rearrange("p (g x) -> p g x", x=12)[:, 2 * (c // 4):2 * (c // 4) + 2, 3 * (c % 4) + 1 + m]
                        step.mark(nc.vector.tensor_tensor(rec[:, 1], rec[:, 0], g, ALU.mult))
                        step.wait()
                        w = rec[:, 1]
                    for hh in range(2):
                        dst = OA[:, i, c, hh]
                        if swa:
                            ins = nc.vector.tensor_scalar(dst, o_[:, hh, 0:DH], w[:, hh:hh + 1], None, ALU.mult)
                        else:
                            ins = nc.vector.scalar_tensor_tensor(dst, o_[:, hh, 0:DH], w[:, hh:hh + 1], dst, ALU.mult, ALU.add)
                        if hh == 0:
                            step.mark(ins)
                        else:
                            ins.then_inc(o_done, 1)
                    dve.wait_ge(o_done, v + 1)

                last = v0 + len(units)
                maxima(v0)
                maxima(v0 + 1)
                evac(v0)
                for v in range(v0, last):
                    if v + 2 < last:
                        maxima(v + 2)
                    if v + 1 < last:
                        evac(v + 1)
                    output(v)

            def attention_out(stage, n0):
                for c in range(KT):
                    dve.wait_ge(oa_mm, n0 + c + 1)
                    lo(stage, c, psum(2 + c % 2))

            def ffn(layer):
                st, t0 = f"gu{layer}", T0[f"gu{layer}"]
                fcw = cols[:, COLS[f"fcw{layer}"]:COLS[f"fcw{layer}"] + 3 * FT]
                fcb = cols[:, COLS[f"fcb{layer}"]:COLS[f"fcb{layer}"] + FT]
                step.mark(nc.vector.memset(AP_[:, :, 0:2], 0.0))
                step.wait()
                before = step.n
                with dve.Fori(0, FT // 2) as it:
                    step.off = 4 * it
                    for b in range(2):
                        w = [fcw[:, bass.ds(t * FT + b + 2 * it, 1)] for t in range(3)]
                        bias = fcb[:, bass.ds(b + 2 * it, 1)]
                        bank = (t0 + 2 * b) % 2
                        dve.wait_ge(tile_used, W0[st] + 4 * it + (2 * b + 1))
                        nc.vector.tensor_tensor(AP_[:, b, 2:2 + S], psum(bank), rstd[:], ALU.mult).then_inc(freed, 1)
                        dve.wait_ge(freed, t0 + 4 * it + (2 * b + 1))
                        step.mark(nc.vector.tensor_scalar(CV[:, b], AP_[:, b, 0:S], w[0], bias, ALU.mult, ALU.add))
                        step.wait()
                        step.mark(nc.vector.scalar_tensor_tensor(CV[:, b], AP_[:, b, 1:1 + S], w[1], CV[:, b], ALU.mult, ALU.add))
                        step.wait()
                        nc.vector.scalar_tensor_tensor(CV[:, b], AP_[:, b, 2:2 + S], w[2], CV[:, b], ALU.mult, ALU.add
                                                       ).then_inc(ff_conv, 1)
                        dve.wait_ge(tile_used, W0[st] + 4 * it + (2 * b + 2))
                        nc.vector.tensor_tensor(TU[:, b], psum(1 - bank), rstd[:], ALU.mult).then_inc(freed, 1)
                        dve.wait_ge(freed, t0 + 4 * it + (2 * b + 2))
                        dve.wait_ge(ff_silu, layer * FT + 2 * it + (b + 1))
                        nc.vector.tensor_tensor(MID[:, bass.ds(2 * it + b, 1)].rearrange("p o t -> p (o t)"), TU[:, b], SA[:, b], ALU.mult).then_inc(mid_ready, 1)
                assert step.n - before == 4
                step.n, step.off = before + 4 * (FT // 2), 0
                for f in range(FT):
                    dve.wait_ge(xh_ready, X0[f"down{layer}"] + f + 1)
                    nc.vector.tensor_tensor(XL[:, f % 4], MID[:, f], XH[:, f % 4].bitcast(F32), ALU.subtract).then_inc(xl_ready, 1)
                for k in range(KT):
                    if k < KT - 1:
                        dve.wait_ge(down_mm, (KT - 1) * layer + k + 1)
                    else:
                        dve.wait_ge(tile_used, W0[f"down{layer}"] + FT)
                    nc.vector.tensor_tensor(R[:, k], psum(k), R[:, k], ALU.add).then_inc(down_added, 1)

            attention(NSA_UNITS, 0, False)
            attention_out("nsa_o", 0)
            add_residual("nsa_o")
            norm(3, "gu0", "g_ffn0")
            ffn(0)

            norm(4, "swa", "g_mix1")
            step.mark(nc.vector.tensor_scalar(nsk, rows[:, 176:192], -1.0, None, ALU.mult))
            step.mark(nc.vector.memset(VS[:, :, :, DH:DH + 1], 1.0))
            dve.wait_ge(consts_in, 16 * 19)
            t0 = T0["swa"]
            for j in range(10):
                if j < 9:
                    b = product("swa", j)
                    nc.vector.tensor_tensor(TB[:, j % 2], psum(b), rstd[:], ALU.mult).then_inc(freed, 1)
                if j >= 1:
                    dve.wait_ge(qb_ready, j)
                    rotary(TB[:, (j - 1) % 2], cs, sn, KS[:, 0] if j == 1 else QN[:, j - 2],
                           1.0 if j == 1 else float(DH) ** -0.5, None)
            dve.wait_ge(rc_mm, 2)
            step.mark(nc.vector.tensor_copy(rcol, psum(6).rearrange("p (t x) -> p t x", x=P)[:, :, 0]))
            step.wait()
            values("swa", 9, lambda i: VS[:, i, 0:2, 0:DH], rows[:, 48:176].rearrange("p (g d) -> p g d", d=DH))
            attention(SWA_UNITS, len(NSA_UNITS), True)
            attention_out("swa_o", KT)
            add_residual("swa_o", "b_o")
            norm(5, "gu1", "g_ffn1")
            ffn(1)
            norm(6)
            norm_in_place("g_fin", KT)

        @block.tensor
        def _(pe):
            mm = nc.tensor.matmul

            def norm(q):
                for k in range(KT):
                    pe.wait_ge(sq_ready, 8 * q + k + 1)
                    if k == 0 and q == 0:
                        pe.wait_ge(consts_in, 16 * 12)
                    mm(psum(7), ones[:], SQ[:, k % 2], start=(k == 0), stop=(k == KT - 1)).then_inc(sq_sum, 1)

            def wait_bank(t):
                if t >= 2:
                    pe.wait_ge(freed, t - 1)

            def channel_major(stage, j, n, xname=None):
                w, t = W0[stage] + j, T0[stage] + j
                x = X0[xname or stage]
                wait_bank(t)
                pe.wait_ge(tile_split, w + 1)
                s = w % SPL
                for k in range(KT):
                    if j == 0:
                        pe.wait_ge(xh_ready, x + k + 1)
                        pe.wait_ge(xl_ready, x + k + 1)
                    out = psum(t % 2)
                    mm(out, WH[:, s, k], XH[:, k], start=(k == 0), stop=False)
                    mm(out, WH[:, s, k], XL[:, k], start=False, stop=False)
                    ins = mm(out, WL[:, s, k], XH[:, k], start=False, stop=(k == KT - 1))
                ins.then_inc(tile_used, 1)

            def token_major(stage, j, n):
                w, t = W0[stage] + j, T0[stage] + j
                wait_bank(t)
                pe.wait_ge(tile_split, w + 1)
                s = w % SPL
                for i in range(NT):
                    out = PS[:, t % 2, n * i:n * (i + 1)]
                    tt = slice(P * i, P * (i + 1))
                    for k in range(KT):
                        mm(out, XH[:, k, tt], WH[:, s, k, 0:n], start=(k == 0), stop=False)
                        mm(out, XL[:, k, tt], WH[:, s, k, 0:n], start=False, stop=False)
                        ins = mm(out, XH[:, k, tt], WL[:, s, k, 0:n], start=False, stop=(k == KT - 1))
                ins.then_inc(tile_used, 1)

            def linear(stage, n=KT):
                for j in range(n):
                    channel_major(stage, j, n)

            def rms_columns(q):
                pe.wait_ge(rstd_ready, q + 1)
                for i in range(NT):
                    ins = nc.tensor.transpose(PS[:, 6, P * i:P * (i + 1)], rstd[:, P * i:P * (i + 1)], ident[:])
                ins.then_inc(rc_mm, 1)

            norm(0)
            linear("in", 32)
            for j in range(KT):
                if j == 0:
                    pe.wait_ge(pooled_ready, KT)
                if j >= 2:
                    pe.wait_ge(yp_ready, j - 1)
                for c in range(2):
                    ins = mm(psum(2 + j % 2), poolw[:, (j // 2) * 4 + 2 * c + j % 2], pooled[:, 2 * (j // 2) + c],
                             start=(c == 0), stop=(c == 1))
                ins.then_inc(pool_mm, 1)
            pe.wait_ge(yp_ready, KT)
            pe.wait_ge(dve_step, 3)
            for j in range(KT + 1):
                if j < KT:
                    pe.wait_ge(c_ready, j + 1)
                    for n, src in enumerate((C[:, j], C[:, j], U[:, j, UPAD:UPAD + S])):
                        if j >= 1:
                            pe.wait_ge(q_out, 3 * (j - 1) + n + 1)
                        mm(psum(2 + n), BD[n][:, j].rearrange("p a b -> p (a b)"), src, start=True, stop=True).then_inc(q_mm, 1)
                    if j >= 1:
                        pe.wait_ge(vt_out, j)
                    for i in range(NT):
                        ins = mm(PS[:, 5, P * i:P * (i + 1)], U[:, j, UPAD + P * i:UPAD + P * (i + 1)],
                                 BD[2][:, j].rearrange("p a b -> p (a b)"), start=True, stop=True)
                    ins.then_inc(vt_mm, 1)
                if j >= 1:
                    pe.wait_ge(q_out, 3 * j)
                    for n, src in enumerate((Q1[:, j - 1], K1[:, j - 1], VT[:, (j - 1) % 2])):
                        ins = mm(PS[0:16, 7, :], wg[:, 8 * n + j - 1], src, start=(j == 1 and n == 0),
                                 stop=(j == KT and n == 2))
                    ins.then_inc(gate_mm, 1)
            pe.wait_ge(g16, 1)
            mm(psum(6), place_w[0:16], G16[0:16], start=True, stop=True).then_inc(g_placed, 1)
            linear("wo_pool")
            pe.wait_ge(a_ready, 1)
            pe.wait_ge(emt_ready, 1)
            pe.wait_ge(g16, 1)
            for n, src in ((0, gr[3]), (1, gr[5])):
                for i in range(NT):
                    ins = nc.tensor.transpose(PS[:, 7, 64 * (4 * n + i):64 * (4 * n + i) + 64], src[0:64, P * i:P * (i + 1)],
                                              ident[0:64, 0:64])
            ins.then_inc(cols_mm, 1)

            offs = [[0, 512, 896, 1152], [0, 128, 384, 768]]

            def scores(h):
                for d in range(2):
                    if h == 0 and d == 0:
                        pe.wait_ge(nm_ready, 1)
                        pe.wait_ge(acol_ready, 1)
                    if h >= 1:
                        pe.wait_ge(w_exp, 8 * h)
                        pe.wait_ge(wd_ready, 2 * h)
                    q = slice(32 * d, 32 * d + 32)
                    mm(psum(6 + d), ident[q, 32 * d + h:32 * d + h + 1].broadcast_to([32, P]), NM[q], start=True, stop=True
                       ).then_inc(m_bc, 1)
                for j in range(NT):
                    if h >= 1:
                        pe.wait_ge(p_ready, 8 * (h - 1) + 2 * j + 2)
                    for e in range(2):
                        ins = mm(psum(2 + j), K1[:, 2 * h + e, P * j:P * (j + 1)], Q1[:, 2 * h + e], start=(e == 0), stop=(e == 1))
                    ins.then_inc(s_mm1, 1)

            def numerators(h):
                pe.wait_ge(p_ready, 8 * (h + 1))
                pe.wait_ge(freed, T0["wo_m"])
                for i in range(NT):
                    for d in range(2):
                        n = 8 * h + 2 * i + d
                        if n >= 2:
                            pe.wait_ge(num_out, n - 1)
                        js = range(i + 1) if d == 0 else range(i, NT)
                        for j in js:
                            at = offs[d][j] + (P * (i - j) if d == 0 else P * i)
                            ins = mm(PS[:, n % 2, 0:257], PW[d][:, at:at + P], V1[:, j, h], start=(j == js[0]), stop=(j == js[-1]))
                        ins.then_inc(num_mm, 1)

            scores(0)
            for h in range(HEADS):
                if h + 1 < HEADS:
                    scores(h + 1)
                numerators(h)
            pe.wait_ge(xhat, 16)
            for j in range(KT):
                if j >= 2:
                    pe.wait_ge(ym_ready, j - 1)
                for i in range(NT):
                    ins = nc.tensor.transpose(PS[:, 2 + j % 2, P * i:P * (i + 1)], H[:, i, P * j:P * (j + 1)], ident[:])
                ins.then_inc(yt_mm, 1)
            linear("wo_m")
            norm(1)
            norm(2)

            for j in range(16):
                channel_major("nsa", j, 21)
            rms_columns(2)
            for j in range(16, 20):
                token_major("nsa", j, P)
            token_major("nsa", 20, 48)
            pe.wait_ge(xb_ready, 32)
            pe.wait_ge(consts_in, 16 * 17)
            for kv in range(2):
                for ht in range(2):
                    for m in range(16):
                        ins = mm(PS[:, 2 + kv, P * ht:P * (ht + 1)], CW1[kv][:, m, P * ht:P * (ht + 1)],
                                 XB[kv][:, m].rearrange("p g c -> p (g c)"), start=(m == 0), stop=(m == 15))
                ins.then_inc(hid_mm, 1)
            pe.wait_ge(hid_ready, 2)
            for ht in range(2):
                ins = mm(PS[:, 4, 0:P], CW2[:, 0, ht], HID[0][:, ht].rearrange("p g c -> p (g c)"), start=(ht == 0), stop=(ht == 1))
            ins.then_inc(cmp_mm, 1)
            pe.wait_ge(kv_ready, 1)
            for g in range(NG):
                for ht in range(2):
                    ins = mm(PS[:, 5, DH * g:DH * (g + 1)], HIDR[:, NG * ht + g].rearrange("p r c -> p (r c)"),
                             CW2[:, 1, ht, 0:DH], start=(ht == 0), stop=(ht == 1))
            ins.then_inc(cmp_mm, 1)
            pe.wait_ge(rope_in, 14)
            pe.wait_ge(cmp_ready, 5)
            for i in range(NT):
                tt = slice(P * i, P * (i + 1))
                if i >= 1:
                    pe.wait_ge(cs_arg, i)
                for odd in range(2):
                    mm(PS[:, 2 + odd, 0:256].rearrange("p (h c) -> p h c", c=CP), identb[:],
                       cmask[:, i].unsqueeze(1).broadcast_to([P, HQ // 2, CP]), start=True, stop=False)
                for h in range(HQ // 2):
                    for odd in range(2):
                        half = slice(DH * odd, DH * odd + DH)
                        ins = mm(PS[:, 2 + odd, CP * h:CP * (h + 1)], QN[half, h, tt], KCC[half, 2 * (h // 4) + odd],
                                 start=False, stop=(h == HQ // 2 - 1))
                ins.then_inc(cs_mm, 1)
                pe.wait_ge(cs_norm, i + 1)
                if i >= 1:
                    pe.wait_ge(cs_tout, i)
                for g in range(NG):
                    ins = nc.tensor.transpose(PS[:, 6, P * g:P * (g + 1)],
                                              SX[:, 4 * g:4 * g + 4].rearrange("p r c -> p (r c)"), ident[:])
                ins.then_inc(cs_t, 1)
                pe.wait_ge(cs_tout, i + 1)
                for g in range(NG):
                    if i >= 1:
                        pe.wait_ge(cs_out, 4 * (i - 1) + 2 * (g // 2) + 2)
                    mm(PS[:, 4 + g // 2, 256 * (g % 2):256 * (g % 2) + 256], PTC[:, 2 * (g % 2) + g // 2],
                       BDV[:, g].rearrange("p r d -> p (r d)"), start=True, stop=True).then_inc(cs_o, 1)
            pe.wait_ge(cs_out, 16)
            pe.wait_ge(freed, T0["nsa_o"])

            def attention(units, v0, swa):
                def keys(i):
                    return (range(max(i - 1, 0), i + 1) if swa else range(i + 1))

                def score(v):
                    c, m, i = units[v - v0]
                    js = keys(i)
                    n, k0 = P * len(js), P * js[0]
                    K = KS[:, 0] if swa else (KS, KW)[m][:, c // 4]
                    if v >= 2:
                        pe.wait_ge(p_exp, v - 1)
                    for hh in range(2):
                        half = slice(DH * hh, DH * hh + DH)
                        b = 2 + 2 * (v % 2) + hh
                        mm(PS[:, b, 0:n], QN[half, c, P * i:P * (i + 1)], K[half, k0:k0 + n], start=True, stop=False)
                        if swa and i >= 1:
                            mm(PS[:, b, 0:P], identb[:], masks[:, 2], start=False, stop=False)
                        ins = mm(PS[:, b, n - P:n], identb[:], masks[:, 1], start=False, stop=True)
                    ins.then_inc(s_mm, 1)

                def turn(v):
                    c, m, i = units[v - v0]
                    pe.wait_ge(p_exp, v + 1)
                    if v >= 1:
                        pe.wait_ge(pt_d, v)
                        pe.wait_ge(pt_a, v)
                    for hh in range(2):
                        for n in range(len(keys(i))):
                            ins = nc.tensor.transpose(PS[:, 6 + hh, P * n:P * (n + 1)], PE_[:, v % 2, hh, P * n:P * (n + 1)],
                                                      ident[:])
                    ins.then_inc(pt_mm, 1)

                def output(v):
                    c, m, i = units[v - v0]
                    V = VS if swa else (VS, VW)[m]
                    pe.wait_ge(pt_d, v + 1)
                    pe.wait_ge(pt_a, v + 1)
                    if v >= 2:
                        pe.wait_ge(o_done, v - 1)
                    for hh in range(2):
                        js = keys(i)
                        for n, j in enumerate(js):
                            ins = mm(PS[:, v % 2, 65 * hh:65 * hh + 65], PT_[:, v % 2, hh, P * n:P * (n + 1)],
                                     V[:, j, hh + (0 if swa else 2 * (c // 4))], start=(n == 0), stop=(n == len(js) - 1))
                    ins.then_inc(o_mm, 1)

                last = v0 + len(units)
                score(v0)
                score(v0 + 1)
                turn(v0)
                for v in range(v0, last):
                    if v + 2 < last:
                        score(v + 2)
                    if v + 1 < last:
                        turn(v + 1)
                    output(v)

            def attention_out(stage, n0, units):
                pe.wait_ge(o_done, units)
                for c in range(KT):
                    if c >= 2:
                        pe.wait_ge(xl_ready, X0[stage] + c - 1)
                    for i in range(NT):
                        ins = nc.tensor.transpose(PS[:, 2 + c % 2, P * i:P * (i + 1)], OA[:, i, c].rearrange("p a d -> p (a d)"),
                                                  ident[:])
                    ins.then_inc(oa_mm, 1)

            def ffn(layer):
                st, sd = f"gu{layer}", f"down{layer}"
                w0, t0, x0 = W0[st], T0[st], X0[st]
                wd, xd = W0[sd], X0[sd]
                pe.wait_ge(xh_ready, x0 + KT)
                pe.wait_ge(xl_ready, x0 + KT)
                with pe.Fori(0, FT // 2) as it:
                    for b in range(4):
                        pe.wait_ge(freed, t0 + 4 * it + (b - 1))
                        pe.wait_ge(tile_split, w0 + 4 * it + (b + 1))
                        s, out = (w0 + b) % SPL, psum((t0 + b) % 2)
                        for k in range(KT):
                            mm(out, WH[:, s, k], XH[:, k], start=(k == 0), stop=False)
                            mm(out, WH[:, s, k], XL[:, k], start=False, stop=False)
                            ins = mm(out, WL[:, s, k], XH[:, k], start=False, stop=(k == KT - 1))
                        ins.then_inc(tile_used, 1)
                pe.wait_ge(freed, t0 + 2 * FT)
                for f in range(FT):
                    s, x = (wd + f) % SPL, f % 4
                    pe.wait_ge(tile_split, wd + f + 1)
                    pe.wait_ge(xh_ready, xd + f + 1)
                    pe.wait_ge(xl_ready, xd + f + 1)
                    for k in range(KT):
                        mm(psum(k), WH[:, s, k], XH[:, x], start=(f == 0), stop=False)
                        mm(psum(k), WH[:, s, k], XL[:, x], start=False, stop=False)
                        ins = mm(psum(k), WL[:, s, k], XH[:, x], start=False, stop=(f == FT - 1))
                        if f == FT - 1 and k < KT - 1:
                            ins.then_inc(down_mm, 1)
                    ins.then_inc(tile_used, 1)

            attention(NSA_UNITS, 0, False)
            attention_out("nsa_o", 0, len(NSA_UNITS))
            linear("nsa_o")
            norm(3)
            ffn(0)
            pe.wait_ge(down_added, KT)
            norm(4)
            for j in range(9):
                channel_major("swa", j, 10)
            rms_columns(4)
            token_major("swa", 9, P)
            pe.wait_ge(freed, T0["swa"] + 10)
            pe.wait_ge(rope_in, 14 + 9)
            attention(SWA_UNITS, len(NSA_UNITS), True)
            attention_out("swa_o", KT, len(NSA_UNITS) + len(SWA_UNITS))
            linear("swa_o")
            norm(5)
            ffn(1)
            pe.wait_ge(down_added, 2 * KT)
            norm(6)



def _tiles(w):
    k, m = w.shape
    return np.ascontiguousarray(w.reshape(KT, P, m // P, P).transpose(2, 1, 0, 3))


def _vec(v):
    return v.reshape(-1, P).T


_QUADS = [np.arange(16 * q, 16 * q + 16) for q in range(2)]
PERM = np.concatenate([np.concatenate([x, x + 32]) for x in _QUADS])


def _constants():
    r, c = np.arange(P)[:, None], np.arange(P)[None, :]
    low = np.float32(-1e30)
    masks = np.stack([np.where(m, np.float32(0), low) for m in (c >= r, c <= r, c > r)], 1)
    pos = np.arange(S)
    end = np.arange(CP) * 16 + CLEN - 1
    cm = np.where((end[None, :] <= pos[:, None]) & (np.arange(CP)[None, :] < CMP), np.float32(0), low)
    cmask = np.ascontiguousarray(cm.reshape(NT, P, CP).transpose(1, 0, 2))
    counts = []
    for w in WINDOWS:
        left = (w - 1) // 2
        counts.append(np.minimum(pos + w - 1 - left, S - 1) - np.maximum(pos - left, 0) + 1)
    invc = (1.0 / np.stack(counts)).astype(np.float32)
    inv = np.float32(10000.0) ** (-np.arange(0, DH, 2, dtype=np.float32) / np.float32(DH))
    ang = np.arange(S, dtype=np.float32)[:, None] * inv[None, :]
    cos, sin = np.cos(ang).astype(np.float32).T, np.sin(ang).astype(np.float32).T
    freq = np.tile(PERM % 32, 2)
    sign = np.tile(np.where(PERM < 32, -1.0, 1.0), 2).astype(np.float32)[:, None]
    place = np.zeros((16, P), np.float32)
    for d in range(2):
        for g in range(8):
            place[8 * d + g, 32 * d + g if g < 4 else 64 + 32 * d + g - 4] = 1.0
    return {
        "ident": np.eye(P, dtype=np.float32), "ones": np.ones((P, P), np.float32),
        "masks": masks, "cmask": cmask,
        "invc": np.ascontiguousarray(np.broadcast_to(invc, (P, 4, S))),
        "bdm": (r // 4 == np.arange(32)[None, :]).astype(np.float32),
        "cos": np.ascontiguousarray(cos[freq]), "sin": np.ascontiguousarray(sin[freq] * sign), "place": place,
    }


def _layout(i):
    f = {k: np.asarray(v) for k, v in i.items()}
    w_in = f["w_in"][0]
    part = lambda n: w_in[:, n * D:(n + 1) * D]
    head_nsa = [(2 * (c // 4) + hh) * 4 + c % 4 for c in range(8) for hh in range(2)]
    head_swa = [hh * 8 + c for c in range(8) for hh in range(2)]
    rot = lambda heads: np.concatenate([h * DH + PERM for h in heads])
    flat = lambda heads: np.concatenate([h * DH + np.arange(DH) for h in heads])
    nw = f["nsa_w_in_2"][0]
    kv = lambda n: nw[:, HQ * DH + 256 * n:HQ * DH + 256 * (n + 1)]
    gates = np.zeros((D, P), np.float32)
    gates[:, 0:48] = nw[:, HQ * DH + 6 * 256:]
    k4, k2 = rot(range(4)), rot(range(2))
    nsa = np.concatenate([kv(0)[:, k4], kv(1), kv(2)[:, k4], kv(4)[:, k4], nw[:, :HQ * DH][:, rot(head_nsa)],
                          kv(3), kv(5), gates], 1)
    sw, sbias = f["swa_w_qkv_2"][0], f["swa_b_qkv_2"][0]
    swa = np.concatenate([sw[:, HQ * DH:HQ * DH + P][:, k2], sw[:, :HQ * DH][:, rot(head_swa)], sw[:, HQ * DH + P:]], 1)
    gu = []
    for n in range(2):
        g = f["ffn_w_gu_2"][n].reshape(D, 2, FT, P).transpose(0, 2, 1, 3)
        gu.append(_tiles(g.reshape(D, 2 * FF)))
    down = [f["ffn_w_down_2"][n].reshape(FT, P, KT, P) for n in range(2)]
    w = np.concatenate([
        _tiles(np.concatenate([part(2), part(0), part(1), part(3)], 1)),
        _tiles(f["w_out"][0][:D]), _tiles(f["w_out"][0][D:]), _tiles(nsa),
        _tiles(f["nsa_w_o_2"][0][flat(head_nsa)]), gu[0], down[0],
        _tiles(swa), _tiles(f["swa_w_o_2"][0][flat(head_swa)]), gu[1], down[1]])
    c = np.zeros((P, NCOL), np.float32)

    def put(name, v):
        c[:, COLS[name]:COLS[name] + v.shape[1]] = v

    for name, v in (("g_in", f["norm_in_g"][0]), ("g_out", f["norm_out_g"]), ("pool_scale", f["pool_scale"][0]),
                    ("conv_w", f["conv_w"][0]), ("conv_b", f["conv_b"][0]), ("mh", f["mh_norm_w"][0]),
                    ("skip", f["skip_w"][0]), ("g_mix0", f["norm_mix_2"][0]), ("g_mix1", f["norm_mix_2"][1]),
                    ("g_ffn0", f["norm_ffn_2"][0]), ("g_ffn1", f["norm_ffn_2"][1]), ("g_fin", f["norm_final_2"]),
                    ("b_q", sbias[:HQ * DH][rot(head_swa)]), ("b_k", sbias[HQ * DH:HQ * DH + P][k2]),
                    ("b_o", f["swa_b_o_2"][0]), ("fcw0", f["ffn_conv_w_2"][0]), ("fcw1", f["ffn_conv_w_2"][1]),
                    ("fcb0", f["ffn_conv_b_2"][0]), ("fcb1", f["ffn_conv_b_2"][1])):
        put(name, _vec(v))
    c[0:16, COLS["b_gates"]] = f["b_gates"][0].reshape(16)
    pe = f["nsa_cmp_pe_2"][0]
    put("pe_k", np.tile(pe[0].T[PERM], (2, 1)))
    put("pe_v", np.tile(pe[1].T, (2, 1)))
    row = np.concatenate([f["nsa_gate_b_2"][0], sbias[HQ * DH + P:], f["swa_sinks_2"][0]])
    w1, w2 = f["nsa_cmp_w1_2"][0], f["nsa_cmp_w2_2"][0]
    w1 = [w1[0].reshape(CLEN, DH, 256)[:, PERM].reshape(16, P, 256), w1[1].reshape(16, P, 256)]
    w2 = [np.concatenate([x, x], 1).reshape(2, P, P) for x in (w2[0][:, PERM], w2[1])]
    maps = np.stack([f[n][0].reshape(KT, P, 4) for n in ("w_q", "w_k", "w_v")])
    return {
        "x": f["x"][0].T.reshape(KT, P, S).transpose(1, 0, 2), "w": w, "cols": c,
        "rows": np.broadcast_to(row, (P, NROW)), "wqkv": maps.transpose(2, 0, 1, 3),
        "wg": f["w_gates"][0].transpose(1, 0, 2).reshape(24, P, 16).transpose(1, 0, 2),
        "pool_w": f["pool_w"][0].reshape(4, 2, P, 2, P).transpose(2, 0, 1, 3, 4).reshape(P, 16, P),
        "cmp_w1k": w1[0].transpose(1, 0, 2), "cmp_w1v": w1[1].transpose(1, 0, 2),
        "cmp_w2": np.stack(w2).transpose(2, 0, 1, 3),
    }


def kernel(**inputs):
    import concourse.bacc as bacc
    from concourse.bass_utils import run_bass_kernel_spmd

    nc = bacc.Bacc("TRN2", target_bir_lowering=False, num_devices=1)
    arrays = {**_constants(), **_layout(inputs)}
    arrays = {f"in_{n}": np.ascontiguousarray(v) for n, v in arrays.items()}
    aps = {n[3:]: nc.dram_tensor(n, v.shape, mybir.dt.from_np(v.dtype), kind="ExternalInput").ap() for n, v in arrays.items()}
    aps["out"] = nc.dram_tensor("out", (P, KT, S), F32, kind="ExternalOutput").ap()
    build(nc, aps)
    r = run_bass_kernel_spmd(nc, [arrays], core_ids=[0])
    got = r.results[0]["out"]
    return np.ascontiguousarray(got.transpose(2, 1, 0).reshape(1, S, D))
```

```python
from contextlib import ExitStack

import numpy as np

import concourse.bass as bass
from concourse import mybir

F32 = mybir.dt.float32
F32R = mybir.dt.float32r
BF16 = mybir.dt.bfloat16
ALU = mybir.AluOpType
ACT = mybir.ActivationFunctionType
AX = mybir.AxisListType

P = 128
S = 512
NT = S // P
D = 1024
KT = D // P
EPS = 1e-6

HEADS = 4
HD = 256
WINDOWS = (2, 4, 8, 16)
TAPS = 5
UPAD = 2
US = S + 2 * UPAD

HQ = 16
DH = 64
NG = 4
CMP = 31
CP = 32
CLEN = 32
FF = 2816
FT = FF // P
FTAPS = 3

RAW = 4
SPL = 2

STAGES = [("in", 32), ("wo_pool", 8), ("wo_m", 8), ("nsa", 21), ("nsa_o", 8), ("gu0", 2 * FT),
          ("down0", FT), ("swa", 10), ("swa_o", 8), ("gu1", 2 * FT), ("down1", FT)]
W0, T0, _w, _t = {}, {}, 0, 0
for _name, _n in STAGES:
    W0[_name], T0[_name] = _w, _t
    _w += _n
    _t += 0 if _name.startswith("down") else _n
NW = _w

XST = [("in", 8), ("wo_pool", 8), ("wo_m", 8), ("nsa", 8), ("nsa_o", 8), ("gu0", 8), ("down0", FT),
       ("swa", 8), ("swa_o", 8), ("gu1", 8), ("down1", FT)]
X0, _x = {}, 0
for _name, _n in XST:
    X0[_name] = _x
    _x += _n

COLS, _c = {}, 0
for _name, _n in [("g_in", 8), ("g_out", 8), ("pool_scale", 8), ("conv_w", 40), ("conv_b", 8), ("mh", 8),
                  ("skip", 8), ("b_gates", 1), ("g_mix0", 8), ("g_mix1", 8), ("g_ffn0", 8), ("g_ffn1", 8),
                  ("g_fin", 8), ("b_q", 8), ("b_k", 1), ("b_v", 1), ("b_o", 8), ("fcw0", 3 * FT), ("fcw1", 3 * FT),
                  ("fcb0", FT), ("fcb1", FT), ("pe_k", 32), ("pe_v", 32)]:
    COLS[_name] = _c
    _c += _n
NCOL = _c

NROW = 64

POOL_TILES = [(2, 3), (4, 5), (6,), (7,)]

NSA_UNITS = [(c, m, i) for c in range(8) for m in range(2) for i in range(NT)]
SWA_UNITS = [(c, 0, i) for c in range(8) for i in range(NT)]


class Steps:

    def __init__(self, eng, sem):
        self.eng, self.sem, self.n, self.off = eng, sem, 0, 0

    def mark(self, ins):
        ins.then_inc(self.sem, 1)
        self.n += 1
        return self.n

    def wait(self, n=None):
        self.eng.wait_ge(self.sem, self.off + (self.n if n is None else n))


def build(nc, a):
    with ExitStack() as ctx:
        def sb(name, shape, dt=F32):
            return ctx.enter_context(nc.sbuf_tensor("sb_" + name, shape, dt))

        def sem(name):
            return ctx.enter_context(nc.semaphore(name))

        R = sb("resid", [P, KT, S])
        XH = sb("x_hi", [P, KT, S], F32R)
        XL = sb("x_lo", [P, KT, S], F32R)
        raw = sb("raw", [P, RAW, KT, P])
        WH = sb("w_hi", [P, SPL, KT, P], F32R)
        WL = sb("w_lo", [P, SPL, KT, P], F32R)
        cols = sb("cols", [P, NCOL])
        rows = sb("rows", [P, NROW])
        ident = sb("ident", [P, P])
        ones = sb("ones", [P, P])
        identb = sb("identb", [P, P], BF16)
        masks = sb("masks", [P, 3, P], BF16)
        cmask = sb("cmask", [P, NT, P], BF16)
        rstd = sb("rstd", [P, S])
        small = sb("small", [P, 160])
        PS = ctx.enter_context(nc.psum_tensor("ps", [P, 8, S], F32))
        NA = 30712
        arena = sb("arena", [P, NA])

        def col(name, k=0):
            return cols[:, COLS[name] + k:COLS[name] + k + 1]

        def carve(at, *shape):
            n = int(np.prod(shape))
            v = arena[:, at:at + n]
            if len(shape) == 2:
                v = v.rearrange("p (a b) -> p a b", b=shape[1])
            if len(shape) == 3:
                v = v.rearrange("p (a b c) -> p a b c", b=shape[1], c=shape[2])
            if len(shape) == 4:
                v = v.rearrange("p (a b c d) -> p a b c d", b=shape[1], c=shape[2], d=shape[3])
            return v

        o_u, o_mz, o_c, o_q, o_k, o_v = 0, 4128, 8224, 12320, 16416, 20512
        o_b = o_v + NT * HEADS * 257
        o_nm = o_b + 4608
        U = carve(o_u, KT, US)
        H = carve(o_u, NT, 1024)
        MZ = carve(o_mz, KT, S)
        px = [carve(o_mz + 544 * i, 544) for i in range(3)]
        C = carve(o_c, KT, S)
        Q1, K1 = carve(o_q, KT, S), carve(o_k, KT, S)
        pooled, SZ = Q1, K1
        V1 = carve(o_v, NT, HEADS, 257)
        poolw = carve(o_v, 16, P)
        invc = carve(o_v + 2048, 4, S)
        BD = [carve(o_b + 1024 * i, KT, 32, 4) for i in range(3)]
        wg = carve(o_b + 3072, 24, 16)
        VT = carve(o_b + 3456, 2, S)
        PW = [carve(o_b, 1280), carve(o_b + 1280, 1280)]
        WD = carve(o_b + 2560, 2, NT, P)
        WE = carve(o_b + 3584, 2, S)
        NM = carve(o_nm, S)
        ACOL = carve(o_nm + S, 8, DH)
        wqkv = carve(o_c, 3, KT, 4)
        bdm = carve(o_c + 96, 32)
        place_w = carve(o_nm, P)
        masks32, cmask32 = carve(o_q, 3, P), carve(o_q + 384, NT, P)
        G16 = carve(o_u, S)
        gr = [carve(o_u + S * (i + 1), S) for i in range(6)]
        one5 = carve(o_u + S * 7, S)
        SQ, RMS = carve(0, 2, S), carve(1024, S)

        o = 1536
        cs, sn = carve(o, S), carve(o + 512, S)
        csr, snr = carve(o + 1024, S), carve(o + 1536, S)
        QN = carve(o + 2048, KT, S)
        KC, VC = carve(o + 6144, 2, S), carve(o + 7168, 2, S)
        KS, KW = carve(o + 8192, 2, S), carve(o + 9216, 2, S)
        VS, VW = carve(o + 10240, NT, NG, 65), carve(o + 11280, NT, NG, 65)
        VN = 96
        v_rows = [arena[:, o + 10240 + 1040 * m:o + 10240 + 1040 * (m + 1) + VN - 65] for m in range(2)]
        v_pad = arena[:, o + 12320:o + 12352]
        o1 = o + 12352
        CW1 = [carve(o1 + 4096 * i, 16, 2 * P) for i in range(2)]
        OA = carve(o1, NT, 8, 2, DH)
        XB = [carve(o1 + 8192 + 2048 * i, 16, NG, CP) for i in range(2)]
        PE_ = carve(o1 + 8192, 2, 2, S)
        PT_ = carve(o1 + 10240, 2, 2, S)
        o2 = o1 + 12288
        CW2 = carve(o2, 2, 2, P)
        HID = [carve(o2 + 512 + 256 * i, 2, NG, CP) for i in range(2)]
        HIDR = carve(o2 + 1024, NG, 2, 2 * CP)
        BDK = carve(o2 + 1536, 2, P)
        BDV = carve(o2 + 1792, 2, 4, DH)
        TS, TM = carve(o2 + 3200, S), carve(o2 + 3712, S)
        GT = carve(o2 + 4224, NT, 48)
        SX = [carve(o1 + 8192 + 512 * i, HQ, CP) for i in range(2)]
        PTC = [carve(o1 + 10240 + 512 * i, 4, P) for i in range(2)]
        assert o2 + 4416 <= NA
        MID = carve(o, FT, S)
        AP_ = carve(o + 11264, 2, S + 2)
        CV = carve(o + 12292, 2, S)
        SA = carve(o + 13316, 2, S)
        TU = carve(o + 14340, 2, S)

        TB = KW
        nmx = small[:, 4:12].rearrange("p (a b) -> p a b", b=2)
        nmr = small[:, 12:20].rearrange("p (a b) -> p a b", b=2)
        esk = small[:, 20:28].rearrange("p (a b) -> p a b", b=2)
        ske = small[:, 28:36].rearrange("p (a b) -> p a b", b=2)
        rec = small[:, 36:44].rearrange("p (a b) -> p a b", b=2)
        nsk = small[:, 44:60]
        cst = small[:, 60:108].rearrange("p (a b) -> p a b", b=16)
        bn6 = small[:, 108:114]
        zero = sb("zero", [P, KT])[:, :]
        mv = sb("mv", [P, 16, 2])
        rv = sb("rv", [P, 16])
        dn = sb("dn", [P, 4])

        consts_in = sem("consts_in")
        x_in = [sem(f"x_in{k}") for k in range(KT)]
        cols_in = sem("cols_in")
        raw_in = [sem(f"raw_in{i}") for i in range(RAW)]
        zero_set = sem("zero_set")
        hi_made = sem("hi_made")
        tile_split = sem("tile_split")
        tile_used = sem("tile_used")
        freed = sem("freed")
        xh_ready, xl_ready = sem("xh_ready"), sem("xl_ready")
        sq_ready, sq_sum, rms_ready, std_ready = sem("sq_ready"), sem("sq_sum"), sem("rms_ready"), sem("std_ready")
        rstd_ready = sem("rstd_ready")
        dve_step = sem("dve_step")
        act_step = sem("act_step")
        normed = sem("normed")
        down_added = sem("down_added")
        bd_ready = sem("bd_ready")
        pool_in = sem("pool_in")
        conv_ready, c_ready, mz_raw, mz_ready = sem("conv_ready"), sem("c_ready"), sem("mz_raw"), sem("mz_ready")
        pooled_ready, sz_ready, pool_mm, yp_ready = sem("pooled_ready"), sem("sz_ready"), sem("pool_mm"), sem("yp_ready")
        q_mm, q_out, vt_mm, vt_out, gate_mm, g16 = (sem(x) for x in ("q_mm", "q_out", "vt_mm", "vt_out", "gate_mm", "g16"))
        g_placed, f_rest, nm_ready, fm_ready, emt_ready, cols_mm, acol_ready = (
            sem(x) for x in ("g_placed", "f_rest", "nm_ready", "fm_ready", "emt_ready", "cols_mm", "acol_ready"))
        a_ready = sem("a_ready")
        m_bc, s_mm1, wd_ready, w_exp, p_ready, num_mm, num_out = (
            sem(x) for x in ("m_bc", "s_mm1", "wd_ready", "w_exp", "p_ready", "num_mm", "num_out"))
        var_ready, hstd, xhat, yt_mm, skip_ready, ym_ready = (
            sem(x) for x in ("var_ready", "hstd", "xhat", "yt_mm", "skip_ready", "ym_ready"))
        rope_in, kv_ready = sem("rope_in"), sem("kv_ready")
        tok_t, tok_out = sem("tok_t"), sem("tok_out")
        gt_raw, gt_ready = sem("gt_raw"), sem("gt_ready")
        xb_ready, hid_mm, hid_ready, cmp_mm, cmp_ready = (
            sem(x) for x in ("xb_ready", "hid_mm", "hid_ready", "cmp_mm", "cmp_ready"))
        cs_mm, cs_arg, cs_exp, cs_norm, cs_t, cs_tout, cs_o, cs_out = (
            sem(x) for x in ("cs_mm", "cs_arg", "cs_exp", "cs_norm", "cs_t", "cs_tout", "cs_o", "cs_out"))
        s_mm, nmax, p_exp, pt_mm, pt_d, pt_a, o_mm, o_done = (
            sem(x) for x in ("s_mm", "nmax", "p_exp", "pt_mm", "pt_d", "pt_a", "o_mm", "o_done"))
        oa_mm = sem("oa_mm")
        qb_raw, qb_ready = sem("qb_raw"), sem("qb_ready")
        ff_conv, ff_silu, mid_ready, down_mm = sem("ff_conv"), sem("ff_silu"), sem("mid_ready"), sem("down_mm")
        out_ready, out_done = sem("out_ready"), sem("out_done")

        block = ctx.enter_context(nc.Block())

        def psum(bank, n=S):
            return PS[:, bank, 0:n]

        def xst(name):
            return X0[name]

        @block.sync
        def _(sp):
            for k in range(KT):
                sp.dma_start(R[:, k, :], a["x"][:, k, :]).then_inc(x_in[k], 16)

            def load(it, s, first=False):
                if not first:
                    sp.wait_ge(tile_split, 4 * it + (s - RAW + 1))
                sp.dma_start(raw[:, s], a["w"][bass.ds(4 * it + s, 1)].rearrange("o p k m -> (o p) k m")
                             ).then_inc(raw_in[s], 16)

            for s in range(RAW):
                load(0, s, first=True)
            with sp.Fori(1, NW // RAW) as it:
                for s in range(RAW):
                    load(it, s)
            for s in range(NW % RAW):
                load(NW // RAW, s)
            for k in range(KT):
                sp.wait_ge(normed, KT + k + 1)
                sp.dma_start(a["out"][:, k, :], R[:, k, :]).then_inc(out_done, 16)
            sp.wait_ge(out_done, 16 * KT)

        @block.gpsimd
        def _(pool):
            def split(it, s, first=False):
                pool.wait_ge(raw_in[s], 16 * (it + 1))
                if not first:
                    pool.wait_ge(tile_used, 4 * it + (s - SPL + 1))
                nc.gpsimd.tensor_tensor(WH[:, s % SPL], raw[:, s], zero.unsqueeze(2).broadcast_to([P, KT, P]), ALU.add
                                        ).then_inc(hi_made, 1)
                pool.wait_ge(hi_made, 4 * it + (s + 1))
                nc.gpsimd.tensor_tensor(WL[:, s % SPL], raw[:, s], WH[:, s % SPL].bitcast(F32),
                                        ALU.subtract).then_inc(tile_split, 1)

            nc.gpsimd.memset(zero, 0.0).then_inc(zero_set, 1)
            nc.gpsimd.memset(ones[:], 1.0).then_inc(zero_set, 1)
            pool.wait_ge(zero_set, 2)
            for s in range(RAW):
                split(0, s, first=s < SPL)
            with pool.Fori(1, NW // RAW) as it:
                for s in range(RAW):
                    split(it, s)
            for s in range(NW % RAW):
                split(NW // RAW, s)

        @block.scalar
        def _(act):
            step = Steps(act, act_step)
            act.dma_start(cols[:], a["cols"]).then_inc(cols_in, 16)

            def constants():
                for dst, name in ((wqkv, "wqkv"), (bdm, "bdm"), (poolw, "pool_w"),
                                  (invc, "invc"), (wg, "wg"), (ident[:], "ident"), (rows[:], "rows"),
                                  (masks32, "masks"), (cmask32, "cmask"),
                                  (place_w[0:16], "place")):
                    act.dma_start(dst, a[name]).then_inc(consts_in, 16)

            def norm(q, ready, gain=None, x=None, used=0, late=False):
                if gain:
                    if used:
                        act.wait_ge(tile_used, used)
                    for k in range(KT):
                        act.wait_ge(*ready(k))
                        nc.scalar.mul(XH[:, k], R[:, k], col(gain, k)).then_inc(xh_ready, 1)
                if late:
                    constants()
                for k in range(KT):
                    if not gain:
                        act.wait_ge(*ready(k))
                    if 8 * q + k >= 2:
                        act.wait_ge(sq_sum, 8 * q + k - 1)
                    nc.scalar.activation(SQ[:, k % 2], R[:, k], ACT.Square).then_inc(sq_ready, 1)
                act.wait_ge(rms_ready, q + 1)
                nc.scalar.activation(RMS, RMS, ACT.Sqrt).then_inc(std_ready, 1)

            act.wait_ge(cols_in, 16)
            norm(0, lambda k: (x_in[k], 16), "g_in", late=True)
            for j in range(KT):
                act.wait_ge(conv_ready, j + 1)
                nc.scalar.activation(C[:, j], C[:, j], ACT.Silu).then_inc(c_ready, 1)
            for j in range(KT):
                act.wait_ge(freed, 16 + j + 1)
                nc.scalar.activation(SZ[:, j], SZ[:, j], ACT.Silu).then_inc(sz_ready, 1)
            for j in range(KT):
                act.wait_ge(freed, 24 + j + 1)
                nc.scalar.activation(MZ[:, j], MZ[:, j], ACT.Silu).then_inc(mz_ready, 1)
            act.wait_ge(tile_used, W0["wo_pool"])
            for k in range(KT):
                act.wait_ge(yp_ready, k + 1)
                nc.scalar.copy(XH[:, k], SZ[:, k]).then_inc(xh_ready, 1)
            act.wait_ge(xl_ready, X0["wo_pool"] + KT)
            for j in range(KT):
                act.wait_ge(q_mm, 3 * j + 1)
                nc.scalar.copy(Q1[:, j], psum(2)).then_inc(q_out, 1)
                act.wait_ge(q_mm, 3 * j + 2)
                nc.scalar.copy(K1[:, j], psum(3)).then_inc(q_out, 1)
                act.wait_ge(q_mm, 3 * j + 3)
                if j >= 2:
                    act.wait_ge(gate_mm, j - 1)
                nc.scalar.copy(VT[:, j % 2], psum(4)).then_inc(q_out, 1)
            act.wait_ge(gate_mm, KT)
            nc.scalar.activation(G16[0:16], PS[0:16, 7, :], ACT.Identity, bias=cols[0:16, COLS["b_gates"]:COLS["b_gates"] + 1]
                                 ).then_inc(g16, 1)
            act.wait_ge(g_placed, 1)
            t = gr[1]
            step.mark(nc.scalar.activation(t[64:128], PS[64:128, 6, :], ACT.Abs))
            step.wait()
            step.mark(nc.scalar.activation(t[64:128], t[64:128], ACT.Exp, scale=-1.0))
            step.wait()
            nc.scalar.activation(t[64:128], t[64:128], ACT.Ln, bias=1.0).then_inc(f_rest, 1)
            act.wait_ge(fm_ready, 1)
            nc.scalar.activation(gr[5][0:64], gr[4][0:64], ACT.Exp, scale=-1.0).then_inc(emt_ready, 1)
            act.wait_ge(acol_ready, 1)
            for h in range(HEADS):
                act.wait_ge(wd_ready, 2 * (h + 1))
                for j in range(NT):
                    for d in range(2):
                        n = 8 * h + 2 * j + d
                        if n >= 2:
                            act.wait_ge(p_ready, n - 1)
                        bias = ACOL[:, j, 32 * d + h:32 * d + h + 1]
                        w = WE[:, n % 2]
                        dg, rest = (0, P) if d == 0 else (P * j, 0)
                        others = (P * (j + 1), S) if d == 0 else (0, P * j)
                        if others[1] > others[0]:
                            nc.scalar.activation(w[:, rest:rest + others[1] - others[0]],
                                                 PS[:, 6 + d, others[0]:others[1]], ACT.Exp, bias=bias)
                        nc.scalar.activation(w[:, dg:dg + P], WD[:, d, j], ACT.Exp, bias=bias).then_inc(w_exp, 1)
            for j in range(KT):
                nc.scalar.mul(C[:, j], C[:, j], col("skip", j)).then_inc(skip_ready, 1)
            act.wait_ge(var_ready, 1)
            nc.scalar.activation(rv[:], rv[:], ACT.Sqrt).then_inc(hstd, 1)
            act.wait_ge(tile_used, W0["wo_m"])
            for k in range(KT):
                act.wait_ge(ym_ready, k + 1)
                nc.scalar.copy(XH[:, k], MZ[:, k]).then_inc(xh_ready, 1)
            act.wait_ge(xl_ready, X0["wo_m"] + KT)
            for dst, name in ((cs, "cos"), (sn, "sin"), (CW1[0], "cmp_w1k"), (CW1[1], "cmp_w1v"), (CW2, "cmp_w2")):
                act.dma_start(dst, a[name]).then_inc(consts_in, 16)
            norm(1, lambda k: (freed, T0["wo_m"] + k + 1))
            norm(2, lambda k: (normed, k + 1), "g_mix0", used=W0["nsa"])
            for kv in range(2):
                act.wait_ge(hid_mm, kv + 1)
                nc.scalar.activation(HID[kv], PS[:, 2 + kv, 0:2 * P].rearrange("p (a b c) -> p a b c", a=2, b=NG),
                                     ACT.Gelu_apprx_tanh).then_inc(hid_ready, 1)
            act.wait_ge(gt_raw, 1)
            nc.scalar.activation(GT, GT, ACT.Sigmoid).then_inc(gt_ready, 1)

            def c_exp(i):
                act.wait_ge(cs_arg, i + 1)
                nc.scalar.activation(SX[i % 2], SX[i % 2], ACT.Exp).then_inc(cs_exp, 1)

            def c_tout(i):
                act.wait_ge(cs_t, i + 1)
                if i >= 2:
                    act.wait_ge(cs_o, 2 * (i - 1))
                nc.scalar.copy(PTC[i % 2], psum(6).rearrange("p (g t) -> p g t", g=NG)).then_inc(cs_tout, 1)

            def c_out(i):
                for gp in range(2):
                    act.wait_ge(cs_o, 2 * i + gp + 1)
                    nc.scalar.copy(OA[:, i, 4 * gp:4 * gp + 4].rearrange("p c a d -> p (c a d)"), psum(4 + gp)
                                   ).then_inc(cs_out, 1)

            def values_out(n):
                act.wait_ge(tok_t, n + 2)
                g = 2 * (n % 2)
                nc.scalar.copy((VS, VW)[n // 2][:, :, g:g + 2, 0:DH], psum(7).rearrange("p (t g d) -> p t g d", t=NT, d=DH)
                               ).then_inc(tok_out, 1)

            c_exp(0)
            values_out(0)
            c_exp(1)
            c_tout(0)
            values_out(1)
            c_out(0)
            c_tout(1)
            c_exp(2)
            values_out(2)
            c_out(1)
            c_tout(2)
            c_exp(3)
            values_out(3)
            c_out(2)
            c_tout(3)
            c_out(3)

            def n_keys(i, swa):
                return P * min(i + 1, 2) if swa else P * (i + 1)

            def attention(units, v0, swa):
                def exps(v):
                    n = n_keys(units[v - v0][2], swa)
                    act.wait_ge(nmax, v + 1)
                    if v >= 2:
                        act.wait_ge(pt_mm, v - 1)
                    if swa:
                        act.wait_ge(qb_raw, v - v0 + 1)
                        nc.scalar.activation(esk[:, v % 4], ske[:, v % 4], ACT.Exp)
                    nc.scalar.activation(PE_[:, v % 2, 0, 0:n], PS[:, 2 + 2 * (v % 2), 0:n], ACT.Exp,
                                         bias=nmr[:, v % 4, 0:1])
                    nc.scalar.activation(PE_[:, v % 2, 1, 0:n], PS[:, 3 + 2 * (v % 2), 0:n], ACT.Exp,
                                         bias=nmr[:, v % 4, 1:2]).then_inc(p_exp, 1)

                def evac(v):
                    n = n_keys(units[v - v0][2], swa)
                    act.wait_ge(pt_mm, v + 1)
                    if v >= 2:
                        act.wait_ge(o_mm, v - 1)
                    nc.scalar.copy(PT_[:, v % 2, 1, 0:n], psum(7, n)).then_inc(pt_a, 1)

                last = v0 + len(units)
                exps(v0)
                for v in range(v0, last):
                    if v + 1 < last:
                        exps(v + 1)
                    evac(v)

            def attention_out(stage, n0):
                act.wait_ge(tile_used, W0[stage])
                for c in range(KT):
                    act.wait_ge(oa_mm, n0 + c + 1)
                    nc.scalar.copy(XH[:, c], psum(2 + c % 2)).then_inc(xh_ready, 1)

            def ffn(layer):
                with act.Fori(0, FT // 2) as it:
                    for b in range(2):
                        act.wait_ge(ff_conv, layer * FT + 2 * it + (b + 1))
                        nc.scalar.activation(SA[:, b], CV[:, b], ACT.Silu).then_inc(ff_silu, 1)
                x0, w0, wd = X0[f"down{layer}"], W0[f"gu{layer}"], W0[f"down{layer}"]
                for f in range(FT):
                    if f < 4:
                        act.wait_ge(tile_used, wd)
                    else:
                        act.wait_ge(tile_used, wd + f - 3)
                    act.wait_ge(mid_ready, layer * FT + f + 1)
                    nc.scalar.copy(XH[:, f % 4], MID[:, f]).then_inc(xh_ready, 1)

            attention(NSA_UNITS, 0, False)
            attention_out("nsa_o", 0)
            norm(3, lambda k: (freed, T0["nsa_o"] + k + 1), "g_ffn0", used=W0["gu0"])
            ffn(0)
            act.wait_ge(mid_ready, FT)
            act.wait_ge(tile_used, W0["swa"])
            for dst, name in ((cs, "cos"), (sn, "sin")):
                act.dma_start(dst, a[name]).then_inc(consts_in, 16)
            norm(4, lambda k: (down_added, k + 1), "g_mix1", used=W0["swa"])
            for j in range(10):
                act.wait_ge(freed, T0["swa"] + j + 1)
                b = TB[:, j % 2]
                bias = col("b_k") if j == 0 else col("b_q", j - 1) if j < 9 else col("b_v")
                nc.scalar.activation(b, b, ACT.Identity, bias=bias).then_inc(qb_ready, 1)
            act.wait_ge(tok_t, 6)
            nc.scalar.copy(VS[:, :, 0:2, 0:DH], psum(7).rearrange("p (t g d) -> p t g d", t=NT, d=DH)).then_inc(tok_out, 1)
            attention(SWA_UNITS, len(NSA_UNITS), True)
            attention_out("swa_o", KT)
            norm(5, lambda k: (freed, T0["swa_o"] + k + 1), "g_ffn1", used=W0["gu1"])
            ffn(1)
            norm(6, lambda k: (down_added, KT + k + 1))

        @block.vector
        def _(dve):
            step = Steps(dve, dve_step)

            def norm(q, x=None, gain=None):
                if gain:
                    for k in range(KT):
                        dve.wait_ge(xh_ready, X0[x] + k + 1)
                        nc.vector.scalar_tensor_tensor(XL[:, k], R[:, k], col(gain, k), XH[:, k].bitcast(F32),
                                                       ALU.mult, ALU.subtract).then_inc(xl_ready, 1)
                if q == 2:
                    dve.wait_ge(normed, KT)
                dve.wait_ge(sq_sum, 8 * (q + 1))
                nc.vector.tensor_scalar(RMS, psum(7), 1.0 / D, EPS, ALU.mult, ALU.add).then_inc(rms_ready, 1)
                dve.wait_ge(std_ready, q + 1)
                nc.vector.reciprocal(rstd[:], RMS).then_inc(rstd_ready, 1)
                dve.wait_ge(rstd_ready, q + 1)

            def product(stage, j):
                dve.wait_ge(tile_used, W0[stage] + j + 1)
                return (T0[stage] + j) % 2

            def lo(stage, k, src):
                dve.wait_ge(xh_ready, X0[stage] + k + 1)
                nc.vector.tensor_tensor(XL[:, k], src, XH[:, k].bitcast(F32), ALU.subtract).then_inc(xl_ready, 1)

            def add_residual(stage, bias=None, tiles=range(KT)):
                for k in tiles:
                    b = product(stage, k)
                    if bias:
                        ins = nc.vector.scalar_tensor_tensor(R[:, k], psum(b), col(bias, k), R[:, k], ALU.add, ALU.add)
                    else:
                        ins = nc.vector.tensor_tensor(R[:, k], psum(b), R[:, k], ALU.add)
                    ins.then_inc(freed, 1)

            def norm_in_place(gain, n0):
                for k in range(KT):
                    nc.vector.scalar_tensor_tensor(R[:, k], R[:, k], col(gain, k), rstd[:], ALU.mult, ALU.mult
                                                   ).then_inc(normed, 1)

            dve.wait_ge(cols_in, 16)
            norm(0, "in", "g_in")
            dve.wait_ge(consts_in, 16 * 10)
            for n in range(3):
                step.mark(nc.vector.tensor_tensor(
                    BD[n], wqkv[:, n].unsqueeze(2).broadcast_to([P, KT, 32, 4]),
                    bdm.unsqueeze(1).unsqueeze(3).broadcast_to([P, KT, 32, 4]), ALU.mult))
            for dst, src in ((identb[:], ident[:]), (masks[:], masks32), (cmask[:], cmask32)):
                step.mark(nc.vector.tensor_copy(dst, src))
            step.mark(nc.vector.memset(U[:, :, 0:UPAD], 0.0))
            step.mark(nc.vector.memset(U[:, :, US - UPAD:US], 0.0))
            for p in px:
                step.mark(nc.vector.memset(p, 0.0))
            step.wait()
            for j in range(KT):
                b = product("in", j)
                nc.vector.tensor_tensor(U[:, j, UPAD:UPAD + S], psum(b), rstd[:], ALU.mult).then_inc(freed, 1)
                dve.wait_ge(freed, j + 1)
                step.mark(nc.vector.tensor_scalar(C[:, j], U[:, j, 0:S], col("conv_w", j), col("conv_b", j), ALU.mult, ALU.add))
                for t in range(1, TAPS):
                    step.wait()
                    ins = nc.vector.scalar_tensor_tensor(C[:, j], U[:, j, t:t + S], col("conv_w", 8 * t + j), C[:, j],
                                                         ALU.mult, ALU.add)
                    if t < TAPS - 1:
                        step.mark(ins)
                    else:
                        ins.then_inc(conv_ready, 1)
            for j in range(KT):
                w = WINDOWS[j // 2]
                left = (w - 1) // 2
                b = product("in", 8 + j)
                x, s0, s1 = px
                if j >= 1:
                    dve.wait_ge(pooled_ready, j)
                nc.vector.tensor_tensor(x[:, 8:8 + S], psum(b), rstd[:], ALU.mult).then_inc(freed, 1)
                dve.wait_ge(freed, 8 + j + 1)
                src, dst, width, sh = x, s0, 536, 1
                while sh < w:
                    width -= sh
                    step.mark(nc.vector.tensor_tensor(dst[:, 0:width], src[:, 0:width], src[:, sh:sh + width], ALU.add))
                    step.wait()
                    src, dst, sh = dst, (s1 if dst is s0 else s0), 2 * sh
                step.mark(nc.vector.tensor_tensor(dst[:, 0:S], src[:, 8 - left:8 - left + S], invc[:, j // 2], ALU.mult))
                step.wait()
                nc.vector.tensor_tensor(pooled[:, j], dst[:, 0:S], x[:, 8:8 + S], ALU.subtract).then_inc(pooled_ready, 1)
            for j in range(KT):
                b = product("in", 16 + j)
                nc.vector.tensor_tensor(SZ[:, j], psum(b), rstd[:], ALU.mult).then_inc(freed, 1)
            dve.wait_ge(pooled_ready, KT)
            for j in range(KT):
                b = product("in", 24 + j)
                nc.vector.tensor_tensor(MZ[:, j], psum(b), rstd[:], ALU.mult).then_inc(freed, 1)
            for j in range(KT):
                dve.wait_ge(pool_mm, j + 1)
                dve.wait_ge(sz_ready, j + 1)
                nc.vector.scalar_tensor_tensor(SZ[:, j], psum(2 + j % 2), col("pool_scale", j), SZ[:, j], ALU.mult, ALU.mult
                                               ).then_inc(yp_ready, 1)
            for k in range(KT):
                lo("wo_pool", k, SZ[:, k])
            nc.vector.memset(V1[:, :, :, 256:257], 1.0)
            for j in range(KT):
                dve.wait_ge(vt_mm, j + 1)
                nc.vector.tensor_copy(V1[:, :, j // 2, P * (j % 2):P * (j % 2) + P],
                                      psum(5).rearrange("p (t e) -> p t e", t=NT)).then_inc(vt_out, 1)
            lf, t, F, A, FM, EM = gr
            dve.wait_ge(g_placed, 1)
            step.mark(nc.vector.memset(one5, 1.0))
            dve.wait_ge(f_rest, 1)
            step.mark(nc.vector.scalar_tensor_tensor(lf[64:128], PS[64:128, 6, :], 0.0, t[64:128], ALU.min, ALU.subtract))
            step.wait()
            step.mark(nc.vector.tensor_tensor_scan(F[0:32], one5[64:96], lf[64:96], 0.0, ALU.mult, ALU.add))
            step.mark(nc.vector.tensor_tensor_scan(F[32:64, ::-1], one5[96:128, ::-1], lf[96:128, ::-1], 0.0, ALU.mult, ALU.add))
            step.wait()
            nc.vector.tensor_tensor(A[0:64], PS[0:64, 6, :], F[0:64], ALU.subtract).then_inc(a_ready, 1)
            dve.wait_ge(a_ready, 1)
            M = t
            step.mark(nc.vector.tensor_tensor_scan(M[0:32], one5[0:32], A[0:32], 0.0, ALU.mult, ALU.max))
            step.mark(nc.vector.tensor_tensor_scan(M[32:64, ::-1], one5[32:64, ::-1], A[32:64, ::-1], 0.0, ALU.mult, ALU.max))
            step.wait()
            nc.vector.tensor_scalar(NM[0:64], M[0:64], -1.0, None, ALU.mult).then_inc(nm_ready, 1)
            nc.vector.tensor_tensor(FM[0:64], F[0:64], M[0:64], ALU.add).then_inc(fm_ready, 1)
            add_residual("wo_pool", tiles=range(2))
            dve.wait_ge(cols_mm, 1)
            nc.vector.tensor_copy(ACOL, psum(7).rearrange("p (a b) -> p a b", b=64)).then_inc(acol_ready, 1)
            dve.wait_ge(acol_ready, 1)

            offs = [[0, 512, 896, 1152], [0, 128, 384, 768]]

            def weights(h):
                for d in range(2):
                    dve.wait_ge(m_bc, 2 * h + d + 1)
                    nc.vector.tensor_tensor(WD[:, d], psum(6 + d).rearrange("p (j t) -> p j t", j=NT),
                                            masks[:, d].unsqueeze(1).broadcast_to([P, NT, P]), ALU.add).then_inc(wd_ready, 1)
                if h >= 1:
                    dve.wait_ge(num_mm, 8 * h)
                for j in range(NT):
                    dve.wait_ge(s_mm1, NT * h + j + 1)
                    for d in range(2):
                        n = 8 * h + 2 * j + d
                        dve.wait_ge(w_exp, n + 1)
                        lo_, hi_ = (P * j, S) if d == 0 else (0, P * (j + 1))
                        nc.vector.scalar_tensor_tensor(PW[d][:, offs[d][j]:offs[d][j] + hi_ - lo_], PS[:, 2 + j, lo_:hi_],
                                                       float(HD) ** -0.5, WE[:, n % 2, 0:hi_ - lo_], ALU.mult, ALU.mult
                                                       ).then_inc(p_ready, 1)

            def head_out(h):
                for i in range(NT):
                    for d in range(2):
                        n = 8 * h + 2 * i + d
                        dve.wait_ge(num_mm, n + 1)
                        emt = ACOL[:, 4 + i, 32 * d + h:32 * d + h + 1]
                        b = n % 2
                        step.mark(nc.vector.tensor_scalar(dn[:, 0:1], PS[:, b, 256:257], -1.0, emt, ALU.mult, ALU.max))
                        step.wait()
                        step.mark(nc.vector.tensor_tensor(dn[:, 1:2], PS[:, b, 256:257], dn[:, 0:1], ALU.max))
                        step.wait()
                        step.mark(nc.vector.reciprocal(dn[:, 2:3], dn[:, 1:2]))
                        step.wait()
                        out = H[:, i, HD * h:HD * (h + 1)]
                        if d == 0:
                            nc.vector.tensor_scalar(out, PS[:, b, 0:HD], dn[:, 2:3], None, ALU.mult).then_inc(num_out, 1)
                        else:
                            nc.vector.scalar_tensor_tensor(out, PS[:, b, 0:HD], dn[:, 2:3], out, ALU.mult, ALU.add
                                                           ).then_inc(num_out, 1)
                        dve.wait_ge(num_out, n + 1)
                    step.mark(nc.vector.bn_stats(bn6, H[:, i, HD * h:HD * (h + 1)]))
                    step.wait()
                    step.mark(nc.vector.bn_aggr(mv[:, 4 * h + i], bn6))
                    step.wait()

            weights(0)
            for h in range(HEADS):
                add_residual("wo_pool", tiles=POOL_TILES[h])
                head_out(h)
                if h + 1 < HEADS:
                    weights(h + 1)
            nc.vector.tensor_scalar(rv[:], mv[:, :, 1], EPS, None, ALU.add).then_inc(var_ready, 1)
            dve.wait_ge(hstd, 1)
            step.mark(nc.vector.reciprocal(rv[:], rv[:]))
            step.wait()
            for h in range(HEADS):
                for i in range(NT):
                    hh = H[:, i, HD * h:HD * (h + 1)]
                    nc.vector.tensor_scalar(hh, hh, mv[:, 4 * h + i, 0:1], rv[:, 4 * h + i:4 * h + i + 1],
                                            ALU.subtract, ALU.mult).then_inc(xhat, 1)
            for j in range(KT):
                dve.wait_ge(yt_mm, j + 1)
                dve.wait_ge(skip_ready, j + 1)
                dve.wait_ge(mz_ready, j + 1)
                step.mark(nc.vector.scalar_tensor_tensor(C[:, j], psum(2 + j % 2), col("mh", j), C[:, j], ALU.mult, ALU.add))
                step.wait()
                nc.vector.tensor_tensor(MZ[:, j], C[:, j], MZ[:, j], ALU.mult).then_inc(ym_ready, 1)
            for k in range(KT):
                lo("wo_m", k, MZ[:, k])
            add_residual("wo_m")
            norm(1)
            norm_in_place("g_out", 0)

            norm(2, "nsa", "g_mix0")
            dve.wait_ge(consts_in, 16 * 15)
            rotary_tables = [(csr, cs), (snr, sn)]
            for dst, src in rotary_tables:
                step.mark(nc.vector.tensor_tensor(dst, src, rstd[:], ALU.mult))
            for kv in range(2):
                step.mark(nc.vector.memset(XB[kv], 0.0))
            step.mark(nc.vector.memset(BDV, 0.0))
            step.mark(nc.vector.memset(VS[:, :, :, DH:DH + 1], 1.0))
            step.mark(nc.vector.memset(VW[:, :, :, DH:DH + 1], 1.0))
            step.mark(nc.vector.memset(v_pad, 0.0))
            step.mark(nc.vector.memset(BDK, 0.0))
            step.wait()

            swap = [p ^ 16 for p in range(32)]
            ropes = [0]

            def rotary(src, c_, s_, out, scale, signal, first=None):
                if ropes[0]:
                    dve.wait_ge(rope_in, ropes[0])
                ropes[0] += 1
                step.mark(nc.vector.stream_shuffle(TS, src, swap))
                ins = nc.vector.scalar_tensor_tensor(TM, src, scale, c_, ALU.mult, ALU.mult)
                if signal is not None:
                    ins.then_inc(signal, 1)
                else:
                    step.mark(ins)
                step.wait()
                step.mark(nc.vector.scalar_tensor_tensor(TS, TS, scale, s_, ALU.mult, ALU.mult))
                step.wait()
                if signal is not None:
                    dve.wait_ge(signal, first)
                nc.vector.tensor_tensor(out, TM, TS, ALU.add).then_inc(rope_in, 1)

            def compression_input(kv, src):
                pe0 = COLS["pe_k" if kv == 0 else "pe_v"]
                for g in range(NG):
                    half = slice(DH * (g % 2), DH * (g % 2) + DH)
                    tok = src[half, g // 2].rearrange("p (c x two) -> p two x c", two=2, x=8)
                    pe = cols[half, pe0:pe0 + CLEN].rearrange("p (m two) -> p two m", two=2)
                    for par in range(2):
                        for mh in range(2):
                            ins = nc.vector.tensor_tensor(
                                XB[kv][DH * par:DH * par + DH, 8 * mh:8 * mh + 8, g, 0:CMP],
                                tok[:, par, :, mh:mh + CMP],
                                pe[:, par, 8 * mh:8 * mh + 8].unsqueeze(2).broadcast_to([DH, 8, CMP]), ALU.add)
                            ins.then_inc(xb_ready, 1)

            t0 = T0["nsa"]
            for j, out in ((0, KC[:, 0]), (1, KC[:, 1])):
                rotary(psum(product("nsa", j)), csr, snr, out, 1.0, freed, t0 + j + 1)
            for j in range(2):
                nc.vector.tensor_tensor(VC[:, j], psum(product("nsa", 2 + j)), rstd[:], ALU.mult).then_inc(freed, 1)
            for n, out in enumerate((KS[:, 0], KS[:, 1], KW[:, 0], KW[:, 1])):
                rotary(psum(product("nsa", 4 + n)), csr, snr, out, 1.0, freed, t0 + 5 + n)
            dve.wait_ge(rope_in, 6)
            dve.wait_ge(freed, t0 + 4)
            compression_input(0, KC)
            for n in range(4):
                rotary(psum(product("nsa", 8 + n)), csr, snr, QN[:, n], float(DH) ** -0.5, freed, t0 + 9 + n)
            compression_input(1, VC)
            for n in range(4, 8):
                rotary(psum(product("nsa", 8 + n)), csr, snr, QN[:, n], float(DH) ** -0.5, freed, t0 + 9 + n)

            def tokens(j):
                b = product("nsa", 16 + j)
                if j >= 2:
                    dve.wait_ge(tok_t, j - 1)
                nc.vector.tensor_tensor((TS, TM)[j % 2], psum(b), rstd[:], ALU.mult).then_inc(freed, 1)

            def c_arg(i):
                s_ = PS[:, 2:4, :].rearrange("p a (r c) -> p a r c", c=P)[:, :, :, 0:2 * CP]
                dve.wait_ge(cs_mm, i + 1)
                if i >= 2:
                    dve.wait_ge(cs_t, i - 1)
                step.wait()
                for gp in range(2):
                    step.mark(nc.vector.tensor_reduce(cst[:, 0, 8 * gp:8 * gp + 8],
                                                      s_[:, gp].rearrange("p r (o c) -> p r o c", c=CP), AX.X, ALU.max, negate=True))
                step.wait()
                step.mark(nc.vector.tensor_scalar(cst[:, 0], cst[:, 0], 1e20, None, ALU.min))
                step.wait()
                for gp in range(2):
                    ins = nc.vector.tensor_tensor(
                        SX[i % 2][:, 8 * gp:8 * gp + 8].rearrange("p (r o) c -> p r o c", o=2),
                        s_[:, gp].rearrange("p r (o c) -> p r o c", c=CP),
                        cst[:, 0, 8 * gp:8 * gp + 8].rearrange("p (r o) -> p r o", o=2).unsqueeze(3).broadcast_to([P, 4, 2, CP]),
                        ALU.add)
                    if gp == 0:
                        step.mark(ins)
                    else:
                        ins.then_inc(cs_arg, 1)

            def c_norm(i):
                dve.wait_ge(cs_exp, i + 1)
                step.mark(nc.vector.tensor_reduce(cst[:, 1], SX[i % 2], AX.X, ALU.add))
                step.wait()
                step.mark(nc.vector.tensor_scalar(cst[:, 1], cst[:, 1], 1e-30, None, ALU.max))
                step.wait()
                step.mark(nc.vector.reciprocal(cst[:, 2], cst[:, 1]))
                step.wait()
                step.mark(nc.vector.tensor_tensor(
                    cst[:, 2].rearrange("p (g r o) -> p g r o", g=2, o=2), cst[:, 2].rearrange("p (g r o) -> p g r o", g=2, o=2),
                    GT[:, i].rearrange("p (g o r m) -> p g r o m", g=2, o=2, m=3)[:, :, :, :, 0], ALU.mult))
                step.wait()
                nc.vector.tensor_tensor(SX[i % 2], SX[i % 2], cst[:, 2].unsqueeze(2).broadcast_to([P, HQ, CP]), ALU.mult
                                        ).then_inc(cs_norm, 1)
                dve.wait_ge(cs_norm, i + 1)

            dve.wait_ge(rope_in, 14)
            tokens(0)
            dve.wait_ge(hid_ready, 2)
            nc.vector.tensor_copy(HIDR, HID[1].rearrange("p a (g o) c -> p (a g) (o c)", g=2).unsqueeze(2).broadcast_to(
                [P, NG, 2, 2 * CP])).then_inc(kv_ready, 1)
            dve.wait_ge(cmp_mm, 1)
            for odd in range(2):
                q = slice(DH * odd, DH * odd + DH)
                nc.vector.tensor_copy(BDK[q, :, CP * odd:CP * odd + CP],
                                      PS[q, 4, 0:P].rearrange("p (g o c) -> p g o c", g=2, o=2)[:, :, odd]).then_inc(cmp_ready, 1)
            dve.wait_ge(cmp_mm, 2)
            for r in range(4):
                q = slice(32 * r, 32 * r + 32)
                nc.vector.tensor_copy(BDV[q, :, r, :], PS[q, 5, 0:256].rearrange("p (g d) -> p g d", g=2)[:, :, 0:DH]
                                      ).then_inc(cmp_ready, 1)
            tokens(1)
            dve.wait_ge(tok_t, 1)
            nc.vector.tensor_tensor(GT, psum(7).rearrange("p (t x) -> p t x", x=P)[:, :, 0:48],
                                    rows[:, 0:48].unsqueeze(1).broadcast_to([P, NT, 48]), ALU.add).then_inc(gt_raw, 1)
            c_arg(0)
            tokens(2)
            dve.wait_ge(gt_ready, 1)
            c_norm(0)
            c_arg(1)
            tokens(3)
            c_norm(1)
            c_arg(2)
            tokens(4)
            c_norm(2)
            c_arg(3)
            c_norm(3)

            def attention(units, v0, swa):
                def maxima(v):
                    c, m, i = units[v - v0]
                    n = P * min(i + 1, 2) if swa else P * (i + 1)
                    dve.wait_ge(s_mm, v + 1)
                    b = 2 + 2 * (v % 2)
                    s_ = PS[:, b:b + 2, 0:n]
                    if not swa:
                        nc.vector.tensor_reduce(nmr[:, v % 4], s_, AX.X, ALU.max, negate=True).then_inc(nmax, 1)
                        return
                    step.mark(nc.vector.tensor_reduce(nmx[:, v % 4], s_, AX.X, ALU.max, negate=True))
                    step.wait()
                    nc.vector.tensor_tensor(nmr[:, v % 4], nmx[:, v % 4], nsk.rearrange("p (a b) -> p a b", a=2)[:, :, c],
                                            ALU.min).then_inc(nmax, 1)
                    dve.wait_ge(nmax, v + 1)
                    nc.vector.tensor_tensor(ske[:, v % 4], nmr[:, v % 4], nsk.rearrange("p (a b) -> p a b", a=2)[:, :, c],
                                            ALU.subtract).then_inc(qb_raw, 1)

                def evac(v):
                    c, m, i = units[v - v0]
                    n = P * min(i + 1, 2) if swa else P * (i + 1)
                    dve.wait_ge(pt_mm, v + 1)
                    if v >= 2:
                        dve.wait_ge(o_mm, v - 1)
                    nc.vector.tensor_copy(PT_[:, v % 2, 0, 0:n], psum(6, n)).then_inc(pt_d, 1)

                def output(v):
                    c, m, i = units[v - v0]
                    dve.wait_ge(o_mm, v + 1)
                    o_ = PS[:, v % 2, 0:2 * VN].rearrange("p (a b) -> p a b", b=VN)
                    if swa:
                        dve.wait_ge(p_exp, v + 1)
                        step.mark(nc.vector.tensor_tensor(rec[:, 2], o_[:, :, DH], esk[:, v % 4], ALU.add))
                        step.wait()
                        step.mark(nc.vector.reciprocal(rec[:, 0], rec[:, 2]))
                    else:
                        step.mark(nc.vector.reciprocal(rec[:, 0], o_[:, :, DH]))
                    step.wait()
                    w = rec[:, 0]
                    if not swa:
                        g = GT[:, i].rearrange("p (g x) -> p g x", x=12)[:, 2 * (c // 4):2 * (c // 4) + 2, 3 * (c % 4) + 1 + m]
                        step.mark(nc.vector.tensor_tensor(rec[:, 1], rec[:, 0], g, ALU.mult))
                        step.wait()
                        w = rec[:, 1]
                    for hh in range(2):
                        dst = OA[:, i, c, hh]
                        if swa:
                            ins = nc.vector.tensor_scalar(dst, o_[:, hh, 0:DH], w[:, hh:hh + 1], None, ALU.mult)
                        else:
                            ins = nc.vector.scalar_tensor_tensor(dst, o_[:, hh, 0:DH], w[:, hh:hh + 1], dst, ALU.mult, ALU.add)
                        if hh == 0:
                            step.mark(ins)
                        else:
                            ins.then_inc(o_done, 1)
                    dve.wait_ge(o_done, v + 1)

                last = v0 + len(units)
                maxima(v0)
                maxima(v0 + 1)
                evac(v0)
                for v in range(v0, last):
                    if v + 2 < last:
                        maxima(v + 2)
                    if v + 1 < last:
                        evac(v + 1)
                    output(v)

            def attention_out(stage, n0):
                for c in range(KT):
                    dve.wait_ge(oa_mm, n0 + c + 1)
                    lo(stage, c, psum(2 + c % 2))

            def ffn(layer):
                st, t0 = f"gu{layer}", T0[f"gu{layer}"]
                fcw = cols[:, COLS[f"fcw{layer}"]:COLS[f"fcw{layer}"] + 3 * FT]
                fcb = cols[:, COLS[f"fcb{layer}"]:COLS[f"fcb{layer}"] + FT]
                step.mark(nc.vector.memset(AP_[:, :, 0:2], 0.0))
                step.wait()
                before = step.n
                with dve.Fori(0, FT // 2) as it:
                    step.off = 4 * it
                    for b in range(2):
                        w = [fcw[:, bass.ds(t * FT + b + 2 * it, 1)] for t in range(3)]
                        bias = fcb[:, bass.ds(b + 2 * it, 1)]
                        bank = (t0 + 2 * b) % 2
                        dve.wait_ge(tile_used, W0[st] + 4 * it + (2 * b + 1))
                        nc.vector.tensor_tensor(AP_[:, b, 2:2 + S], psum(bank), rstd[:], ALU.mult).then_inc(freed, 1)
                        dve.wait_ge(freed, t0 + 4 * it + (2 * b + 1))
                        step.mark(nc.vector.tensor_scalar(CV[:, b], AP_[:, b, 0:S], w[0], bias, ALU.mult, ALU.add))
                        step.wait()
                        step.mark(nc.vector.scalar_tensor_tensor(CV[:, b], AP_[:, b, 1:1 + S], w[1], CV[:, b], ALU.mult, ALU.add))
                        step.wait()
                        nc.vector.scalar_tensor_tensor(CV[:, b], AP_[:, b, 2:2 + S], w[2], CV[:, b], ALU.mult, ALU.add
                                                       ).then_inc(ff_conv, 1)
                        dve.wait_ge(tile_used, W0[st] + 4 * it + (2 * b + 2))
                        nc.vector.tensor_tensor(TU[:, b], psum(1 - bank), rstd[:], ALU.mult).then_inc(freed, 1)
                        dve.wait_ge(freed, t0 + 4 * it + (2 * b + 2))
                        dve.wait_ge(ff_silu, layer * FT + 2 * it + (b + 1))
                        nc.vector.tensor_tensor(MID[:, bass.ds(2 * it + b, 1)].rearrange("p o t -> p (o t)"), TU[:, b], SA[:, b], ALU.mult).then_inc(mid_ready, 1)
                assert step.n - before == 4
                step.n, step.off = before + 4 * (FT // 2), 0
                for f in range(FT):
                    dve.wait_ge(xh_ready, X0[f"down{layer}"] + f + 1)
                    nc.vector.tensor_tensor(XL[:, f % 4], MID[:, f], XH[:, f % 4].bitcast(F32), ALU.subtract).then_inc(xl_ready, 1)
                for k in range(KT):
                    if k < KT - 1:
                        dve.wait_ge(down_mm, (KT - 1) * layer + k + 1)
                    else:
                        dve.wait_ge(tile_used, W0[f"down{layer}"] + FT)
                    nc.vector.tensor_tensor(R[:, k], psum(k), R[:, k], ALU.add).then_inc(down_added, 1)

            attention(NSA_UNITS, 0, False)
            attention_out("nsa_o", 0)
            add_residual("nsa_o")
            norm(3, "gu0", "g_ffn0")
            ffn(0)

            norm(4, "swa", "g_mix1")
            step.mark(nc.vector.tensor_scalar(nsk, rows[:, 48:64], -1.0, None, ALU.mult))
            step.mark(nc.vector.memset(VS[:, :, :, DH:DH + 1], 1.0))
            dve.wait_ge(consts_in, 16 * 17)
            t0 = T0["swa"]
            for j in range(10):
                b = product("swa", j)
                if j >= 2:
                    dve.wait_ge(rope_in, 14 + j - 1)
                nc.vector.tensor_tensor(TB[:, j % 2], psum(b), rstd[:], ALU.mult).then_inc(freed, 1)
                if j >= 1:
                    dve.wait_ge(qb_ready, j)
                    rotary(TB[:, (j - 1) % 2], cs, sn, KS[:, 0] if j == 1 else QN[:, j - 2],
                           1.0 if j == 1 else float(DH) ** -0.5, None)
            attention(SWA_UNITS, len(NSA_UNITS), True)
            attention_out("swa_o", KT)
            add_residual("swa_o", "b_o")
            norm(5, "gu1", "g_ffn1")
            ffn(1)
            norm(6)
            norm_in_place("g_fin", KT)

        @block.tensor
        def _(pe):
            mm = nc.tensor.matmul

            def norm(q):
                for k in range(KT):
                    pe.wait_ge(sq_ready, 8 * q + k + 1)
                    if k == 0 and q == 0:
                        pe.wait_ge(zero_set, 2)
                    mm(psum(7), ones[:], SQ[:, k % 2], start=(k == 0), stop=(k == KT - 1)).then_inc(sq_sum, 1)

            def wait_bank(t):
                if t >= 2:
                    pe.wait_ge(freed, t - 1)

            def channel_major(stage, j, n, xname=None):
                w, t = W0[stage] + j, T0[stage] + j
                x = X0[xname or stage]
                wait_bank(t)
                pe.wait_ge(tile_split, w + 1)
                s = w % SPL
                for k in range(KT):
                    if j == 0:
                        pe.wait_ge(xh_ready, x + k + 1)
                        pe.wait_ge(xl_ready, x + k + 1)
                    out = psum(t % 2)
                    mm(out, WH[:, s, k], XH[:, k], start=(k == 0), stop=False)
                    mm(out, WH[:, s, k], XL[:, k], start=False, stop=False)
                    ins = mm(out, WL[:, s, k], XH[:, k], start=False, stop=(k == KT - 1))
                ins.then_inc(tile_used, 1)

            def linear(stage, n=KT, q=None):
                for j in range(n):
                    channel_major(stage, j, n)
                    if j == 0 and q is not None:
                        norm(q)

            def turn_values(n, src, ready, value, bank_free):
                pe.wait_ge(ready, value)
                if bank_free:
                    pe.wait_ge(tok_out, bank_free - 1)
                for i in range(NT):
                    ins = nc.tensor.transpose(PS[:, 7, P * i:P * (i + 1)], src[:, P * i:P * (i + 1)], ident[:])
                ins.then_inc(tok_t, 1)

            def head_scores(h):
                for j in range(NT):
                    if h >= 1:
                        pe.wait_ge(p_ready, 8 * (h - 1) + 2 * j + 2)
                    for e in range(2):
                        ins = mm(psum(2 + j), K1[:, 2 * h + e, P * j:P * (j + 1)], Q1[:, 2 * h + e], start=(e == 0), stop=(e == 1))
                    ins.then_inc(s_mm1, 1)

            linear("in", 32, 0)
            for j in range(KT):
                if j == 0:
                    pe.wait_ge(pooled_ready, KT)
                if j >= 2:
                    pe.wait_ge(yp_ready, j - 1)
                for c in range(2):
                    ins = mm(psum(2 + j % 2), poolw[:, (j // 2) * 4 + 2 * c + j % 2], pooled[:, 2 * (j // 2) + c],
                             start=(c == 0), stop=(c == 1))
                ins.then_inc(pool_mm, 1)
            pe.wait_ge(yp_ready, KT)
            pe.wait_ge(dve_step, 3)
            for j in range(KT + 1):
                if j < KT:
                    pe.wait_ge(c_ready, j + 1)
                    for n, src in enumerate((C[:, j], C[:, j], U[:, j, UPAD:UPAD + S])):
                        if j >= 1:
                            pe.wait_ge(q_out, 3 * (j - 1) + n + 1)
                        mm(psum(2 + n), BD[n][:, j].rearrange("p a b -> p (a b)"), src, start=True, stop=True).then_inc(q_mm, 1)
                    if j >= 1:
                        pe.wait_ge(vt_out, j)
                    for i in range(NT):
                        ins = mm(PS[:, 5, P * i:P * (i + 1)], U[:, j, UPAD + P * i:UPAD + P * (i + 1)],
                                 BD[2][:, j].rearrange("p a b -> p (a b)"), start=True, stop=True)
                    ins.then_inc(vt_mm, 1)
                if j >= 1:
                    pe.wait_ge(q_out, 3 * j)
                    for n, src in enumerate((Q1[:, j - 1], K1[:, j - 1], VT[:, (j - 1) % 2])):
                        ins = mm(PS[0:16, 7, :], wg[:, 8 * n + j - 1], src, start=(j == 1 and n == 0),
                                 stop=(j == KT and n == 2))
                    ins.then_inc(gate_mm, 1)
            pe.wait_ge(g16, 1)
            mm(psum(6), place_w[0:16], G16[0:16], start=True, stop=True).then_inc(g_placed, 1)
            pe.wait_ge(q_out, 3 * KT)
            pe.wait_ge(vt_out, KT)
            head_scores(0)
            for j in range(2):
                channel_major("wo_pool", j, KT)
            pe.wait_ge(a_ready, 1)
            pe.wait_ge(emt_ready, 1)
            pe.wait_ge(g16, 1)
            for n, src in ((0, gr[3]), (1, gr[5])):
                for i in range(NT):
                    ins = nc.tensor.transpose(PS[:, 7, 64 * (4 * n + i):64 * (4 * n + i) + 64], src[0:64, P * i:P * (i + 1)],
                                              ident[0:64, 0:64])
            ins.then_inc(cols_mm, 1)

            offs = [[0, 512, 896, 1152], [0, 128, 384, 768]]

            def maxima_rows(h):
                if h == 0:
                    pe.wait_ge(nm_ready, 1)
                    pe.wait_ge(acol_ready, 1)
                else:
                    pe.wait_ge(w_exp, 8 * h)
                    pe.wait_ge(wd_ready, 2 * h)
                for d in range(2):
                    q = slice(32 * d, 32 * d + 32)
                    mm(psum(6 + d), ident[q, 32 * d + h:32 * d + h + 1].broadcast_to([32, P]), NM[q], start=True, stop=True
                       ).then_inc(m_bc, 1)

            def numerators(h):
                pe.wait_ge(p_ready, 8 * (h + 1))
                for i in range(NT):
                    for d in range(2):
                        n = 8 * h + 2 * i + d
                        if n >= 2:
                            pe.wait_ge(num_out, n - 1)
                        js = range(i + 1) if d == 0 else range(i, NT)
                        for j in js:
                            at = offs[d][j] + (P * (i - j) if d == 0 else P * i)
                            ins = mm(PS[:, n % 2, 0:257], PW[d][:, at:at + P], V1[:, j, h], start=(j == js[0]), stop=(j == js[-1]))
                        ins.then_inc(num_mm, 1)

            maxima_rows(0)
            for h in range(HEADS):
                if h >= 1:
                    pe.wait_ge(num_out, 8 * h)
                for j in POOL_TILES[h]:
                    channel_major("wo_pool", j, KT)
                if h + 1 < HEADS:
                    maxima_rows(h + 1)
                    head_scores(h + 1)
                pe.wait_ge(freed, T0["wo_pool"] + POOL_TILES[h][-1] + 1)
                numerators(h)
            pe.wait_ge(xhat, 16)
            for j in range(KT):
                if j >= 2:
                    pe.wait_ge(ym_ready, j - 1)
                for i in range(NT):
                    ins = nc.tensor.transpose(PS[:, 2 + j % 2, P * i:P * (i + 1)], H[:, i, P * j:P * (j + 1)], ident[:])
                ins.then_inc(yt_mm, 1)
            linear("wo_m")
            norm(1)

            linear("nsa", 16, 2)
            pe.wait_ge(xb_ready, 32)
            pe.wait_ge(consts_in, 16 * 15)
            for kv in range(2):
                for ht in range(2):
                    for m in range(16):
                        ins = mm(PS[:, 2 + kv, P * ht:P * (ht + 1)], CW1[kv][:, m, P * ht:P * (ht + 1)],
                                 XB[kv][:, m].rearrange("p g c -> p (g c)"), start=(m == 0), stop=(m == 15))
                ins.then_inc(hid_mm, 1)
            channel_major("nsa", 16, 21)
            pe.wait_ge(hid_ready, 2)
            for ht in range(2):
                ins = mm(PS[:, 4, 0:P], CW2[:, 0, ht], HID[0][:, ht].rearrange("p g c -> p (g c)"), start=(ht == 0), stop=(ht == 1))
            ins.then_inc(cmp_mm, 1)
            pe.wait_ge(kv_ready, 1)
            for gp in range(2):
                for ht in range(2):
                    ins = mm(PS[:, 5, P * gp:P * (gp + 1)], HIDR[:, 2 * ht + gp].rearrange("p r c -> p (r c)"),
                             CW2[:, 1, ht], start=(ht == 0), stop=(ht == 1))
            ins.then_inc(cmp_mm, 1)

            def c_scores(i):
                if i == 0:
                    pe.wait_ge(rope_in, 14)
                    pe.wait_ge(cmp_ready, 6)
                else:
                    pe.wait_ge(cs_arg, i)
                for gp in range(2):
                    mm(psum(2 + gp).rearrange("p (r c) -> p r c", c=P), identb[:],
                       cmask[:, i].unsqueeze(1).broadcast_to([P, 4, P]), start=True, stop=False)
                    for r in range(4):
                        ins = mm(PS[:, 2 + gp, P * r:P * (r + 1)], QN[:, 4 * gp + r, P * i:P * (i + 1)], BDK[:, gp],
                                 start=False, stop=(r == 3))
                ins.then_inc(cs_mm, 1)

            def c_turn(i):
                pe.wait_ge(cs_norm, i + 1)
                if i >= 1:
                    pe.wait_ge(cs_tout, i)
                for n in range(4):
                    ins = nc.tensor.transpose(PS[:, 6, P * n:P * (n + 1)],
                                              SX[i % 2][:, 4 * n:4 * n + 4].rearrange("p r c -> p (r c)"), ident[:])
                ins.then_inc(cs_t, 1)

            def c_out(i):
                pe.wait_ge(cs_tout, i + 1)
                for n in range(4):
                    if i >= 1 and n % 2 == 0:
                        pe.wait_ge(cs_out, 2 * (i - 1) + n // 2 + 1)
                    ins = mm(PS[:, 4 + n // 2, 256 * (n % 2):256 * (n % 2) + 256], PTC[i % 2][:, n],
                             BDV[:, n // 2].rearrange("p r d -> p (r d)"), start=True, stop=True)
                    if n % 2 == 1:
                        ins.then_inc(cs_o, 1)

            t0 = T0["nsa"]
            channel_major("nsa", 17, 21)
            turn_values(0, TS, freed, t0 + 17, 0)
            c_scores(0)
            channel_major("nsa", 18, 21)
            pe.wait_ge(gt_raw, 1)
            turn_values(1, TM, freed, t0 + 18, 0)
            c_scores(1)
            c_turn(0)
            channel_major("nsa", 19, 21)
            turn_values(2, TS, freed, t0 + 19, 2)
            c_out(0)
            c_turn(1)
            c_scores(2)
            channel_major("nsa", 20, 21)
            turn_values(3, TM, freed, t0 + 20, 3)
            c_out(1)
            c_turn(2)
            c_scores(3)
            turn_values(4, TS, freed, t0 + 21, 4)
            c_out(2)
            c_turn(3)
            c_out(3)
            pe.wait_ge(tok_out, 4)
            pe.wait_ge(cs_out, 8)
            pe.wait_ge(freed, T0["nsa_o"])

            def attention(units, v0, swa):
                def keys(i):
                    return (range(max(i - 1, 0), i + 1) if swa else range(i + 1))

                def score(v):
                    c, m, i = units[v - v0]
                    js = keys(i)
                    n, k0 = P * len(js), P * js[0]
                    K = KS[:, 0] if swa else (KS, KW)[m][:, c // 4]
                    if v >= 2:
                        pe.wait_ge(p_exp, v - 1)
                    for hh in range(2):
                        half = slice(DH * hh, DH * hh + DH)
                        b = 2 + 2 * (v % 2) + hh
                        mm(PS[:, b, 0:n], QN[half, c, P * i:P * (i + 1)], K[half, k0:k0 + n], start=True, stop=False)
                        if swa and i >= 1:
                            mm(PS[:, b, 0:P], identb[:], masks[:, 2], start=False, stop=False)
                        ins = mm(PS[:, b, n - P:n], identb[:], masks[:, 1], start=False, stop=True)
                    ins.then_inc(s_mm, 1)

                def turn(v):
                    c, m, i = units[v - v0]
                    pe.wait_ge(p_exp, v + 1)
                    if v >= 1:
                        pe.wait_ge(pt_d, v)
                        pe.wait_ge(pt_a, v)
                    for hh in range(2):
                        for n in range(len(keys(i))):
                            ins = nc.tensor.transpose(PS[:, 6 + hh, P * n:P * (n + 1)], PE_[:, v % 2, hh, P * n:P * (n + 1)],
                                                      ident[:])
                    ins.then_inc(pt_mm, 1)

                def output(v):
                    c, m, i = units[v - v0]
                    pe.wait_ge(pt_d, v + 1)
                    pe.wait_ge(pt_a, v + 1)
                    if v >= 2:
                        pe.wait_ge(o_done, v - 1)
                    for hh in range(2):
                        js = keys(i)
                        for n, j in enumerate(js):
                            at = 65 * (NG * j + hh + (0 if swa else 2 * (c // 4)))
                            ins = mm(PS[:, v % 2, VN * hh:VN * (hh + 1)], PT_[:, v % 2, hh, P * n:P * (n + 1)],
                                     v_rows[0 if swa else m][:, at:at + VN], start=(n == 0), stop=(n == len(js) - 1))
                    ins.then_inc(o_mm, 1)

                last = v0 + len(units)
                score(v0)
                score(v0 + 1)
                turn(v0)
                for v in range(v0, last):
                    if v + 2 < last:
                        score(v + 2)
                    if v + 1 < last:
                        turn(v + 1)
                    output(v)

            def attention_out(stage, n0, units):
                pe.wait_ge(o_done, units)
                for c in range(KT):
                    if c >= 2:
                        pe.wait_ge(xl_ready, X0[stage] + c - 1)
                    for i in range(NT):
                        ins = nc.tensor.transpose(PS[:, 2 + c % 2, P * i:P * (i + 1)], OA[:, i, c].rearrange("p a d -> p (a d)"),
                                                  ident[:])
                    ins.then_inc(oa_mm, 1)

            def ffn(layer, q):
                st, sd = f"gu{layer}", f"down{layer}"
                w0, t0, x0 = W0[st], T0[st], X0[st]
                wd, xd = W0[sd], X0[sd]
                for j in range(4):
                    channel_major(st, j, 2 * FT)
                    if j == 0:
                        norm(q)
                with pe.Fori(1, FT // 2) as it:
                    for b in range(4):
                        pe.wait_ge(freed, t0 + 4 * it + (b - 1))
                        pe.wait_ge(tile_split, w0 + 4 * it + (b + 1))
                        s, out = (w0 + b) % SPL, psum((t0 + b) % 2)
                        for k in range(KT):
                            mm(out, WH[:, s, k], XH[:, k], start=(k == 0), stop=False)
                            mm(out, WH[:, s, k], XL[:, k], start=False, stop=False)
                            ins = mm(out, WL[:, s, k], XH[:, k], start=False, stop=(k == KT - 1))
                        ins.then_inc(tile_used, 1)
                pe.wait_ge(freed, t0 + 2 * FT)
                for f in range(FT):
                    s, x = (wd + f) % SPL, f % 4
                    pe.wait_ge(tile_split, wd + f + 1)
                    pe.wait_ge(xh_ready, xd + f + 1)
                    pe.wait_ge(xl_ready, xd + f + 1)
                    for k in range(KT):
                        mm(psum(k), WH[:, s, k], XH[:, x], start=(f == 0), stop=False)
                        mm(psum(k), WH[:, s, k], XL[:, x], start=False, stop=False)
                        ins = mm(psum(k), WL[:, s, k], XH[:, x], start=False, stop=(f == FT - 1))
                        if f == FT - 1 and k < KT - 1:
                            ins.then_inc(down_mm, 1)
                    ins.then_inc(tile_used, 1)

            attention(NSA_UNITS, 0, False)
            attention_out("nsa_o", 0, len(NSA_UNITS))
            linear("nsa_o")
            ffn(0, 3)
            pe.wait_ge(down_added, KT)
            linear("swa", 10, 4)
            turn_values(10, TB[:, 1], qb_ready, 10, 5)
            pe.wait_ge(tok_out, 5)
            pe.wait_ge(rope_in, 14 + 9)
            attention(SWA_UNITS, len(NSA_UNITS), True)
            attention_out("swa_o", KT, len(NSA_UNITS) + len(SWA_UNITS))
            linear("swa_o")
            ffn(1, 5)
            pe.wait_ge(down_added, 2 * KT)
            norm(6)



def _tiles(w):
    k, m = w.shape
    return np.ascontiguousarray(w.reshape(KT, P, m // P, P).transpose(2, 1, 0, 3))


def _vec(v):
    return v.reshape(-1, P).T


_QUADS = [np.arange(16 * q, 16 * q + 16) for q in range(2)]
PERM = np.concatenate([np.concatenate([x, x + 32]) for x in _QUADS])


def _constants():
    r, c = np.arange(P)[:, None], np.arange(P)[None, :]
    low = np.float32(-1e30)
    masks = np.stack([np.where(m, np.float32(0), low) for m in (c >= r, c <= r, c > r)], 1)
    pos = np.arange(S)
    end = np.arange(CP) * 16 + CLEN - 1
    cm = np.where((end[None, :] <= pos[:, None]) & (np.arange(CP)[None, :] < CMP), np.float32(0), low)
    cm = np.concatenate([cm, cm, np.zeros((S, 2 * CP), np.float32)], 1)
    cmask = np.ascontiguousarray(cm.reshape(NT, P, P).transpose(1, 0, 2))
    counts = []
    for w in WINDOWS:
        left = (w - 1) // 2
        counts.append(np.minimum(pos + w - 1 - left, S - 1) - np.maximum(pos - left, 0) + 1)
    invc = (1.0 / np.stack(counts)).astype(np.float32)
    inv = np.float32(10000.0) ** (-np.arange(0, DH, 2, dtype=np.float32) / np.float32(DH))
    ang = np.arange(S, dtype=np.float32)[:, None] * inv[None, :]
    cos, sin = np.cos(ang).astype(np.float32).T, np.sin(ang).astype(np.float32).T
    freq = np.tile(PERM % 32, 2)
    sign = np.tile(np.where(PERM < 32, -1.0, 1.0), 2).astype(np.float32)[:, None]
    place = np.zeros((16, P), np.float32)
    for d in range(2):
        for g in range(8):
            place[8 * d + g, 32 * d + g if g < 4 else 64 + 32 * d + g - 4] = 1.0
    return {
        "ident": np.eye(P, dtype=np.float32),
        "masks": masks, "cmask": cmask,
        "invc": np.ascontiguousarray(np.broadcast_to(invc, (P, 4, S))),
        "bdm": (r // 4 == np.arange(32)[None, :]).astype(np.float32),
        "cos": np.ascontiguousarray(cos[freq]), "sin": np.ascontiguousarray(sin[freq] * sign), "place": place,
    }


def _layout(i):
    f = {k: np.asarray(v) for k, v in i.items()}
    w_in = f["w_in"][0]
    part = lambda n: w_in[:, n * D:(n + 1) * D]
    head_nsa = [(2 * (c // 4) + hh) * 4 + c % 4 for c in range(8) for hh in range(2)]
    head_swa = [hh * 8 + c for c in range(8) for hh in range(2)]
    rot = lambda heads: np.concatenate([h * DH + PERM for h in heads])
    flat = lambda heads: np.concatenate([h * DH + np.arange(DH) for h in heads])
    nw = f["nsa_w_in_2"][0]
    kv = lambda n: nw[:, HQ * DH + 256 * n:HQ * DH + 256 * (n + 1)]
    gates = np.zeros((D, P), np.float32)
    gates[:, 0:48] = nw[:, HQ * DH + 6 * 256:]
    k4, k2 = rot(range(4)), rot(range(2))
    nsa = np.concatenate([kv(0)[:, k4], kv(1), kv(2)[:, k4], kv(4)[:, k4], nw[:, :HQ * DH][:, rot(head_nsa)],
                          gates, kv(3), kv(5)], 1)
    sw, sbias = f["swa_w_qkv_2"][0], f["swa_b_qkv_2"][0]
    swa = np.concatenate([sw[:, HQ * DH:HQ * DH + P][:, k2], sw[:, :HQ * DH][:, rot(head_swa)], sw[:, HQ * DH + P:]], 1)
    gu = []
    for n in range(2):
        g = f["ffn_w_gu_2"][n].reshape(D, 2, FT, P).transpose(0, 2, 1, 3)
        gu.append(_tiles(g.reshape(D, 2 * FF)))
    down = [f["ffn_w_down_2"][n].reshape(FT, P, KT, P) for n in range(2)]
    w = np.concatenate([
        _tiles(np.concatenate([part(2), part(0), part(1), part(3)], 1)),
        _tiles(f["w_out"][0][:D]), _tiles(f["w_out"][0][D:]), _tiles(nsa),
        _tiles(f["nsa_w_o_2"][0][flat(head_nsa)]), gu[0], down[0],
        _tiles(swa), _tiles(f["swa_w_o_2"][0][flat(head_swa)]), gu[1], down[1]])
    c = np.zeros((P, NCOL), np.float32)

    def put(name, v):
        c[:, COLS[name]:COLS[name] + v.shape[1]] = v

    for name, v in (("g_in", f["norm_in_g"][0]), ("g_out", f["norm_out_g"]), ("pool_scale", f["pool_scale"][0]),
                    ("conv_w", f["conv_w"][0]), ("conv_b", f["conv_b"][0]), ("mh", f["mh_norm_w"][0]),
                    ("skip", f["skip_w"][0]), ("g_mix0", f["norm_mix_2"][0]), ("g_mix1", f["norm_mix_2"][1]),
                    ("g_ffn0", f["norm_ffn_2"][0]), ("g_ffn1", f["norm_ffn_2"][1]), ("g_fin", f["norm_final_2"]),
                    ("b_q", sbias[:HQ * DH][rot(head_swa)]), ("b_k", sbias[HQ * DH:HQ * DH + P][k2]),
                    ("b_v", sbias[HQ * DH + P:]),
                    ("b_o", f["swa_b_o_2"][0]), ("fcw0", f["ffn_conv_w_2"][0]), ("fcw1", f["ffn_conv_w_2"][1]),
                    ("fcb0", f["ffn_conv_b_2"][0]), ("fcb1", f["ffn_conv_b_2"][1])):
        put(name, _vec(v))
    c[0:16, COLS["b_gates"]] = f["b_gates"][0].reshape(16)
    pe = f["nsa_cmp_pe_2"][0]
    put("pe_k", np.tile(pe[0].T[PERM], (2, 1)))
    put("pe_v", np.tile(pe[1].T, (2, 1)))
    row = np.concatenate([f["nsa_gate_b_2"][0], f["swa_sinks_2"][0]])
    w1, w2 = f["nsa_cmp_w1_2"][0], f["nsa_cmp_w2_2"][0]
    w1 = [w1[0].reshape(CLEN, DH, 256)[:, PERM].reshape(16, P, 256), w1[1].reshape(16, P, 256)]
    w2 = [np.concatenate([x, x], 1).reshape(2, P, P) for x in (w2[0][:, PERM], w2[1])]
    maps = np.stack([f[n][0].reshape(KT, P, 4) for n in ("w_q", "w_k", "w_v")])
    return {
        "x": f["x"][0].T.reshape(KT, P, S).transpose(1, 0, 2), "w": w, "cols": c,
        "rows": np.broadcast_to(row, (P, NROW)), "wqkv": maps.transpose(2, 0, 1, 3),
        "wg": f["w_gates"][0].transpose(1, 0, 2).reshape(24, P, 16).transpose(1, 0, 2),
        "pool_w": f["pool_w"][0].reshape(4, 2, P, 2, P).transpose(2, 0, 1, 3, 4).reshape(P, 16, P),
        "cmp_w1k": w1[0].transpose(1, 0, 2), "cmp_w1v": w1[1].transpose(1, 0, 2),
        "cmp_w2": np.stack(w2).transpose(2, 0, 1, 3),
    }


def kernel(**inputs):
    import concourse.bacc as bacc
    from concourse.bass_utils import run_bass_kernel_spmd

    nc = bacc.Bacc("TRN2", target_bir_lowering=False, num_devices=1)
    arrays = {**_constants(), **_layout(inputs)}
    arrays = {f"in_{n}": np.ascontiguousarray(v) for n, v in arrays.items()}
    aps = {n[3:]: nc.dram_tensor(n, v.shape, mybir.dt.from_np(v.dtype), kind="ExternalInput").ap() for n, v in arrays.items()}
    aps["out"] = nc.dram_tensor("out", (P, KT, S), F32, kind="ExternalOutput").ap()
    build(nc, aps)
    r = run_bass_kernel_spmd(nc, [arrays], core_ids=[0])
    got = r.results[0]["out"]
    return np.ascontiguousarray(got.transpose(2, 1, 0).reshape(1, S, D))
```

```python
from contextlib import ExitStack

import numpy as np

import concourse.bass as bass
from concourse import mybir

F32 = mybir.dt.float32
F32R = mybir.dt.float32r
BF16 = mybir.dt.bfloat16
ALU = mybir.AluOpType
ACT = mybir.ActivationFunctionType
AX = mybir.AxisListType

P = 128
S = 512
NT = S // P
D = 1024
KT = D // P
EPS = 1e-6

HEADS = 4
HD = 256
WINDOWS = (2, 4, 8, 16)
TAPS = 5
UPAD = 2
US = S + 2 * UPAD

HQ = 16
DH = 64
NG = 4
CMP = 31
CP = 32
CLEN = 32
FF = 2816
FT = FF // P
FTAPS = 3

RAW = 4
SPL = 2

STAGES = [("in", 32), ("wo_pool", 8), ("wo_m", 8), ("nsa", 21), ("nsa_o", 8), ("gu0", 2 * FT),
          ("down0", FT), ("swa", 10), ("swa_o", 8), ("gu1", 2 * FT), ("down1", FT)]
W0, T0, _w, _t = {}, {}, 0, 0
for _name, _n in STAGES:
    W0[_name], T0[_name] = _w, _t
    _w += _n
    _t += 0 if _name.startswith("down") else _n
NW = _w

XST = [("in", 8), ("wo_pool", 8), ("wo_m", 8), ("nsa", 8), ("nsa_o", 8), ("gu0", 8), ("down0", FT),
       ("swa", 8), ("swa_o", 8), ("gu1", 8), ("down1", FT)]
X0, _x = {}, 0
for _name, _n in XST:
    X0[_name] = _x
    _x += _n

COLS, _c = {}, 0
for _name, _n in [("g_in", 8), ("g_out", 8), ("pool_scale", 8), ("conv_w", 40), ("conv_b", 8), ("mh", 8),
                  ("skip", 8), ("b_gates", 1), ("g_mix0", 8), ("g_mix1", 8), ("g_ffn0", 8), ("g_ffn1", 8),
                  ("g_fin", 8), ("b_q", 8), ("b_k", 1), ("b_v", 1), ("b_o", 8), ("fcw0", 3 * FT), ("fcw1", 3 * FT),
                  ("fcb0", FT), ("fcb1", FT), ("pe_k", 32), ("pe_v", 32)]:
    COLS[_name] = _c
    _c += _n
NCOL = _c

NROW = 64

POOL_TILES = [(2, 3), (4, 5), (6,), (7,)]

NSA_UNITS = [(c, 1 if i >= 2 else 2, m, i) for i in range(NT) for c in range(0, 8, 1 if i >= 2 else 2) for m in range(2)]
SWA_UNITS = [(c, 2, 0, i) for i in range(NT) for c in range(0, 8, 2)]


def key_tiles(i, swa):
    return range(max(i - 1, 0), i + 1) if swa else range(i + 1)


class Steps:

    def __init__(self, eng, sem):
        self.eng, self.sem, self.n, self.off = eng, sem, 0, 0

    def mark(self, ins):
        ins.then_inc(self.sem, 1)
        self.n += 1
        return self.n

    def wait(self, n=None):
        self.eng.wait_ge(self.sem, self.off + (self.n if n is None else n))


def build(nc, a):
    with ExitStack() as ctx:
        def sb(name, shape, dt=F32):
            return ctx.enter_context(nc.sbuf_tensor("sb_" + name, shape, dt))

        def sem(name):
            return ctx.enter_context(nc.semaphore(name))

        R = sb("resid", [P, KT, S])
        XH = sb("x_hi", [P, KT, S], F32R)
        XL = sb("x_lo", [P, KT, S], F32R)
        raw = sb("raw", [P, RAW, KT, P])
        WH = sb("w_hi", [P, SPL, KT, P], F32R)
        WL = sb("w_lo", [P, SPL, KT, P], F32R)
        cols = sb("cols", [P, NCOL])
        rows = sb("rows", [P, NROW])
        ident = sb("ident", [P, P])
        ones = sb("ones", [P, P])
        identb = sb("identb", [P, P], BF16)
        masks = sb("masks", [P, 3, P], BF16)
        cmask = sb("cmask", [P, NT, P], BF16)
        rstd = sb("rstd", [P, S])
        small = sb("small", [P, 160])
        PS = ctx.enter_context(nc.psum_tensor("ps", [P, 8, S], F32))
        NA = 30712
        arena = sb("arena", [P, NA])

        def col(name, k=0):
            return cols[:, COLS[name] + k:COLS[name] + k + 1]

        def carve(at, *shape):
            n = int(np.prod(shape))
            v = arena[:, at:at + n]
            if len(shape) == 2:
                v = v.rearrange("p (a b) -> p a b", b=shape[1])
            if len(shape) == 3:
                v = v.rearrange("p (a b c) -> p a b c", b=shape[1], c=shape[2])
            if len(shape) == 4:
                v = v.rearrange("p (a b c d) -> p a b c d", b=shape[1], c=shape[2], d=shape[3])
            return v

        o_u, o_mz, o_c, o_q, o_k, o_v = 0, 4128, 8224, 12320, 16416, 20512
        o_b = o_v + NT * HEADS * 257
        o_nm = o_b + 4608
        U = carve(o_u, KT, US)
        H = carve(o_u, NT, 1024)
        MZ = carve(o_mz, KT, S)
        px = [carve(o_mz + 544 * i, 544) for i in range(3)]
        C = carve(o_c, KT, S)
        Q1, K1 = carve(o_q, KT, S), carve(o_k, KT, S)
        pooled, SZ = Q1, K1
        V1 = carve(o_v, NT, HEADS, 257)
        poolw = carve(o_v, 16, P)
        invc = carve(o_v + 2048, 4, S)
        BD = [carve(o_b + 1024 * i, KT, 32, 4) for i in range(3)]
        wgm = carve(o_b + 3072, 24, 16)
        PW = [carve(o_b, 1280), carve(o_b + 1280, 1280)]
        WD = carve(o_b + 2560, 2, NT, P)
        WE = carve(o_b + 3584, 2, S)
        NM = carve(o_nm, S)
        ACOL = carve(o_nm + S, 8, DH)
        wqkv = carve(o_b + 4480 - 32, 3, KT, 4)
        bdm = carve(o_b + 4544, 32)
        place_w = carve(o_nm, P)
        wg = carve(o_q + 896, 96, 16)
        masks32, cmask32 = carve(o_q, 3, P), carve(o_q + 384, NT, P)
        G16 = carve(o_u, S)
        gr = [carve(o_u + S * (i + 1), S) for i in range(6)]
        one5 = carve(o_u + S * 7, S)
        SQ, RMS = carve(0, 2, S), carve(1024, S)

        o = 1536
        cs, sn = carve(o, S), carve(o + 512, S)
        csr, snr = carve(o + 1024, S), carve(o + 1536, S)
        QN = carve(o + 2048, KT, S)
        KC, VC = carve(o + 6144, 2, S), carve(o + 7168, 2, S)
        KS, KW = carve(o + 8192, 2, S), carve(o + 9216, 2, S)
        VS, VW = carve(o + 10240, NT, NG, 65), carve(o + 11280, NT, NG, 65)
        VN = 96
        v_rows = [arena[:, o + 10240 + 1040 * m:o + 10240 + 1040 * (m + 1) + VN - 65] for m in range(2)]
        v_pad = arena[:, o + 12320:o + 12352]
        o1 = o + 12352
        CW1 = [carve(o1 + 4096 * i, 16, 2 * P) for i in range(2)]
        OA = carve(o1, NT, 8, 2, DH)
        XB = [carve(o1 + 8192 + 2048 * i, 16, NG, CP) for i in range(2)]
        PE_ = carve(o1 + 8192, 2, 2, S)
        PT_ = carve(o1 + 10240, 2, 2, S)
        o2 = o1 + 12288
        CW2 = carve(o2, 2, 2, P)
        HID = [carve(o2 + 512 + 256 * i, 2, NG, CP) for i in range(2)]
        HIDR = carve(o2 + 1024, NG, 2, 2 * CP)
        BDK = carve(o2 + 1536, 2, P)
        BDV = carve(o2 + 1792, 2, 4, DH)
        RS1 = carve(o2 + 2304, S)
        TS, TM = carve(o2 + 3200, S), carve(o2 + 3712, S)
        GT = carve(o2 + 4224, NT, 48)
        SX = [carve(o1 + 8192 + 512 * i, HQ, CP) for i in range(2)]
        PTC = [carve(o1 + 10240 + 512 * i, 4, P) for i in range(2)]
        assert o2 + 4416 <= NA
        MID = carve(o, FT, S)
        AP_ = carve(o + 11264, 2, S + 2)
        CV = carve(o + 12292, 2, S)
        SA = carve(o + 13316, 2, S)
        TU = carve(o + 14340, 2, S)

        TB = KW
        four = lambda at: small[:, at:at + 16].rearrange("p (v h r) -> p v h r", h=2, r=2)
        nmx, nmr, rec = four(122), four(138), four(4)
        esk, ske = four(60), four(76)
        nsk = small[:, 44:60]
        cst = small[:, 60:108].rearrange("p (a b) -> p a b", b=16)
        bn6 = small[:, 108:114]
        eps, warm = small[:, 120:121], small[:, 121:122]
        zero = sb("zero", [P, KT])[:, :]
        mv = sb("mv", [P, 16, 2])
        rv = sb("rv", [P, 16])
        mb = small[:, 92:108]
        dn = sb("dn", [P, 4])

        consts_in = sem("consts_in")
        x_in = [sem(f"x_in{k}") for k in range(KT)]
        cols_in = sem("cols_in")
        raw_in = [sem(f"raw_in{i}") for i in range(RAW)]
        zero_set = sem("zero_set")
        hi_made = sem("hi_made")
        tile_split = sem("tile_split")
        tile_used = sem("tile_used")
        freed = sem("freed")
        xh_ready, xl_ready = sem("xh_ready"), sem("xl_ready")
        sq_ready, sq_acc, sq_sum, std_ready = sem("sq_ready"), sem("sq_acc"), sem("sq_sum"), sem("std_ready")
        gains_ready, ms_ready = sem("gains_ready"), sem("ms_ready")
        rstd_ready = sem("rstd_ready")
        dve_step = sem("dve_step")
        act_step = sem("act_step")
        normed = sem("normed")
        down_added = sem("down_added")
        bd_ready = sem("bd_ready")
        pool_in = sem("pool_in")
        conv_ready, c_ready, mz_raw, mz_ready = sem("conv_ready"), sem("c_ready"), sem("mz_raw"), sem("mz_ready")
        pooled_ready, sz_ready, pool_mm, yp_ready = sem("pooled_ready"), sem("sz_ready"), sem("pool_mm"), sem("yp_ready")
        q_mm, q_out, vt_mm, vt_out, gate_mm, g16 = (sem(x) for x in ("q_mm", "q_out", "vt_mm", "vt_out", "gate_mm", "g16"))
        g_placed, f_rest, nm_ready, fm_ready, emt_ready, cols_mm, acol_ready = (
            sem(x) for x in ("g_placed", "f_rest", "nm_ready", "fm_ready", "emt_ready", "cols_mm", "acol_ready"))
        a_ready = sem("a_ready")
        m_bc, s_mm1, wd_ready, w_exp, p_ready, num_mm, num_out = (
            sem(x) for x in ("m_bc", "s_mm1", "wd_ready", "w_exp", "p_ready", "num_mm", "num_out"))
        var_ready, hstd, inv_ready, xhat, xhat_last, yt_mm, skip_ready, yc_ready, ym_ready = (
            sem(x) for x in ("var_ready", "hstd", "inv_ready", "xhat", "xhat_last", "yt_mm", "skip_ready", "yc_ready",
                             "ym_ready"))
        rope_in, kv_ready = sem("rope_in"), sem("kv_ready")
        tok_t, tok_out = sem("tok_t"), sem("tok_out")
        gt_raw, gt_ready = sem("gt_raw"), sem("gt_ready")
        xb_ready, hid_mm, hid_ready, cmp_mm, cmp_ready = (
            sem(x) for x in ("xb_ready", "hid_mm", "hid_ready", "cmp_mm", "cmp_ready"))
        cs_mm, cs_arg, cs_exp, cs_norm, cs_t, cs_tout, cs_o, cs_out = (
            sem(x) for x in ("cs_mm", "cs_arg", "cs_exp", "cs_norm", "cs_t", "cs_tout", "cs_o", "cs_out"))
        s_mm, nmax, p_exp, pt_mm, pt_d, pt_a, o_mm, o_done = (
            sem(x) for x in ("s_mm", "nmax", "p_exp", "pt_mm", "pt_d", "pt_a", "o_mm", "o_done"))
        oa_mm = sem("oa_mm")
        qb_raw, qb_ready = sem("qb_raw"), sem("qb_ready")
        ff_conv, ff_silu, mid_ready, down_mm = sem("ff_conv"), sem("ff_silu"), sem("mid_ready"), sem("down_mm")
        out_ready, out_done = sem("out_ready"), sem("out_done")

        block = ctx.enter_context(nc.Block())

        def psum(bank, n=S):
            return PS[:, bank, 0:n]

        def xst(name):
            return X0[name]

        @block.sync
        def _(sp):
            def load(it, s, first=False):
                if not first:
                    sp.wait_ge(tile_split, 4 * it + (s - RAW + 1))
                sp.dma_start(raw[:, s], a["w"][bass.ds(4 * it + s, 1)].rearrange("o p k m -> (o p) k m")
                             ).then_inc(raw_in[s], 16)

            for s in range(RAW):
                load(0, s, first=True)
                if s == 0:
                    for k in range(KT):
                        sp.dma_start(R[:, k, :], a["x"][:, k, :]).then_inc(x_in[k], 16)
            with sp.Fori(1, NW // RAW) as it:
                for s in range(RAW):
                    load(it, s)
            for s in range(NW % RAW):
                load(NW // RAW, s)
            for k in range(KT):
                sp.wait_ge(normed, KT + k + 1)
                sp.dma_start(a["out"][:, k, :], R[:, k, :]).then_inc(out_done, 16)
            sp.wait_ge(out_done, 16 * KT)

        @block.gpsimd
        def _(pool):
            def split(it, s, first=False):
                pool.wait_ge(raw_in[s], 16 * (it + 1))
                if not first:
                    pool.wait_ge(tile_used, 4 * it + (s - SPL + 1))
                nc.gpsimd.tensor_tensor(WH[:, s % SPL], raw[:, s], zero.unsqueeze(2).broadcast_to([P, KT, P]), ALU.add
                                        ).then_inc(hi_made, 1)
                pool.wait_ge(hi_made, 4 * it + (s + 1))
                nc.gpsimd.tensor_tensor(WL[:, s % SPL], raw[:, s], WH[:, s % SPL].bitcast(F32),
                                        ALU.subtract).then_inc(tile_split, 1)

            nc.gpsimd.memset(zero, 0.0).then_inc(zero_set, 1)
            nc.gpsimd.memset(ones[:], 1.0).then_inc(zero_set, 1)
            nc.gpsimd.memset(eps, EPS).then_inc(zero_set, 1)
            pool.wait_ge(zero_set, 3)
            for s in range(RAW):
                split(0, s, first=s < SPL)
            n = W0["wo_m"] // RAW
            assert W0["wo_m"] % RAW == 0
            with pool.Fori(1, n) as it:
                for s in range(RAW):
                    split(it, s)
            for s in range(RAW):
                split(n, s)
                if s == 1:
                    for j in range(KT):
                        pool.wait_ge(yc_ready, j + 1)
                        pool.wait_ge(mz_ready, j + 1)
                        nc.gpsimd.tensor_tensor(MZ[:, j], C[:, j], MZ[:, j], ALU.mult).then_inc(ym_ready, 1)
            with pool.Fori(n + 1, NW // RAW) as it:
                for s in range(RAW):
                    split(it, s)
            for s in range(NW % RAW):
                split(NW // RAW, s)

        @block.scalar
        def _(act):
            step = Steps(act, act_step)
            act.dma_start(cols[:], a["cols"]).then_inc(cols_in, 16)

            def constants():
                for dst, name in ((wqkv, "wqkv"), (bdm, "bdm"), (poolw, "pool_w"),
                                  (invc, "invc"), (wg, "wg"), (ident[:], "ident"), (rows[:], "rows"),
                                  (masks32, "masks"), (cmask32, "cmask"),
                                  (place_w[0:16], "place")):
                    act.dma_start(dst, a[name]).then_inc(consts_in, 16)

            def square(q, k, ready=None):
                if ready:
                    act.wait_ge(*ready(k))
                if k == 0 and q:
                    act.wait_ge(rstd_ready, q)
                if k >= 3:
                    act.wait_ge(sq_acc, 7 * q + k - 2)
                nc.scalar.activation(SQ[:, k % 2] if k else RMS, R[:, k], ACT.Square).then_inc(sq_ready, 1)

            def times_gain(ready, gain, used=0):
                if used:
                    act.wait_ge(tile_used, used)
                for k in range(KT):
                    act.wait_ge(*ready(k))
                    nc.scalar.mul(XH[:, k], R[:, k], col(gain, k)).then_inc(xh_ready, 1)

            def root(q):
                nc.scalar.activation(warm, eps, ACT.Sqrt)
                act.wait_ge(sq_sum, q + 1)
                nc.scalar.activation(RMS, psum(7), ACT.Sqrt, scale=1.0 / D, bias=eps).then_inc(std_ready, 1)

            act.wait_ge(cols_in, 16)
            times_gain(lambda k: (x_in[k], 16), "g_in")
            for k in range(KT):
                square(0, k)
            act.wait_ge(zero_set, 3)
            root(0)
            constants()
            for j in range(KT):
                act.wait_ge(conv_ready, j + 1)
                nc.scalar.activation(C[:, j], C[:, j], ACT.Silu).then_inc(c_ready, 1)
            for j in range(KT):
                act.wait_ge(freed, 16 + j + 1)
                nc.scalar.activation(SZ[:, j], SZ[:, j], ACT.Silu).then_inc(sz_ready, 1)
            for j in range(KT):
                act.wait_ge(freed, 24 + j + 1)
                nc.scalar.activation(MZ[:, j], MZ[:, j], ACT.Silu).then_inc(mz_ready, 1)
            act.wait_ge(tile_used, W0["wo_pool"])
            for k in range(KT):
                act.wait_ge(yp_ready, k + 1)
                nc.scalar.copy(XH[:, k], SZ[:, k]).then_inc(xh_ready, 1)
            act.wait_ge(xl_ready, X0["wo_pool"] + KT)
            for j in range(KT):
                act.wait_ge(q_mm, 2 * j + 1)
                nc.scalar.copy(Q1[:, j], psum(2)).then_inc(q_out, 1)
                act.wait_ge(q_mm, 2 * j + 2)
                nc.scalar.copy(K1[:, j], psum(3)).then_inc(q_out, 1)
            act.wait_ge(gate_mm, 1)
            nc.scalar.activation(G16[0:16], PS[0:16, 7, :], ACT.Identity, bias=cols[0:16, COLS["b_gates"]:COLS["b_gates"] + 1]
                                 ).then_inc(g16, 1)
            act.wait_ge(g_placed, 1)
            t = gr[1]
            step.mark(nc.scalar.activation(t[64:128], PS[64:128, 6, :], ACT.Abs))
            step.wait()
            step.mark(nc.scalar.activation(t[64:128], t[64:128], ACT.Exp, scale=-1.0))
            step.wait()
            nc.scalar.activation(t[64:128], t[64:128], ACT.Ln, bias=1.0).then_inc(f_rest, 1)
            act.wait_ge(fm_ready, 1)
            nc.scalar.activation(gr[5][0:64], gr[4][0:64], ACT.Exp, scale=-1.0).then_inc(emt_ready, 1)
            act.wait_ge(acol_ready, 1)
            for h in range(HEADS):
                act.wait_ge(wd_ready, 2 * (h + 1))
                for j in range(NT):
                    for d in range(2):
                        n = 8 * h + 2 * j + d
                        if n >= 2:
                            act.wait_ge(p_ready, n - 1)
                        bias = ACOL[:, j, 32 * d + h:32 * d + h + 1]
                        w = WE[:, n % 2]
                        dg, rest = (0, P) if d == 0 else (P * j, 0)
                        others = (P * (j + 1), S) if d == 0 else (0, P * j)
                        if others[1] > others[0]:
                            nc.scalar.activation(w[:, rest:rest + others[1] - others[0]],
                                                 PS[:, 6 + d, others[0]:others[1]], ACT.Exp, bias=bias)
                        nc.scalar.activation(w[:, dg:dg + P], WD[:, d, j], ACT.Exp, bias=bias).then_inc(w_exp, 1)
            for j in range(KT):
                nc.scalar.mul(C[:, j], C[:, j], col("skip", j)).then_inc(skip_ready, 1)
            act.wait_ge(var_ready, 1)
            nc.scalar.activation(rv[:, 0:12], rv[:, 0:12], ACT.Sqrt).then_inc(hstd, 1)
            act.wait_ge(inv_ready, 1)
            for n in range(12):
                hh = H[:, n % NT, HD * (n // NT):HD * (n // NT + 1)]
                nc.scalar.activation(hh, hh, ACT.Identity, scale=rv[:, n:n + 1], bias=mb[:, n:n + 1]).then_inc(xhat, 1)
            act.wait_ge(var_ready, 2)
            nc.scalar.activation(rv[:, 12:16], rv[:, 12:16], ACT.Sqrt).then_inc(hstd, 1)
            act.wait_ge(tile_used, W0["wo_m"])
            for k in range(KT):
                act.wait_ge(ym_ready, k + 1)
                nc.scalar.copy(XH[:, k], MZ[:, k]).then_inc(xh_ready, 1)
            act.wait_ge(xl_ready, X0["wo_m"] + KT)
            for dst, name in ((cs, "cos"), (sn, "sin"), (CW1[0], "cmp_w1k"), (CW1[1], "cmp_w1v"), (CW2, "cmp_w2")):
                act.dma_start(dst, a[name]).then_inc(consts_in, 16)
            act.wait_ge(rstd_ready, 1)
            act.wait_ge(gains_ready, 1)

            def two_squares(k):
                act.wait_ge(freed, T0["wo_m"] + k + 1)
                if k >= 2:
                    act.wait_ge(sq_acc, 7 + 2 * (k - 1))
                nc.scalar.activation(SQ[:, 0] if k else RMS, R[:, k], ACT.Square).then_inc(sq_ready, 1)
                nc.scalar.activation(SQ[:, 1] if k else rstd[:], R[:, k], ACT.Square, scale=col("g_out", k)
                                     ).then_inc(sq_ready, 1)

            for k in range(KT - 1):
                two_squares(k)
            times_gain(lambda k: (freed, T0["wo_m"] + k + 1), "g_mix0", W0["nsa"])
            two_squares(KT - 1)
            nc.scalar.activation(warm, eps, ACT.Sqrt)
            act.wait_ge(ms_ready, 1)
            nc.scalar.activation(RMS, RMS, ACT.Sqrt).then_inc(std_ready, 1)
            act.wait_ge(rstd_ready, 2)
            nc.scalar.activation(RMS, psum(7), ACT.Sqrt, scale=1.0 / D, bias=eps).then_inc(std_ready, 1)
            for kv in range(2):
                act.wait_ge(hid_mm, kv + 1)
                nc.scalar.activation(HID[kv], PS[:, 2 + kv, 0:2 * P].rearrange("p (a b c) -> p a b c", a=2, b=NG),
                                     ACT.Gelu_apprx_tanh).then_inc(hid_ready, 1)
            act.wait_ge(gt_raw, 1)
            nc.scalar.activation(GT, GT, ACT.Sigmoid).then_inc(gt_ready, 1)

            def c_exp(i):
                act.wait_ge(cs_arg, i + 1)
                nc.scalar.activation(SX[i % 2], SX[i % 2], ACT.Exp).then_inc(cs_exp, 1)

            def c_tout(i):
                act.wait_ge(cs_t, i + 1)
                if i >= 2:
                    act.wait_ge(cs_o, 2 * (i - 1))
                nc.scalar.copy(PTC[i % 2], psum(6).rearrange("p (g t) -> p g t", g=NG)).then_inc(cs_tout, 1)

            def c_out(i):
                for gp in range(2):
                    act.wait_ge(cs_o, 2 * i + gp + 1)
                    nc.scalar.copy(OA[:, i, 4 * gp:4 * gp + 4].rearrange("p c a d -> p (c a d)"), psum(4 + gp)
                                   ).then_inc(cs_out, 1)

            def values_out(n):
                act.wait_ge(tok_t, n + 2)
                g = 2 * (n % 2)
                nc.scalar.copy((VS, VW)[n // 2][:, :, g:g + 2, 0:DH], psum(7).rearrange("p (t g d) -> p t g d", t=NT, d=DH)
                               ).then_inc(tok_out, 1)

            c_exp(0)
            values_out(0)
            c_exp(1)
            c_tout(0)
            values_out(1)
            c_out(0)
            c_tout(1)
            c_exp(2)
            values_out(2)
            c_out(1)
            c_tout(2)
            c_exp(3)
            values_out(3)
            c_out(2)
            c_tout(3)
            c_out(3)

            def attention(units, v0, swa):
                def exps(v):
                    c, pairs, m, i = units[v - v0]
                    n = P * len(key_tiles(i, swa))
                    act.wait_ge(nmax, v + 1)
                    if v >= 2:
                        act.wait_ge(pt_mm, v - 1)
                    if swa:
                        act.wait_ge(qb_raw, v - v0 + 1)
                        nc.scalar.activation(esk[:, v % 4], ske[:, v % 4], ACT.Exp)
                    for hh in range(2):
                        for r in range(pairs):
                            ins = nc.scalar.activation(PE_[:, v % 2, hh, n * r:n * (r + 1)],
                                                       PS[:, 2 + 2 * (v % 2) + hh, n * r:n * (r + 1)], ACT.Exp,
                                                       bias=nmr[:, v % 4, hh, r:r + 1])
                    ins.then_inc(p_exp, 1)

                def evac(v):
                    c, pairs, m, i = units[v - v0]
                    n = P * pairs * len(key_tiles(i, swa))
                    act.wait_ge(pt_mm, v + 1)
                    if v >= 2:
                        act.wait_ge(o_mm, v - 1)
                    nc.scalar.copy(PT_[:, v % 2, 1, 0:n], psum(7, n)).then_inc(pt_a, 1)

                last = v0 + len(units)
                exps(v0)
                for v in range(v0, last):
                    if v + 1 < last:
                        exps(v + 1)
                    evac(v)

            def attention_out(stage, n0):
                act.wait_ge(tile_used, W0[stage])
                for c in range(KT):
                    act.wait_ge(oa_mm, n0 + c + 1)
                    nc.scalar.copy(XH[:, c], psum(2 + c % 6)).then_inc(xh_ready, 1)

            def ffn(layer):
                with act.Fori(0, FT // 2) as it:
                    for b in range(2):
                        act.wait_ge(ff_conv, layer * FT + 2 * it + (b + 1))
                        nc.scalar.activation(SA[:, b], CV[:, b], ACT.Silu).then_inc(ff_silu, 1)
                x0, w0, wd = X0[f"down{layer}"], W0[f"gu{layer}"], W0[f"down{layer}"]
                for f in range(FT):
                    if f < 4:
                        act.wait_ge(tile_used, wd)
                    else:
                        act.wait_ge(tile_used, wd + f - 3)
                    act.wait_ge(mid_ready, layer * FT + f + 1)
                    nc.scalar.copy(XH[:, f % 4], MID[:, f]).then_inc(xh_ready, 1)

            attention(NSA_UNITS, 0, False)
            attention_out("nsa_o", 0)
            done = lambda k: (freed, T0["nsa_o"] + k + 1)
            for k in range(KT - 1):
                square(3, k, done)
            times_gain(done, "g_ffn0", W0["gu0"])
            square(3, KT - 1)
            root(3)
            ffn(0)
            act.wait_ge(mid_ready, FT)
            act.wait_ge(tile_used, W0["swa"])
            for dst, name in ((cs, "cos"), (sn, "sin")):
                act.dma_start(dst, a[name]).then_inc(consts_in, 16)
            times_gain(lambda k: (down_added, k + 1), "g_mix1", W0["swa"])
            for k in range(KT):
                square(4, k)
            root(4)
            for j in range(10):
                act.wait_ge(freed, T0["swa"] + j + 1)
                b = TB[:, j % 2]
                bias = col("b_k") if j == 0 else col("b_q", j - 1) if j < 9 else col("b_v")
                nc.scalar.activation(b, b, ACT.Identity, bias=bias).then_inc(qb_ready, 1)
            act.wait_ge(tok_t, 6)
            nc.scalar.copy(VS[:, :, 0:2, 0:DH], psum(7).rearrange("p (t g d) -> p t g d", t=NT, d=DH)).then_inc(tok_out, 1)
            attention(SWA_UNITS, len(NSA_UNITS), True)
            attention_out("swa_o", KT)
            done = lambda k: (freed, T0["swa_o"] + k + 1)
            for k in range(KT - 1):
                square(5, k, done)
            times_gain(done, "g_ffn1", W0["gu1"])
            square(5, KT - 1)
            root(5)
            ffn(1)
            for k in range(KT):
                square(6, k, lambda k: (down_added, KT + k + 1))
            root(6)

        @block.vector
        def _(dve):
            step = Steps(dve, dve_step)

            def split_rest(x, gain):
                for k in range(KT):
                    dve.wait_ge(xh_ready, X0[x] + k + 1)
                    nc.vector.scalar_tensor_tensor(XL[:, k], R[:, k], col(gain, k), XH[:, k].bitcast(F32),
                                                   ALU.mult, ALU.subtract).then_inc(xl_ready, 1)

            def add_square(q, k):
                dve.wait_ge(sq_ready, 8 * q + k + 1)
                if 7 * q + k > 1:
                    dve.wait_ge(sq_acc, 7 * q + k - 1)
                nc.vector.tensor_tensor(RMS, RMS, SQ[:, k % 2], ALU.add).then_inc(sq_acc, 1)

            def add_two_squares(k):
                for n, total in enumerate((RMS, rstd[:])):
                    dve.wait_ge(sq_ready, 8 + 2 * k + n + 1)
                    dve.wait_ge(sq_acc, 7 + max(2 * (k - 2) + n + 1, 0))
                    nc.vector.tensor_tensor(total, total, SQ[:, n], ALU.add).then_inc(sq_acc, 1)

            def inverse(q, out):
                dve.wait_ge(std_ready, q + 1)
                nc.vector.reciprocal(out, RMS).then_inc(rstd_ready, 1)
                dve.wait_ge(rstd_ready, q + 1)

            def product(stage, j):
                dve.wait_ge(tile_used, W0[stage] + j + 1)
                return (T0[stage] + j) % 2

            def lo(stage, k, src):
                dve.wait_ge(xh_ready, X0[stage] + k + 1)
                nc.vector.tensor_tensor(XL[:, k], src, XH[:, k].bitcast(F32), ALU.subtract).then_inc(xl_ready, 1)

            def add_residual(stage, bias=None, tiles=range(KT), behind=None):
                for k in tiles:
                    b = product(stage, k)
                    if bias:
                        ins = nc.vector.scalar_tensor_tensor(R[:, k], psum(b), col(bias, k), R[:, k], ALU.add, ALU.add)
                    else:
                        ins = nc.vector.tensor_tensor(R[:, k], psum(b), R[:, k], ALU.add)
                    ins.then_inc(freed, 1)
                    if behind and k >= 1:
                        behind(k - 1)

            def norm_tile(k, gain, by):
                nc.vector.scalar_tensor_tensor(R[:, k], R[:, k], col(gain, k), by, ALU.mult, ALU.mult).then_inc(normed, 1)

            dve.wait_ge(cols_in, 16)
            split_rest("in", "g_in")
            for k in range(1, KT):
                add_square(0, k)
            g2 = cols[:, COLS["g_mix0"]:COLS["g_mix0"] + KT]
            nc.vector.tensor_tensor(g2, g2, cols[:, COLS["g_out"]:COLS["g_out"] + KT], ALU.mult).then_inc(gains_ready, 1)
            inverse(0, rstd[:])
            step.mark(nc.vector.memset(U[:, :, 0:UPAD], 0.0))
            step.mark(nc.vector.memset(U[:, :, US - UPAD:US], 0.0))
            step.wait()

            def set_up(j):
                if j == 1:
                    dve.wait_ge(consts_in, 16 * 10)
                if 1 <= j <= 3:
                    nc.vector.tensor_tensor(
                        BD[j - 1], wqkv[:, j - 1].unsqueeze(2).broadcast_to([P, KT, 32, 4]),
                        bdm.unsqueeze(1).unsqueeze(3).broadcast_to([P, KT, 32, 4]), ALU.mult).then_inc(bd_ready, 1)
                if j == 6:
                    step.mark(nc.vector.tensor_tensor(wg, wg, wqkv.rearrange("p n k o -> p (n k o)").unsqueeze(2)
                                                      .broadcast_to([P, 96, 16]), ALU.mult))
                    step.wait()
                    step.mark(nc.vector.tensor_reduce(wgm, wg.rearrange("p (x o) g -> p x g o", o=4), AX.X, ALU.add))
                    step.wait()
                    nc.vector.tensor_tensor(wgm[:, 0:8], wgm[:, 0:8], wgm[:, 8:16], ALU.add).then_inc(bd_ready, 1)
                if j == 4:
                    for dst, src in ((identb[:], ident[:]), (masks[:], masks32), (cmask[:], cmask32)):
                        step.mark(nc.vector.tensor_copy(dst, src))
                if j == 5:
                    for p in px:
                        step.mark(nc.vector.memset(p, 0.0))

            for j in range(KT):
                b = product("in", j)
                nc.vector.tensor_tensor(U[:, j, UPAD:UPAD + S], psum(b), rstd[:], ALU.mult).then_inc(freed, 1)
                dve.wait_ge(freed, j + 1)
                step.mark(nc.vector.tensor_scalar(C[:, j], U[:, j, 0:S], col("conv_w", j), col("conv_b", j), ALU.mult, ALU.add))
                for t in range(1, TAPS):
                    step.wait()
                    ins = nc.vector.scalar_tensor_tensor(C[:, j], U[:, j, t:t + S], col("conv_w", 8 * t + j), C[:, j],
                                                         ALU.mult, ALU.add)
                    if t < TAPS - 1:
                        step.mark(ins)
                    else:
                        ins.then_inc(conv_ready, 1)
                set_up(j)
            for j in range(KT):
                w = WINDOWS[j // 2]
                left = (w - 1) // 2
                b = product("in", 8 + j)
                x, s0, s1 = px
                if j >= 1:
                    dve.wait_ge(pooled_ready, j)
                nc.vector.tensor_tensor(x[:, 8:8 + S], psum(b), rstd[:], ALU.mult).then_inc(freed, 1)
                dve.wait_ge(freed, 8 + j + 1)
                src, dst, width, sh = x, s0, 536, 1
                while sh < w:
                    width -= sh
                    step.mark(nc.vector.tensor_tensor(dst[:, 0:width], src[:, 0:width], src[:, sh:sh + width], ALU.add))
                    step.wait()
                    src, dst, sh = dst, (s1 if dst is s0 else s0), 2 * sh
                step.mark(nc.vector.tensor_tensor(dst[:, 0:S], src[:, 8 - left:8 - left + S], invc[:, j // 2], ALU.mult))
                step.wait()
                nc.vector.tensor_tensor(pooled[:, j], dst[:, 0:S], x[:, 8:8 + S], ALU.subtract).then_inc(pooled_ready, 1)
            for j in range(KT):
                b = product("in", 16 + j)
                nc.vector.tensor_tensor(SZ[:, j], psum(b), rstd[:], ALU.mult).then_inc(freed, 1)
            dve.wait_ge(pooled_ready, KT)
            for j in range(KT):
                b = product("in", 24 + j)
                nc.vector.tensor_tensor(MZ[:, j], psum(b), rstd[:], ALU.mult).then_inc(freed, 1)
            for j in range(KT):
                dve.wait_ge(pool_mm, j + 1)
                dve.wait_ge(sz_ready, j + 1)
                nc.vector.scalar_tensor_tensor(SZ[:, j], psum(2 + j % 2), col("pool_scale", j), SZ[:, j], ALU.mult, ALU.mult
                                               ).then_inc(yp_ready, 1)
            for k in range(KT):
                lo("wo_pool", k, SZ[:, k])
            nc.vector.memset(V1[:, :, :, 256:257], 1.0)
            for j in range(KT):
                dve.wait_ge(vt_mm, j + 1)
                nc.vector.tensor_copy(V1[:, :, j // 2, P * (j % 2):P * (j % 2) + P],
                                      psum(5).rearrange("p (t e) -> p t e", t=NT)).then_inc(vt_out, 1)
            lf, t, F, A, FM, EM = gr
            dve.wait_ge(g_placed, 1)
            step.mark(nc.vector.memset(one5, 1.0))
            dve.wait_ge(f_rest, 1)
            step.mark(nc.vector.scalar_tensor_tensor(lf[64:128], PS[64:128, 6, :], 0.0, t[64:128], ALU.min, ALU.subtract))
            step.wait()
            step.mark(nc.vector.tensor_tensor_scan(F[0:32], one5[64:96], lf[64:96], 0.0, ALU.mult, ALU.add))
            step.mark(nc.vector.tensor_tensor_scan(F[32:64, ::-1], one5[96:128, ::-1], lf[96:128, ::-1], 0.0, ALU.mult, ALU.add))
            step.wait()
            nc.vector.tensor_tensor(A[0:64], PS[0:64, 6, :], F[0:64], ALU.subtract).then_inc(a_ready, 1)
            dve.wait_ge(a_ready, 1)
            M = t
            step.mark(nc.vector.tensor_tensor_scan(M[0:32], one5[0:32], A[0:32], 0.0, ALU.mult, ALU.max))
            step.mark(nc.vector.tensor_tensor_scan(M[32:64, ::-1], one5[32:64, ::-1], A[32:64, ::-1], 0.0, ALU.mult, ALU.max))
            step.wait()
            nc.vector.tensor_scalar(NM[0:64], M[0:64], -1.0, None, ALU.mult).then_inc(nm_ready, 1)
            nc.vector.tensor_tensor(FM[0:64], F[0:64], M[0:64], ALU.add).then_inc(fm_ready, 1)
            add_residual("wo_pool", tiles=range(2))
            dve.wait_ge(cols_mm, 1)
            nc.vector.tensor_copy(ACOL, psum(7).rearrange("p (a b) -> p a b", b=64)).then_inc(acol_ready, 1)
            dve.wait_ge(acol_ready, 1)

            offs = [[0, 512, 896, 1152], [0, 128, 384, 768]]

            def weights(h):
                for d in range(2):
                    dve.wait_ge(m_bc, 2 * h + d + 1)
                    nc.vector.tensor_tensor(WD[:, d], psum(6 + d).rearrange("p (j t) -> p j t", j=NT),
                                            masks[:, d].unsqueeze(1).broadcast_to([P, NT, P]), ALU.add).then_inc(wd_ready, 1)
                if h >= 1:
                    dve.wait_ge(num_mm, 8 * h)
                for j in range(NT):
                    dve.wait_ge(s_mm1, NT * h + j + 1)
                    for d in range(2):
                        n = 8 * h + 2 * j + d
                        dve.wait_ge(w_exp, n + 1)
                        lo_, hi_ = (P * j, S) if d == 0 else (0, P * (j + 1))
                        nc.vector.scalar_tensor_tensor(PW[d][:, offs[d][j]:offs[d][j] + hi_ - lo_], PS[:, 2 + j, lo_:hi_],
                                                       float(HD) ** -0.5, WE[:, n % 2, 0:hi_ - lo_], ALU.mult, ALU.mult
                                                       ).then_inc(p_ready, 1)

            def head_out(h):
                for i in range(NT):
                    for d in range(2):
                        n = 8 * h + 2 * i + d
                        dve.wait_ge(num_mm, n + 1)
                        emt = ACOL[:, 4 + i, 32 * d + h:32 * d + h + 1]
                        b = n % 2
                        step.mark(nc.vector.tensor_scalar(dn[:, 0:1], PS[:, b, 256:257], -1.0, emt, ALU.mult, ALU.max))
                        step.wait()
                        step.mark(nc.vector.tensor_tensor(dn[:, 1:2], PS[:, b, 256:257], dn[:, 0:1], ALU.max))
                        step.wait()
                        step.mark(nc.vector.reciprocal(dn[:, 2:3], dn[:, 1:2]))
                        step.wait()
                        out = H[:, i, HD * h:HD * (h + 1)]
                        if d == 0:
                            nc.vector.tensor_scalar(out, PS[:, b, 0:HD], dn[:, 2:3], None, ALU.mult).then_inc(num_out, 1)
                        else:
                            nc.vector.scalar_tensor_tensor(out, PS[:, b, 0:HD], dn[:, 2:3], out, ALU.mult, ALU.add
                                                           ).then_inc(num_out, 1)
                        dve.wait_ge(num_out, n + 1)
                    step.mark(nc.vector.bn_stats(bn6, H[:, i, HD * h:HD * (h + 1)]))
                    step.wait()
                    step.mark(nc.vector.bn_aggr(mv[:, 4 * h + i], bn6))
                    step.wait()

            def variance(h0, h1):
                nc.vector.tensor_scalar(rv[:, NT * h0:NT * h1], mv[:, NT * h0:NT * h1, 1], EPS, None, ALU.add
                                        ).then_inc(var_ready, 1)

            weights(0)
            for h in range(HEADS):
                add_residual("wo_pool", tiles=POOL_TILES[h])
                if h == HEADS - 1:
                    dve.wait_ge(hstd, 1)
                    step.mark(nc.vector.reciprocal(rv[:, 0:12], rv[:, 0:12]))
                    step.wait()
                    nc.vector.scalar_tensor_tensor(mb[:, 0:12], mv[:, 0:12, 0], -1.0, rv[:, 0:12], ALU.mult, ALU.mult
                                                   ).then_inc(inv_ready, 1)
                head_out(h)
                if h == HEADS - 2:
                    variance(0, HEADS - 1)
                if h + 1 < HEADS:
                    weights(h + 1)
            variance(HEADS - 1, HEADS)

            def add_skip(j):
                dve.wait_ge(yt_mm, j + 1)
                dve.wait_ge(skip_ready, j + 1)
                nc.vector.scalar_tensor_tensor(C[:, j], psum(2 + j % 6), col("mh", j), C[:, j], ALU.mult, ALU.add
                                               ).then_inc(yc_ready, 1)

            add_skip(0)
            dve.wait_ge(hstd, 2)
            step.mark(nc.vector.reciprocal(rv[:, 12:16], rv[:, 12:16]))
            step.wait()
            for n in range(12, 16):
                hh = H[:, n % NT, HD * (n // NT):HD * (n // NT + 1)]
                nc.vector.tensor_scalar(hh, hh, mv[:, n, 0:1], rv[:, n:n + 1], ALU.subtract, ALU.mult).then_inc(xhat_last, 1)
            add_skip(1)
            for j in range(2, KT):
                add_skip(j)
                lo("wo_m", j - 2, MZ[:, j - 2])
            for k in range(KT - 2, KT):
                lo("wo_m", k, MZ[:, k])

            def behind_wo_m(k):
                if k >= 1:
                    add_two_squares(k)
                if k == 1:
                    for kv in range(2):
                        step.mark(nc.vector.memset(XB[kv], 0.0))
                if k == 2:
                    step.mark(nc.vector.memset(BDV, 0.0))
                    step.mark(nc.vector.memset(VS[:, :, :, DH:DH + 1], 1.0))
                    step.mark(nc.vector.memset(VW[:, :, :, DH:DH + 1], 1.0))
                    step.mark(nc.vector.memset(v_pad, 0.0))
                    step.mark(nc.vector.memset(BDK, 0.0))

            add_residual("wo_m", behind=behind_wo_m)
            dve.wait_ge(gains_ready, 1)
            split_rest("nsa", "g_mix0")
            add_two_squares(KT - 1)
            dve.wait_ge(sq_sum, 3)
            step.mark(nc.vector.tensor_scalar(RMS, psum(7), EPS / D, EPS * EPS, ALU.mult, ALU.add))
            step.wait()
            nc.vector.scalar_tensor_tensor(RMS, psum(6), 1.0 / D, RMS, ALU.mult, ALU.add).then_inc(ms_ready, 1)
            inverse(1, rstd[:])

            dve.wait_ge(consts_in, 16 * 15)
            rotary_tables = [(csr, cs), (snr, sn)]
            for dst, src in rotary_tables:
                step.mark(nc.vector.tensor_tensor(dst, src, rstd[:], ALU.mult))
            step.wait()
            dve.wait_ge(xl_ready, X0["nsa"] + KT)

            swap = [p ^ 16 for p in range(32)]
            ropes = [0]

            def rotary(src, c_, s_, out, scale, signal, first=None):
                if ropes[0]:
                    dve.wait_ge(rope_in, ropes[0])
                ropes[0] += 1
                step.mark(nc.vector.stream_shuffle(TS, src, swap))
                ins = nc.vector.scalar_tensor_tensor(TM, src, scale, c_, ALU.mult, ALU.mult)
                if signal is not None:
                    ins.then_inc(signal, 1)
                else:
                    step.mark(ins)
                step.wait()
                step.mark(nc.vector.scalar_tensor_tensor(TS, TS, scale, s_, ALU.mult, ALU.mult))
                step.wait()
                if signal is not None:
                    dve.wait_ge(signal, first)
                nc.vector.tensor_tensor(out, TM, TS, ALU.add).then_inc(rope_in, 1)

            def compression_input(kv, src):
                pe0 = COLS["pe_k" if kv == 0 else "pe_v"]
                for g in range(NG):
                    half = slice(DH * (g % 2), DH * (g % 2) + DH)
                    tok = src[half, g // 2].rearrange("p (c x two) -> p two x c", two=2, x=8)
                    pe = cols[half, pe0:pe0 + CLEN].rearrange("p (m two) -> p two m", two=2)
                    for par in range(2):
                        for mh in range(2):
                            ins = nc.vector.tensor_tensor(
                                XB[kv][DH * par:DH * par + DH, 8 * mh:8 * mh + 8, g, 0:CMP],
                                tok[:, par, :, mh:mh + CMP],
                                pe[:, par, 8 * mh:8 * mh + 8].unsqueeze(2).broadcast_to([DH, 8, CMP]), ALU.add)
                            ins.then_inc(xb_ready, 1)

            t0 = T0["nsa"]
            for j, out in ((0, KC[:, 0]), (1, KC[:, 1])):
                rotary(psum(product("nsa", j)), csr, snr, out, 1.0, freed, t0 + j + 1)
            inverse(2, RS1)
            for j in range(2):
                nc.vector.tensor_tensor(VC[:, j], psum(product("nsa", 2 + j)), rstd[:], ALU.mult).then_inc(freed, 1)
            for n, out in enumerate((KS[:, 0], KS[:, 1], KW[:, 0], KW[:, 1])):
                rotary(psum(product("nsa", 4 + n)), csr, snr, out, 1.0, freed, t0 + 5 + n)
            dve.wait_ge(rope_in, 6)
            dve.wait_ge(freed, t0 + 4)
            compression_input(0, KC)
            for n in range(4):
                norm_tile(n, "g_out", RS1)
                rotary(psum(product("nsa", 8 + n)), csr, snr, QN[:, n], float(DH) ** -0.5, freed, t0 + 9 + n)
            compression_input(1, VC)
            for n in range(4, 8):
                norm_tile(n, "g_out", RS1)
                rotary(psum(product("nsa", 8 + n)), csr, snr, QN[:, n], float(DH) ** -0.5, freed, t0 + 9 + n)

            def tokens(j):
                b = product("nsa", 16 + j)
                if j >= 2:
                    dve.wait_ge(tok_t, j - 1)
                nc.vector.tensor_tensor((TS, TM)[j % 2], psum(b), rstd[:], ALU.mult).then_inc(freed, 1)

            def c_arg(i):
                s_ = PS[:, 2:4, :].rearrange("p a (r c) -> p a r c", c=P)[:, :, :, 0:2 * CP]
                dve.wait_ge(cs_mm, i + 1)
                if i >= 2:
                    dve.wait_ge(cs_t, i - 1)
                step.wait()
                for gp in range(2):
                    step.mark(nc.vector.tensor_reduce(cst[:, 0, 8 * gp:8 * gp + 8],
                                                      s_[:, gp].rearrange("p r (o c) -> p r o c", c=CP), AX.X, ALU.max, negate=True))
                step.wait()
                step.mark(nc.vector.tensor_scalar(cst[:, 0], cst[:, 0], 1e20, None, ALU.min))
                step.wait()
                for gp in range(2):
                    ins = nc.vector.tensor_tensor(
                        SX[i % 2][:, 8 * gp:8 * gp + 8].rearrange("p (r o) c -> p r o c", o=2),
                        s_[:, gp].rearrange("p r (o c) -> p r o c", c=CP),
                        cst[:, 0, 8 * gp:8 * gp + 8].rearrange("p (r o) -> p r o", o=2).unsqueeze(3).broadcast_to([P, 4, 2, CP]),
                        ALU.add)
                    if gp == 0:
                        step.mark(ins)
                    else:
                        ins.then_inc(cs_arg, 1)

            def c_norm(i):
                dve.wait_ge(cs_exp, i + 1)
                step.mark(nc.vector.tensor_reduce(cst[:, 1], SX[i % 2], AX.X, ALU.add))
                step.wait()
                step.mark(nc.vector.tensor_scalar(cst[:, 1], cst[:, 1], 1e-30, None, ALU.max))
                step.wait()
                step.mark(nc.vector.reciprocal(cst[:, 2], cst[:, 1]))
                step.wait()
                step.mark(nc.vector.tensor_tensor(
                    cst[:, 2].rearrange("p (g r o) -> p g r o", g=2, o=2), cst[:, 2].rearrange("p (g r o) -> p g r o", g=2, o=2),
                    GT[:, i].rearrange("p (g o r m) -> p g r o m", g=2, o=2, m=3)[:, :, :, :, 0], ALU.mult))
                step.wait()
                nc.vector.tensor_tensor(SX[i % 2], SX[i % 2], cst[:, 2].unsqueeze(2).broadcast_to([P, HQ, CP]), ALU.mult
                                        ).then_inc(cs_norm, 1)
                dve.wait_ge(cs_norm, i + 1)

            dve.wait_ge(rope_in, 14)
            tokens(0)
            dve.wait_ge(hid_ready, 2)
            nc.vector.tensor_copy(HIDR, HID[1].rearrange("p a (g o) c -> p (a g) (o c)", g=2).unsqueeze(2).broadcast_to(
                [P, NG, 2, 2 * CP])).then_inc(kv_ready, 1)
            dve.wait_ge(cmp_mm, 1)
            for odd in range(2):
                q = slice(DH * odd, DH * odd + DH)
                nc.vector.tensor_copy(BDK[q, :, CP * odd:CP * odd + CP],
                                      PS[q, 4, 0:P].rearrange("p (g o c) -> p g o c", g=2, o=2)[:, :, odd]).then_inc(cmp_ready, 1)
            dve.wait_ge(cmp_mm, 2)
            for r in range(4):
                q = slice(32 * r, 32 * r + 32)
                nc.vector.tensor_copy(BDV[q, :, r, :], PS[q, 5, 0:256].rearrange("p (g d) -> p g d", g=2)[:, :, 0:DH]
                                      ).then_inc(cmp_ready, 1)
            tokens(1)
            dve.wait_ge(tok_t, 1)
            nc.vector.tensor_tensor(GT, psum(7).rearrange("p (t x) -> p t x", x=P)[:, :, 0:48],
                                    rows[:, 0:48].unsqueeze(1).broadcast_to([P, NT, 48]), ALU.add).then_inc(gt_raw, 1)
            c_arg(0)
            tokens(2)
            dve.wait_ge(gt_ready, 1)
            c_norm(0)
            c_arg(1)
            tokens(3)
            c_norm(1)
            c_arg(2)
            tokens(4)
            c_norm(2)
            c_arg(3)
            c_norm(3)

            def attention(units, v0, swa):
                def maxima(v):
                    c, pairs, m, i = units[v - v0]
                    n = P * pairs * len(key_tiles(i, swa))
                    dve.wait_ge(s_mm, v + 1)
                    b = 2 + 2 * (v % 2)
                    s_ = PS[:, b:b + 2, 0:n].rearrange("p h (r n) -> p h r n", r=pairs)
                    low = nmr[:, v % 4, :, 0:pairs]
                    if not swa:
                        nc.vector.tensor_reduce(low, s_, AX.X, ALU.max, negate=True).then_inc(nmax, 1)
                        return
                    sink = nsk.rearrange("p (a b) -> p a b", a=2)[:, :, c:c + pairs]
                    step.mark(nc.vector.tensor_reduce(nmx[:, v % 4, :, 0:pairs], s_, AX.X, ALU.max, negate=True))
                    step.wait()
                    nc.vector.tensor_tensor(low, nmx[:, v % 4, :, 0:pairs], sink, ALU.min).then_inc(nmax, 1)
                    dve.wait_ge(nmax, v + 1)
                    nc.vector.tensor_tensor(ske[:, v % 4, :, 0:pairs], low, sink, ALU.subtract).then_inc(qb_raw, 1)

                def evac(v):
                    c, pairs, m, i = units[v - v0]
                    n = P * pairs * len(key_tiles(i, swa))
                    dve.wait_ge(pt_mm, v + 1)
                    if v >= 2:
                        dve.wait_ge(o_mm, v - 1)
                    nc.vector.tensor_copy(PT_[:, v % 2, 0, 0:n], psum(6, n)).then_inc(pt_d, 1)

                def output(v):
                    c, pairs, m, i = units[v - v0]
                    dve.wait_ge(o_mm, v + 1)
                    o_ = PS[:, v % 2, 0:2 * pairs * VN].rearrange("p (h r x) -> p h r x", h=2, x=VN)
                    inv, total, w = (rec[:, n, :, 0:pairs] for n in range(3))
                    dst = OA[:, i, c:c + pairs].rearrange("p r h d -> p h r d")
                    if swa:
                        dve.wait_ge(p_exp, v + 1)
                        step.mark(nc.vector.tensor_tensor(total, o_[:, :, :, DH], esk[:, v % 4, :, 0:pairs], ALU.add))
                        step.wait()
                        step.mark(nc.vector.reciprocal(inv, total))
                        step.wait()
                        nc.vector.tensor_tensor(dst, o_[:, :, :, 0:DH], inv.unsqueeze(3).broadcast_to([P, 2, pairs, DH]),
                                                ALU.mult).then_inc(o_done, 1)
                    else:
                        g = GT[:, i].rearrange("p (g r x) -> p g r x", g=NG, x=3)
                        g = g[:, 2 * (c // 4):2 * (c // 4) + 2, c % 4:c % 4 + pairs, 1 + m]
                        step.mark(nc.vector.reciprocal(inv, o_[:, :, :, DH]))
                        step.wait()
                        step.mark(nc.vector.tensor_tensor(w, inv, g, ALU.mult))
                        step.wait()
                        for hh in range(2):
                            for r in range(pairs):
                                ins = nc.vector.scalar_tensor_tensor(dst[:, hh, r], o_[:, hh, r, 0:DH], w[:, hh, r:r + 1],
                                                                     dst[:, hh, r], ALU.mult, ALU.add)
                                if hh * pairs + r < 2 * pairs - 1:
                                    step.mark(ins)
                        ins.then_inc(o_done, 1)
                    dve.wait_ge(o_done, v + 1)

                last = v0 + len(units)
                maxima(v0)
                maxima(v0 + 1)
                evac(v0)
                for v in range(v0, last):
                    if v + 2 < last:
                        maxima(v + 2)
                    if v + 1 < last:
                        evac(v + 1)
                    output(v)

            def attention_out(stage, n0):
                for c in range(KT):
                    dve.wait_ge(oa_mm, n0 + c + 1)
                    lo(stage, c, psum(2 + c % 6))

            def ffn(layer):
                st, t0 = f"gu{layer}", T0[f"gu{layer}"]
                fcw = cols[:, COLS[f"fcw{layer}"]:COLS[f"fcw{layer}"] + 3 * FT]
                fcb = cols[:, COLS[f"fcb{layer}"]:COLS[f"fcb{layer}"] + FT]
                step.mark(nc.vector.memset(AP_[:, :, 0:2], 0.0))
                step.wait()
                before = step.n
                with dve.Fori(0, FT // 2) as it:
                    step.off = 4 * it
                    for b in range(2):
                        w = [fcw[:, bass.ds(t * FT + b + 2 * it, 1)] for t in range(3)]
                        bias = fcb[:, bass.ds(b + 2 * it, 1)]
                        bank = (t0 + 2 * b) % 2
                        dve.wait_ge(tile_used, W0[st] + 4 * it + (2 * b + 1))
                        nc.vector.tensor_tensor(AP_[:, b, 2:2 + S], psum(bank), rstd[:], ALU.mult).then_inc(freed, 1)
                        dve.wait_ge(freed, t0 + 4 * it + (2 * b + 1))
                        step.mark(nc.vector.tensor_scalar(CV[:, b], AP_[:, b, 0:S], w[0], bias, ALU.mult, ALU.add))
                        step.wait()
                        step.mark(nc.vector.scalar_tensor_tensor(CV[:, b], AP_[:, b, 1:1 + S], w[1], CV[:, b], ALU.mult, ALU.add))
                        step.wait()
                        nc.vector.scalar_tensor_tensor(CV[:, b], AP_[:, b, 2:2 + S], w[2], CV[:, b], ALU.mult, ALU.add
                                                       ).then_inc(ff_conv, 1)
                        dve.wait_ge(tile_used, W0[st] + 4 * it + (2 * b + 2))
                        nc.vector.tensor_tensor(TU[:, b], psum(1 - bank), rstd[:], ALU.mult).then_inc(freed, 1)
                        dve.wait_ge(freed, t0 + 4 * it + (2 * b + 2))
                        dve.wait_ge(ff_silu, layer * FT + 2 * it + (b + 1))
                        nc.vector.tensor_tensor(MID[:, bass.ds(2 * it + b, 1)].rearrange("p o t -> p (o t)"), TU[:, b], SA[:, b], ALU.mult).then_inc(mid_ready, 1)
                assert step.n - before == 4
                step.n, step.off = before + 4 * (FT // 2), 0
                for f in range(FT):
                    dve.wait_ge(xh_ready, X0[f"down{layer}"] + f + 1)
                    nc.vector.tensor_tensor(XL[:, f % 4], MID[:, f], XH[:, f % 4].bitcast(F32), ALU.subtract).then_inc(xl_ready, 1)
                for k in range(KT):
                    if k < KT - 1:
                        dve.wait_ge(down_mm, (KT - 1) * layer + k + 1)
                    else:
                        dve.wait_ge(tile_used, W0[f"down{layer}"] + FT)
                    nc.vector.tensor_tensor(R[:, k], psum(k), R[:, k], ALU.add).then_inc(down_added, 1)

            attention(NSA_UNITS, 0, False)
            attention_out("nsa_o", 0)
            dve.wait_ge(normed, KT)
            add_residual("nsa_o", behind=lambda k: k and add_square(3, k))
            split_rest("gu0", "g_ffn0")
            add_square(3, KT - 1)
            inverse(3, rstd[:])
            ffn(0)

            split_rest("swa", "g_mix1")
            for k in range(1, KT):
                add_square(4, k)
            inverse(4, rstd[:])
            step.mark(nc.vector.tensor_scalar(nsk, rows[:, 48:64], -1.0, None, ALU.mult))
            step.mark(nc.vector.memset(VS[:, :, :, DH:DH + 1], 1.0))
            dve.wait_ge(consts_in, 16 * 17)
            t0 = T0["swa"]
            for j in range(10):
                b = product("swa", j)
                if j >= 2:
                    dve.wait_ge(rope_in, 14 + j - 1)
                nc.vector.tensor_tensor(TB[:, j % 2], psum(b), rstd[:], ALU.mult).then_inc(freed, 1)
                if j >= 1:
                    dve.wait_ge(qb_ready, j)
                    rotary(TB[:, (j - 1) % 2], cs, sn, KS[:, 0] if j == 1 else QN[:, j - 2],
                           1.0 if j == 1 else float(DH) ** -0.5, None)
            attention(SWA_UNITS, len(NSA_UNITS), True)
            attention_out("swa_o", KT)
            add_residual("swa_o", "b_o", behind=lambda k: k and add_square(5, k))
            split_rest("gu1", "g_ffn1")
            add_square(5, KT - 1)
            inverse(5, rstd[:])
            ffn(1)
            for k in range(1, KT):
                add_square(6, k)
            inverse(6, rstd[:])
            for k in range(KT):
                norm_tile(k, "g_fin", rstd[:])

        @block.tensor
        def _(pe):
            mm = nc.tensor.matmul

            def norm(q):
                pe.wait_ge(sq_acc, 7 * (q + 1))
                if q == 0:
                    pe.wait_ge(zero_set, 2)
                mm(psum(7), ones[:], RMS, start=True, stop=True).then_inc(sq_sum, 1)

            def two_norms():
                pe.wait_ge(sq_acc, 7 * 3)
                mm(psum(7), ones[:], RMS, start=True, stop=True).then_inc(sq_sum, 1)
                mm(psum(6), ones[:], rstd[:], start=True, stop=True).then_inc(sq_sum, 1)

            def wait_bank(t):
                if t >= 2:
                    pe.wait_ge(freed, t - 1)

            def channel_major(stage, j, n, xname=None):
                w, t = W0[stage] + j, T0[stage] + j
                x = X0[xname or stage]
                wait_bank(t)
                pe.wait_ge(tile_split, w + 1)
                s = w % SPL
                for k in range(KT):
                    if j == 0:
                        pe.wait_ge(xh_ready, x + k + 1)
                        pe.wait_ge(xl_ready, x + k + 1)
                    out = psum(t % 2)
                    mm(out, WH[:, s, k], XH[:, k], start=(k == 0), stop=False)
                    mm(out, WH[:, s, k], XL[:, k], start=False, stop=False)
                    ins = mm(out, WL[:, s, k], XH[:, k], start=False, stop=(k == KT - 1))
                ins.then_inc(tile_used, 1)

            def linear(stage, n=KT, q=None):
                for j in range(n):
                    channel_major(stage, j, n)
                    if j == 0 and q is not None:
                        two_norms() if q == 2 else norm(q)

            def turn_values(n, src, ready, value, bank_free):
                pe.wait_ge(ready, value)
                if bank_free:
                    pe.wait_ge(tok_out, bank_free - 1)
                for i in range(NT):
                    ins = nc.tensor.transpose(PS[:, 7, P * i:P * (i + 1)], src[:, P * i:P * (i + 1)], ident[:])
                ins.then_inc(tok_t, 1)

            def head_scores(h):
                for j in range(NT):
                    if h >= 1:
                        pe.wait_ge(p_ready, 8 * (h - 1) + 2 * j + 2)
                    for e in range(2):
                        ins = mm(psum(2 + j), K1[:, 2 * h + e, P * j:P * (j + 1)], Q1[:, 2 * h + e], start=(e == 0), stop=(e == 1))
                    ins.then_inc(s_mm1, 1)

            linear("in", 32, 0)
            for j in range(KT):
                if j == 0:
                    pe.wait_ge(pooled_ready, KT)
                if j >= 2:
                    pe.wait_ge(yp_ready, j - 1)
                for c in range(2):
                    ins = mm(psum(2 + j % 2), poolw[:, (j // 2) * 4 + 2 * c + j % 2], pooled[:, 2 * (j // 2) + c],
                             start=(c == 0), stop=(c == 1))
                ins.then_inc(pool_mm, 1)
            pe.wait_ge(yp_ready, KT)
            pe.wait_ge(bd_ready, 4)
            for j in range(KT):
                pe.wait_ge(c_ready, j + 1)
                for n in range(2):
                    if j >= 1:
                        pe.wait_ge(q_out, 2 * (j - 1) + n + 1)
                    mm(psum(2 + n), BD[n][:, j].rearrange("p a b -> p (a b)"), C[:, j], start=True, stop=True).then_inc(q_mm, 1)
                if j >= 1:
                    pe.wait_ge(vt_out, j)
                for i in range(NT):
                    ins = mm(PS[:, 5, P * i:P * (i + 1)], U[:, j, UPAD + P * i:UPAD + P * (i + 1)],
                             BD[2][:, j].rearrange("p a b -> p (a b)"), start=True, stop=True)
                ins.then_inc(vt_mm, 1)
                mm(PS[0:16, 7, :], wgm[:, j], C[:, j], start=(j == 0), stop=False)
                ins = mm(PS[0:16, 7, :], wgm[:, 16 + j], U[:, j, UPAD:UPAD + S], start=False, stop=(j == KT - 1))
            ins.then_inc(gate_mm, 1)
            pe.wait_ge(g16, 1)
            mm(psum(6), place_w[0:16], G16[0:16], start=True, stop=True).then_inc(g_placed, 1)
            pe.wait_ge(q_out, 2 * KT)
            pe.wait_ge(vt_out, KT)
            head_scores(0)
            for j in range(2):
                channel_major("wo_pool", j, KT)
            pe.wait_ge(a_ready, 1)
            pe.wait_ge(emt_ready, 1)
            pe.wait_ge(g16, 1)
            for n, src in ((0, gr[3]), (1, gr[5])):
                for i in range(NT):
                    ins = nc.tensor.transpose(PS[:, 7, 64 * (4 * n + i):64 * (4 * n + i) + 64], src[0:64, P * i:P * (i + 1)],
                                              ident[0:64, 0:64])
            ins.then_inc(cols_mm, 1)

            offs = [[0, 512, 896, 1152], [0, 128, 384, 768]]

            def maxima_rows(h):
                if h == 0:
                    pe.wait_ge(nm_ready, 1)
                    pe.wait_ge(acol_ready, 1)
                else:
                    pe.wait_ge(w_exp, 8 * h)
                    pe.wait_ge(wd_ready, 2 * h)
                for d in range(2):
                    q = slice(32 * d, 32 * d + 32)
                    mm(psum(6 + d), ident[q, 32 * d + h:32 * d + h + 1].broadcast_to([32, P]), NM[q], start=True, stop=True
                       ).then_inc(m_bc, 1)

            def numerators(h):
                pe.wait_ge(p_ready, 8 * (h + 1))
                for i in range(NT):
                    for d in range(2):
                        n = 8 * h + 2 * i + d
                        if n >= 2:
                            pe.wait_ge(num_out, n - 1)
                        js = range(i + 1) if d == 0 else range(i, NT)
                        for j in js:
                            at = offs[d][j] + (P * (i - j) if d == 0 else P * i)
                            ins = mm(PS[:, n % 2, 0:257], PW[d][:, at:at + P], V1[:, j, h], start=(j == js[0]), stop=(j == js[-1]))
                        ins.then_inc(num_mm, 1)

            maxima_rows(0)
            for h in range(HEADS):
                if h >= 1:
                    pe.wait_ge(num_out, 8 * h)
                for j in POOL_TILES[h]:
                    channel_major("wo_pool", j, KT)
                if h + 1 < HEADS:
                    maxima_rows(h + 1)
                    head_scores(h + 1)
                pe.wait_ge(freed, T0["wo_pool"] + POOL_TILES[h][-1] + 1)
                numerators(h)
            pe.wait_ge(xhat, 12)
            for j in range(KT):
                if j == 6:
                    pe.wait_ge(xhat_last, 4)
                if j >= 6:
                    pe.wait_ge(yc_ready, j - 5)
                for i in range(NT):
                    ins = nc.tensor.transpose(PS[:, 2 + j % 6, P * i:P * (i + 1)], H[:, i, P * j:P * (j + 1)], ident[:])
                ins.then_inc(yt_mm, 1)
            linear("wo_m")

            linear("nsa", 16, 2)
            pe.wait_ge(xb_ready, 32)
            pe.wait_ge(consts_in, 16 * 15)
            for kv in range(2):
                for ht in range(2):
                    for m in range(16):
                        ins = mm(PS[:, 2 + kv, P * ht:P * (ht + 1)], CW1[kv][:, m, P * ht:P * (ht + 1)],
                                 XB[kv][:, m].rearrange("p g c -> p (g c)"), start=(m == 0), stop=(m == 15))
                ins.then_inc(hid_mm, 1)
            channel_major("nsa", 16, 21)
            pe.wait_ge(hid_ready, 2)
            for ht in range(2):
                ins = mm(PS[:, 4, 0:P], CW2[:, 0, ht], HID[0][:, ht].rearrange("p g c -> p (g c)"), start=(ht == 0), stop=(ht == 1))
            ins.then_inc(cmp_mm, 1)
            pe.wait_ge(kv_ready, 1)
            for gp in range(2):
                for ht in range(2):
                    ins = mm(PS[:, 5, P * gp:P * (gp + 1)], HIDR[:, 2 * ht + gp].rearrange("p r c -> p (r c)"),
                             CW2[:, 1, ht], start=(ht == 0), stop=(ht == 1))
            ins.then_inc(cmp_mm, 1)

            def c_scores(i):
                if i == 0:
                    pe.wait_ge(rope_in, 14)
                    pe.wait_ge(cmp_ready, 6)
                else:
                    pe.wait_ge(cs_arg, i)
                for gp in range(2):
                    mm(psum(2 + gp).rearrange("p (r c) -> p r c", c=P), identb[:],
                       cmask[:, i].unsqueeze(1).broadcast_to([P, 4, P]), start=True, stop=False)
                    for r in range(4):
                        ins = mm(PS[:, 2 + gp, P * r:P * (r + 1)], QN[:, 4 * gp + r, P * i:P * (i + 1)], BDK[:, gp],
                                 start=False, stop=(r == 3))
                ins.then_inc(cs_mm, 1)

            def c_turn(i):
                pe.wait_ge(cs_norm, i + 1)
                if i >= 1:
                    pe.wait_ge(cs_tout, i)
                for n in range(4):
                    ins = nc.tensor.transpose(PS[:, 6, P * n:P * (n + 1)],
                                              SX[i % 2][:, 4 * n:4 * n + 4].rearrange("p r c -> p (r c)"), ident[:])
                ins.then_inc(cs_t, 1)

            def c_out(i):
                pe.wait_ge(cs_tout, i + 1)
                for n in range(4):
                    if i >= 1 and n % 2 == 0:
                        pe.wait_ge(cs_out, 2 * (i - 1) + n // 2 + 1)
                    ins = mm(PS[:, 4 + n // 2, 256 * (n % 2):256 * (n % 2) + 256], PTC[i % 2][:, n],
                             BDV[:, n // 2].rearrange("p r d -> p (r d)"), start=True, stop=True)
                    if n % 2 == 1:
                        ins.then_inc(cs_o, 1)

            t0 = T0["nsa"]
            channel_major("nsa", 17, 21)
            turn_values(0, TS, freed, t0 + 17, 0)
            c_scores(0)
            channel_major("nsa", 18, 21)
            pe.wait_ge(gt_raw, 1)
            turn_values(1, TM, freed, t0 + 18, 0)
            c_scores(1)
            c_turn(0)
            channel_major("nsa", 19, 21)
            turn_values(2, TS, freed, t0 + 19, 2)
            c_out(0)
            c_turn(1)
            c_scores(2)
            channel_major("nsa", 20, 21)
            turn_values(3, TM, freed, t0 + 20, 3)
            c_out(1)
            c_turn(2)
            c_scores(3)
            turn_values(4, TS, freed, t0 + 21, 4)
            c_out(2)
            c_turn(3)
            c_out(3)
            pe.wait_ge(tok_out, 4)
            pe.wait_ge(cs_out, 8)
            pe.wait_ge(freed, T0["nsa_o"])

            def attention(units, v0, swa):
                def score(v):
                    c, pairs, m, i = units[v - v0]
                    js = key_tiles(i, swa)
                    n, k0 = P * len(js), P * js[0]
                    K = KS[:, 0] if swa else (KS, KW)[m][:, c // 4]
                    if v >= 2:
                        pe.wait_ge(p_exp, v - 1)
                    for hh in range(2):
                        half = slice(DH * hh, DH * hh + DH)
                        b = 2 + 2 * (v % 2) + hh
                        for r in range(pairs):
                            s_ = PS[:, b, n * r:n * (r + 1)]
                            mm(s_, QN[half, c + r, P * i:P * (i + 1)], K[half, k0:k0 + n], start=True, stop=False)
                            if swa and i >= 1:
                                mm(s_[:, 0:P], identb[:], masks[:, 2], start=False, stop=False)
                            ins = mm(s_[:, n - P:n], identb[:], masks[:, 1], start=False, stop=True)
                    ins.then_inc(s_mm, 1)

                def turn(v):
                    c, pairs, m, i = units[v - v0]
                    pe.wait_ge(p_exp, v + 1)
                    if v >= 1:
                        pe.wait_ge(pt_d, v)
                        pe.wait_ge(pt_a, v)
                    for hh in range(2):
                        for n in range(pairs * len(key_tiles(i, swa))):
                            ins = nc.tensor.transpose(PS[:, 6 + hh, P * n:P * (n + 1)], PE_[:, v % 2, hh, P * n:P * (n + 1)],
                                                      ident[:])
                    ins.then_inc(pt_mm, 1)

                def output(v):
                    c, pairs, m, i = units[v - v0]
                    pe.wait_ge(pt_d, v + 1)
                    pe.wait_ge(pt_a, v + 1)
                    if v >= 2:
                        pe.wait_ge(o_done, v - 1)
                    js = key_tiles(i, swa)
                    for hh in range(2):
                        for r in range(pairs):
                            to = VN * (pairs * hh + r)
                            for n, j in enumerate(js):
                                at = 65 * (NG * j + hh + (0 if swa else 2 * (c // 4)))
                                p0 = P * (len(js) * r + n)
                                ins = mm(PS[:, v % 2, to:to + VN], PT_[:, v % 2, hh, p0:p0 + P],
                                         v_rows[0 if swa else m][:, at:at + VN], start=(n == 0), stop=(n == len(js) - 1))
                    ins.then_inc(o_mm, 1)

                last = v0 + len(units)
                score(v0)
                score(v0 + 1)
                turn(v0)
                for v in range(v0, last):
                    if v + 2 < last:
                        score(v + 2)
                    if v + 1 < last:
                        turn(v + 1)
                    output(v)

            def attention_out(stage, n0, units):
                pe.wait_ge(o_done, units)
                for c in range(KT):
                    if c >= 6:
                        pe.wait_ge(xl_ready, X0[stage] + c - 5)
                    for i in range(NT):
                        ins = nc.tensor.transpose(PS[:, 2 + c % 6, P * i:P * (i + 1)], OA[:, i, c].rearrange("p a d -> p (a d)"),
                                                  ident[:])
                    ins.then_inc(oa_mm, 1)

            def ffn(layer, q):
                st, sd = f"gu{layer}", f"down{layer}"
                w0, t0, x0 = W0[st], T0[st], X0[st]
                wd, xd = W0[sd], X0[sd]
                for j in range(4):
                    channel_major(st, j, 2 * FT)
                    if j == 0:
                        norm(q)
                with pe.Fori(1, FT // 2) as it:
                    for b in range(4):
                        pe.wait_ge(freed, t0 + 4 * it + (b - 1))
                        pe.wait_ge(tile_split, w0 + 4 * it + (b + 1))
                        s, out = (w0 + b) % SPL, psum((t0 + b) % 2)
                        for k in range(KT):
                            mm(out, WH[:, s, k], XH[:, k], start=(k == 0), stop=False)
                            mm(out, WH[:, s, k], XL[:, k], start=False, stop=False)
                            ins = mm(out, WL[:, s, k], XH[:, k], start=False, stop=(k == KT - 1))
                        ins.then_inc(tile_used, 1)
                pe.wait_ge(freed, t0 + 2 * FT)
                for f in range(FT):
                    s, x = (wd + f) % SPL, f % 4
                    pe.wait_ge(tile_split, wd + f + 1)
                    pe.wait_ge(xh_ready, xd + f + 1)
                    pe.wait_ge(xl_ready, xd + f + 1)
                    for k in range(KT):
                        mm(psum(k), WH[:, s, k], XH[:, x], start=(f == 0), stop=False)
                        mm(psum(k), WH[:, s, k], XL[:, x], start=False, stop=False)
                        ins = mm(psum(k), WL[:, s, k], XH[:, x], start=False, stop=(f == FT - 1))
                        if f == FT - 1 and k < KT - 1:
                            ins.then_inc(down_mm, 1)
                    ins.then_inc(tile_used, 1)

            attention(NSA_UNITS, 0, False)
            attention_out("nsa_o", 0, len(NSA_UNITS))
            linear("nsa_o")
            ffn(0, 3)
            pe.wait_ge(down_added, KT)
            linear("swa", 10, 4)
            turn_values(10, TB[:, 1], qb_ready, 10, 5)
            pe.wait_ge(tok_out, 5)
            pe.wait_ge(rope_in, 14 + 9)
            attention(SWA_UNITS, len(NSA_UNITS), True)
            attention_out("swa_o", KT, len(NSA_UNITS) + len(SWA_UNITS))
            linear("swa_o")
            ffn(1, 5)
            pe.wait_ge(down_added, 2 * KT)
            norm(6)



def _tiles(w):
    k, m = w.shape
    return np.ascontiguousarray(w.reshape(KT, P, m // P, P).transpose(2, 1, 0, 3))


def _vec(v):
    return v.reshape(-1, P).T


_QUADS = [np.arange(16 * q, 16 * q + 16) for q in range(2)]
PERM = np.concatenate([np.concatenate([x, x + 32]) for x in _QUADS])


def _constants():
    r, c = np.arange(P)[:, None], np.arange(P)[None, :]
    low = np.float32(-1e30)
    masks = np.stack([np.where(m, np.float32(0), low) for m in (c >= r, c <= r, c > r)], 1)
    pos = np.arange(S)
    end = np.arange(CP) * 16 + CLEN - 1
    cm = np.where((end[None, :] <= pos[:, None]) & (np.arange(CP)[None, :] < CMP), np.float32(0), low)
    cm = np.concatenate([cm, cm, np.zeros((S, 2 * CP), np.float32)], 1)
    cmask = np.ascontiguousarray(cm.reshape(NT, P, P).transpose(1, 0, 2))
    counts = []
    for w in WINDOWS:
        left = (w - 1) // 2
        counts.append(np.minimum(pos + w - 1 - left, S - 1) - np.maximum(pos - left, 0) + 1)
    invc = (1.0 / np.stack(counts)).astype(np.float32)
    inv = np.float32(10000.0) ** (-np.arange(0, DH, 2, dtype=np.float32) / np.float32(DH))
    ang = np.arange(S, dtype=np.float32)[:, None] * inv[None, :]
    cos, sin = np.cos(ang).astype(np.float32).T, np.sin(ang).astype(np.float32).T
    freq = np.tile(PERM % 32, 2)
    sign = np.tile(np.where(PERM < 32, -1.0, 1.0), 2).astype(np.float32)[:, None]
    place = np.zeros((16, P), np.float32)
    for d in range(2):
        for g in range(8):
            place[8 * d + g, 32 * d + g if g < 4 else 64 + 32 * d + g - 4] = 1.0
    return {
        "ident": np.eye(P, dtype=np.float32),
        "masks": masks, "cmask": cmask,
        "invc": np.ascontiguousarray(np.broadcast_to(invc, (P, 4, S))),
        "bdm": (r // 4 == np.arange(32)[None, :]).astype(np.float32),
        "cos": np.ascontiguousarray(cos[freq]), "sin": np.ascontiguousarray(sin[freq] * sign), "place": place,
    }


def _layout(i):
    f = {k: np.asarray(v) for k, v in i.items()}
    w_in = f["w_in"][0]
    part = lambda n: w_in[:, n * D:(n + 1) * D]
    head_nsa = [(2 * (c // 4) + hh) * 4 + c % 4 for c in range(8) for hh in range(2)]
    head_swa = [hh * 8 + c for c in range(8) for hh in range(2)]
    rot = lambda heads: np.concatenate([h * DH + PERM for h in heads])
    flat = lambda heads: np.concatenate([h * DH + np.arange(DH) for h in heads])
    nw = f["nsa_w_in_2"][0]
    kv = lambda n: nw[:, HQ * DH + 256 * n:HQ * DH + 256 * (n + 1)]
    gates = np.zeros((D, P), np.float32)
    gates[:, 0:48] = nw[:, HQ * DH + 6 * 256:]
    k4, k2 = rot(range(4)), rot(range(2))
    nsa = np.concatenate([kv(0)[:, k4], kv(1), kv(2)[:, k4], kv(4)[:, k4], nw[:, :HQ * DH][:, rot(head_nsa)],
                          gates, kv(3), kv(5)], 1)
    sw, sbias = f["swa_w_qkv_2"][0], f["swa_b_qkv_2"][0]
    swa = np.concatenate([sw[:, HQ * DH:HQ * DH + P][:, k2], sw[:, :HQ * DH][:, rot(head_swa)], sw[:, HQ * DH + P:]], 1)
    gu = []
    for n in range(2):
        g = f["ffn_w_gu_2"][n].reshape(D, 2, FT, P).transpose(0, 2, 1, 3)
        gu.append(_tiles(g.reshape(D, 2 * FF)))
    down = [f["ffn_w_down_2"][n].reshape(FT, P, KT, P) for n in range(2)]
    w = np.concatenate([
        _tiles(np.concatenate([part(2), part(0), part(1), part(3)], 1)),
        _tiles(f["w_out"][0][:D]), _tiles(f["w_out"][0][D:]), _tiles(nsa),
        _tiles(f["nsa_w_o_2"][0][flat(head_nsa)]), gu[0], down[0],
        _tiles(swa), _tiles(f["swa_w_o_2"][0][flat(head_swa)]), gu[1], down[1]])
    c = np.zeros((P, NCOL), np.float32)

    def put(name, v):
        c[:, COLS[name]:COLS[name] + v.shape[1]] = v

    for name, v in (("g_in", f["norm_in_g"][0]), ("g_out", f["norm_out_g"]), ("pool_scale", f["pool_scale"][0]),
                    ("conv_w", f["conv_w"][0]), ("conv_b", f["conv_b"][0]), ("mh", f["mh_norm_w"][0]),
                    ("skip", f["skip_w"][0]), ("g_mix0", f["norm_mix_2"][0]), ("g_mix1", f["norm_mix_2"][1]),
                    ("g_ffn0", f["norm_ffn_2"][0]), ("g_ffn1", f["norm_ffn_2"][1]), ("g_fin", f["norm_final_2"]),
                    ("b_q", sbias[:HQ * DH][rot(head_swa)]), ("b_k", sbias[HQ * DH:HQ * DH + P][k2]),
                    ("b_v", sbias[HQ * DH + P:]),
                    ("b_o", f["swa_b_o_2"][0]), ("fcw0", f["ffn_conv_w_2"][0]), ("fcw1", f["ffn_conv_w_2"][1]),
                    ("fcb0", f["ffn_conv_b_2"][0]), ("fcb1", f["ffn_conv_b_2"][1])):
        put(name, _vec(v))
    c[0:16, COLS["b_gates"]] = f["b_gates"][0].reshape(16)
    pe = f["nsa_cmp_pe_2"][0]
    put("pe_k", np.tile(pe[0].T[PERM], (2, 1)))
    put("pe_v", np.tile(pe[1].T, (2, 1)))
    row = np.concatenate([f["nsa_gate_b_2"][0], f["swa_sinks_2"][0]])
    w1, w2 = f["nsa_cmp_w1_2"][0], f["nsa_cmp_w2_2"][0]
    w1 = [w1[0].reshape(CLEN, DH, 256)[:, PERM].reshape(16, P, 256), w1[1].reshape(16, P, 256)]
    w2 = [np.concatenate([x, x], 1).reshape(2, P, P) for x in (w2[0][:, PERM], w2[1])]
    maps = np.stack([f[n][0].reshape(KT, P, 4) for n in ("w_q", "w_k", "w_v")])
    return {
        "x": f["x"][0].T.reshape(KT, P, S).transpose(1, 0, 2), "w": w, "cols": c,
        "rows": np.broadcast_to(row, (P, NROW)), "wqkv": maps.transpose(2, 0, 1, 3),
        "wg": np.repeat(f["w_gates"][0].transpose(1, 0, 2).reshape(24, P // 4, 4, 16), 4, axis=1)
        .transpose(1, 0, 2, 3).reshape(P, 96, 16),
        "pool_w": f["pool_w"][0].reshape(4, 2, P, 2, P).transpose(2, 0, 1, 3, 4).reshape(P, 16, P),
        "cmp_w1k": w1[0].transpose(1, 0, 2), "cmp_w1v": w1[1].transpose(1, 0, 2),
        "cmp_w2": np.stack(w2).transpose(2, 0, 1, 3),
    }


def kernel(**inputs):
    import concourse.bacc as bacc
    from concourse.bass_utils import run_bass_kernel_spmd

    nc = bacc.Bacc("TRN2", target_bir_lowering=False, num_devices=1)
    arrays = {**_constants(), **_layout(inputs)}
    arrays = {f"in_{n}": np.ascontiguousarray(v) for n, v in arrays.items()}
    aps = {n[3:]: nc.dram_tensor(n, v.shape, mybir.dt.from_np(v.dtype), kind="ExternalInput").ap() for n, v in arrays.items()}
    aps["out"] = nc.dram_tensor("out", (P, KT, S), F32, kind="ExternalOutput").ap()
    build(nc, aps)
    r = run_bass_kernel_spmd(nc, [arrays], core_ids=[0])
    got = r.results[0]["out"]
    return np.ascontiguousarray(got.transpose(2, 1, 0).reshape(1, S, D))
```
